# Optimizing a Trainium2 kernel written in Bass

```python
import jax, jax.numpy as jnp
from jax import lax
import numpy as np
import math

D_MODEL = 1024
BATCH = 1
SEQ = 256
DEPTH = 1

MEM_LEN = 256
BLOCK = 128
WINDOW = 128
EPS = 1e-6
DA_HEADS = 8
DA_HEAD_DIM = 64
DA_V_DIM = 2 * DA_HEAD_DIM
WA_HEADS = 16
WA_KV_HEADS = 4
WA_HEAD_DIM = 64
XA_HEADS = 4
XA_HEAD_DIM = 256
N_BRANCH = 3
DA_QK_W = DA_HEADS * 2 * DA_HEAD_DIM
DA_V_W = DA_HEADS * DA_V_DIM
WA_Q_W = WA_HEADS * WA_HEAD_DIM
WA_KV_W = WA_KV_HEADS * WA_HEAD_DIM
XA_W = XA_HEADS * XA_HEAD_DIM
GATE_W = N_BRANCH * D_MODEL
IN_WIDTHS = (DA_QK_W, DA_QK_W, DA_V_W, WA_Q_W, WA_KV_W, WA_KV_W, XA_W, GATE_W)
IN_W = sum(IN_WIDTHS)
N_EXPERTS = 16
EC_FACTOR = 2
D_EXPERT = 2048
LAMBDA_STD = 0.1


def rmsnorm(x, g):
    xf = x.astype(jnp.float32)
    y = xf * lax.rsqrt(jnp.mean(xf * xf, axis=-1, keepdims=True) + EPS)
    return (y * g.astype(jnp.float32)).astype(x.dtype)

def alibi_slopes(n_heads):
    return jnp.exp2(-8.0 * jnp.arange(1, n_heads + 1, dtype=jnp.float32) / n_heads)

def lambda_init(layer):
    return 0.8 - 0.6 * float(np.exp(-0.3 * layer))

def diff_attention(q, k, v, lam, subln_g, lam_init):
    b, s = q.shape[0], q.shape[1]
    nb = s // BLOCK
    scale = DA_HEAD_DIM ** -0.5
    slopes = alibi_slopes(DA_HEADS)[None, :, None, None, None]
    kpos = jnp.arange(s)
    qb = jnp.moveaxis(q.reshape(b, nb, BLOCK, DA_HEADS, 2, DA_HEAD_DIM), 1, 0)

    def one_block(args):
        qi, i = args
        sc = jnp.einsum('bqhmd,bkhmd->bhmqk', qi, k).astype(jnp.float32) * scale
        qpos = i * BLOCK + jnp.arange(BLOCK)
        dist = jnp.abs(qpos[:, None] - kpos[None, :]).astype(jnp.float32)
        p = jax.nn.softmax(sc - slopes * dist, axis=-1)
        a = p[:, :, 0] - lam * p[:, :, 1]
        return jnp.einsum('bhqk,bkhe->bqhe', a.astype(v.dtype), v)

    o = lax.map(one_block, (qb, jnp.arange(nb)))
    o = jnp.moveaxis(o, 0, 1).reshape(b, s, DA_HEADS, DA_V_DIM)
    o = rmsnorm(o, subln_g) * (1.0 - lam_init)
    return o.reshape(b, s, DA_V_W)

def window_attention(q, k, v, sink):
    b, s = q.shape[0], q.shape[1]
    nb = s // BLOCK
    span = BLOCK + 2 * WINDOW
    groups = WA_HEADS // WA_KV_HEADS
    scale = WA_HEAD_DIM ** -0.5
    slopes = alibi_slopes(WA_HEADS).reshape(WA_KV_HEADS, groups)[None, :, :, None, None]
    sink_logit = sink.astype(jnp.float32).reshape(WA_KV_HEADS, groups)[None, :, :, None, None]
    pad = ((0, 0), (WINDOW, WINDOW), (0, 0), (0, 0))
    kp = jnp.pad(k, pad)
    vp = jnp.pad(v, pad)
    qb = jnp.moveaxis(q.reshape(b, nb, BLOCK, WA_KV_HEADS, groups, WA_HEAD_DIM), 1, 0)

    def one_block(args):
        qi, i = args
        start = i * BLOCK
        kb = lax.dynamic_slice_in_dim(kp, start, span, axis=1)
        vb = lax.dynamic_slice_in_dim(vp, start, span, axis=1)
        sc = jnp.einsum('bqhgd,bkhd->bhgqk', qi, kb).astype(jnp.float32) * scale
        qpos = start + jnp.arange(BLOCK)
        kpos = start - WINDOW + jnp.arange(span)
        dist = jnp.abs(qpos[:, None] - kpos[None, :])
        valid = (dist <= WINDOW) & ((kpos >= 0) & (kpos < s))[None, :]
        sc = jnp.where(valid, sc - slopes * dist.astype(jnp.float32), -jnp.inf)
        sinks = jnp.broadcast_to(sink_logit, sc.shape[:-1] + (1,))
        p = jax.nn.softmax(jnp.concatenate([sc, sinks], axis=-1), axis=-1)[..., :span]
        return jnp.einsum('bhgqk,bkhd->bqhgd', p.astype(vb.dtype), vb)

    o = lax.map(one_block, (qb, jnp.arange(nb)))
    return jnp.moveaxis(o, 0, 1).reshape(b, s, WA_Q_W)

def memory_attention(q, mk, mv):
    sc = jnp.einsum('bqhd,bkhd->bhqk', q, mk).astype(jnp.float32) * (XA_HEAD_DIM ** -0.5)
    p = jax.nn.softmax(sc, axis=-1)
    o = jnp.einsum('bhqk,bkhd->bqhd', p.astype(mv.dtype), mv)
    return o.reshape(o.shape[0], o.shape[1], XA_W)

def expert_choice_ffn(h, w_router, w_gate, w_up, w_down):
    b, s, _ = h.shape
    cap = max(1, EC_FACTOR * s // N_EXPERTS)
    logits = jnp.einsum('bsd,de->bse', h, w_router).astype(jnp.float32)
    aff = jax.nn.softmax(logits, axis=-1)
    g, idx = lax.top_k(jnp.swapaxes(aff, 1, 2), cap)
    bidx = jnp.arange(b)[:, None, None]
    xe = h[bidx, idx]
    a = jnp.einsum('becd,edf->becf', xe, w_gate)
    u = jnp.einsum('becd,edf->becf', xe, w_up)
    ye = jnp.einsum('becf,efd->becd', jax.nn.silu(a) * u, w_down)
    ye = ye * g[..., None].astype(ye.dtype)
    return jnp.zeros_like(h).at[bidx, idx].add(ye)

def hybrid_layer(x, mem, layer, attn_norm_g, mem_norm_g, w_in, w_mem_kv,
                 da_lambda_q1, da_lambda_k1, da_lambda_q2, da_lambda_k2, da_subln_g,
                 wa_sink, w_da_o, w_wa_o, w_xa_o, w_out, ffn_norm_g,
                 w_router, w_exp_gate, w_exp_up, w_exp_down):
    b, s, d = x.shape
    h = rmsnorm(x, attn_norm_g)
    m = rmsnorm(mem, mem_norm_g)
    proj = h @ w_in
    offsets = np.cumsum(IN_WIDTHS)[:-1].tolist()
    da_q, da_k, da_v, wa_q, wa_k, wa_v, xa_q, gates = jnp.split(proj, offsets, axis=-1)

    lam_init = lambda_init(layer)
    lam = (jnp.exp(jnp.sum(da_lambda_q1.astype(jnp.float32) * da_lambda_k1.astype(jnp.float32)))
           - jnp.exp(jnp.sum(da_lambda_q2.astype(jnp.float32) * da_lambda_k2.astype(jnp.float32)))
           + lam_init)
    o_da = diff_attention(da_q.reshape(b, s, DA_HEADS, 2, DA_HEAD_DIM),
                          da_k.reshape(b, s, DA_HEADS, 2, DA_HEAD_DIM),
                          da_v.reshape(b, s, DA_HEADS, DA_V_DIM),
                          lam, da_subln_g, lam_init)

    o_wa = window_attention(wa_q.reshape(b, s, WA_HEADS, WA_HEAD_DIM),
                            wa_k.reshape(b, s, WA_KV_HEADS, WA_HEAD_DIM),
                            wa_v.reshape(b, s, WA_KV_HEADS, WA_HEAD_DIM),
                            wa_sink)

    mk, mv = jnp.split(m @ w_mem_kv, 2, axis=-1)
    n_mem = mem.shape[1]
    o_xa = memory_attention(xa_q.reshape(b, s, XA_HEADS, XA_HEAD_DIM),
                            mk.reshape(b, n_mem, XA_HEADS, XA_HEAD_DIM),
                            mv.reshape(b, n_mem, XA_HEADS, XA_HEAD_DIM))

    gate = jax.nn.sigmoid(gates.reshape(b, s, N_BRANCH, d))
    merged = (gate[:, :, 0] * (o_da @ w_da_o)
              + gate[:, :, 1] * (o_wa @ w_wa_o)
              + gate[:, :, 2] * (o_xa @ w_xa_o))
    x = x + merged @ w_out

    h2 = rmsnorm(x, ffn_norm_g)
    return x + expert_choice_ffn(h2, w_router, w_exp_gate, w_exp_up, w_exp_down)

def first_inputs(seed: int = 0) -> dict:
    key = jax.random.key(seed)
    ks = jax.random.split(key, 24)
    L, D = DEPTH, D_MODEL

    def w(k, shape, fan_in):
        return jax.random.normal(k, shape, jnp.float32) * (fan_in ** -0.5)

    def gain(k, shape):
        return 1.0 + 0.05 * jax.random.normal(k, shape, jnp.float32)

    def small(k, shape, scale):
        return scale * jax.random.normal(k, shape, jnp.float32)

    return {
        'x': jax.random.normal(ks[0], (BATCH, SEQ, D), jnp.float32),
        'mem': jax.random.normal(ks[1], (BATCH, MEM_LEN, D), jnp.float32),
        'attn_norm_g': gain(ks[2], (L, D)),
        'mem_norm_g': gain(ks[3], (L, D)),
        'w_in': w(ks[4], (L, D, IN_W), D),
        'w_mem_kv': w(ks[5], (L, D, 2 * XA_W), D),
        'da_lambda_q1': small(ks[6], (L, DA_HEAD_DIM), LAMBDA_STD),
        'da_lambda_k1': small(ks[7], (L, DA_HEAD_DIM), LAMBDA_STD),
        'da_lambda_q2': small(ks[8], (L, DA_HEAD_DIM), LAMBDA_STD),
        'da_lambda_k2': small(ks[9], (L, DA_HEAD_DIM), LAMBDA_STD),
        'da_subln_g': gain(ks[10], (L, DA_V_DIM)),
        'wa_sink': small(ks[11], (L, WA_HEADS), 0.5),
        'w_da_o': w(ks[12], (L, DA_V_W, D), DA_V_W),
        'w_wa_o': w(ks[13], (L, WA_Q_W, D), WA_Q_W),
        'w_xa_o': w(ks[14], (L, XA_W, D), XA_W),
        'w_out': w(ks[15], (L, D, D), D),
        'ffn_norm_g': gain(ks[16], (L, D)),
        'w_router': w(ks[17], (L, D, N_EXPERTS), D),
        'w_exp_gate': w(ks[18], (L, N_EXPERTS, D, D_EXPERT), D),
        'w_exp_up': w(ks[19], (L, N_EXPERTS, D, D_EXPERT), D),
        'w_exp_down': w(ks[20], (L, N_EXPERTS, D_EXPERT, D), D_EXPERT),
        'final_norm_g': gain(ks[21], (D,)),
    }

def first_block(x, mem, attn_norm_g, mem_norm_g, w_in, w_mem_kv,
              da_lambda_q1, da_lambda_k1, da_lambda_q2, da_lambda_k2, da_subln_g,
              wa_sink, w_da_o, w_wa_o, w_xa_o, w_out, ffn_norm_g,
              w_router, w_exp_gate, w_exp_up, w_exp_down, final_norm_g):
    for l in range(DEPTH):
        x = hybrid_layer(x, mem, l, attn_norm_g[l], mem_norm_g[l], w_in[l], w_mem_kv[l],
                         da_lambda_q1[l], da_lambda_k1[l], da_lambda_q2[l], da_lambda_k2[l],
                         da_subln_g[l], wa_sink[l], w_da_o[l], w_wa_o[l], w_xa_o[l], w_out[l],
                         ffn_norm_g[l], w_router[l], w_exp_gate[l], w_exp_up[l], w_exp_down[l])
    return rmsnorm(x, final_norm_g)


DEPTH_2 = 2

N_MIXERS = 2
HEAD_DIM = 64
N_HEADS = D_MODEL // HEAD_DIM
MIX_WIDTH = N_HEADS * HEAD_DIM
N_KV_A = max(1, N_HEADS // 8)
N_KV_B = max(1, N_HEADS // 4)
MOBA_BLOCK = 256
MOBA_TOPK = 3
MOBA_Q_CHUNK = 16
ROPE_THETA = 10000.0
NORM_EPS = 1e-5
NEG = -1e30
N_LAYERS_A = (DEPTH_2 + 1) // 2
N_LAYERS_B = DEPTH_2 // 2
IN_A = 2 * MIX_WIDTH + 2 * N_KV_A * HEAD_DIM
IN_B = 2 * MIX_WIDTH + 2 * N_KV_B * HEAD_DIM


def rmsnorm_2(x, g):
    xf = x.astype(jnp.float32)
    y = xf * lax.rsqrt(jnp.mean(xf * xf, axis=-1, keepdims=True) + NORM_EPS)
    return (y * g.astype(jnp.float32)).astype(x.dtype)

def rope_tables(seq):
    pos = jnp.arange(seq, dtype=jnp.float32)
    inv = ROPE_THETA ** (-jnp.arange(0, HEAD_DIM, 2, dtype=jnp.float32) / HEAD_DIM)
    ang = pos[:, None] * inv[None, :]
    return jnp.cos(ang), jnp.sin(ang)

def apply_rope(x, cos, sin):
    half = HEAD_DIM // 2
    x1, x2 = x[..., :half], x[..., half:]
    c, s = cos[None, :, None, :], sin[None, :, None, :]
    out = jnp.concatenate([x1 * c - x2 * s, x2 * c + x1 * s], axis=-1)
    return out.astype(x.dtype)

def split_proj(h, w_in, n_kv):
    B, S, _ = h.shape
    proj = h @ w_in
    kvw = n_kv * HEAD_DIM
    q = proj[..., :MIX_WIDTH].reshape(B, S, N_HEADS, HEAD_DIM)
    k = proj[..., MIX_WIDTH:MIX_WIDTH + kvw].reshape(B, S, n_kv, HEAD_DIM)
    v = proj[..., MIX_WIDTH + kvw:MIX_WIDTH + 2 * kvw].reshape(B, S, n_kv, HEAD_DIM)
    z = proj[..., MIX_WIDTH + 2 * kvw:]
    return q, k, v, z

def sliding_window_sink_attention(q, k, v, sinks):
    B, S, H, d = q.shape
    kvh = k.shape[2]
    G = H // kvh
    nq = S // WINDOW
    scale = 1.0 / np.sqrt(d)
    qb = q.reshape(B, nq, WINDOW, kvh, G, d)
    pad = ((0, 0), (WINDOW, 0), (0, 0), (0, 0))
    kb = jnp.pad(k, pad).reshape(B, nq + 1, WINDOW, kvh, d)
    vb = jnp.pad(v, pad).reshape(B, nq + 1, WINDOW, kvh, d)
    kband = jnp.concatenate([kb[:, :-1], kb[:, 1:]], axis=2)
    vband = jnp.concatenate([vb[:, :-1], vb[:, 1:]], axis=2)
    s = jnp.einsum('bnikgd,bnjkd->bnkgij', qb, kband).astype(jnp.float32) * scale
    i = jnp.arange(WINDOW)[:, None]
    j = jnp.arange(2 * WINDOW)[None, :]
    band = (j > i) & (j <= i + WINDOW)
    not_pad = (jnp.arange(nq)[:, None, None] > 0) | (j[None] >= WINDOW)
    mask = band[None] & not_pad
    s = jnp.where(mask[None, :, None, None], s, NEG)
    sink = jnp.broadcast_to(sinks.astype(jnp.float32).reshape(kvh, G)[None, None, :, :, None, None],
                            s.shape[:-1] + (1,))
    p = jax.nn.softmax(jnp.concatenate([s, sink], axis=-1), axis=-1)[..., :-1]
    o = jnp.einsum('bnkgij,bnjkd->bnikgd', p.astype(v.dtype), vband)
    return o.reshape(B, S, H, d)

def moba_attention(q, k, v):
    B, S, H, d = q.shape
    kvh = k.shape[2]
    G = H // kvh
    nb = -(-S // MOBA_BLOCK)
    Sp = nb * MOBA_BLOCK
    scale = 1.0 / np.sqrt(d)
    pad = ((0, 0), (0, Sp - S), (0, 0), (0, 0))
    kblk = jnp.pad(k, pad).reshape(B, nb, MOBA_BLOCK, kvh, d).transpose(0, 3, 1, 2, 4)
    vblk = jnp.pad(v, pad).reshape(B, nb, MOBA_BLOCK, kvh, d).transpose(0, 3, 1, 2, 4)
    kmean = jnp.mean(kblk.astype(jnp.float32), axis=3)
    qg = q.reshape(B, S, kvh, G, d)
    gate = jnp.einsum('bskgd,bknd->bskgn', qg.astype(jnp.float32), kmean)
    qblock = jnp.arange(S) // MOBA_BLOCK
    past = jnp.arange(nb)[None, :] < qblock[:, None]
    gate = jnp.where(past[None, :, None, None, :], gate, NEG)
    kk = min(MOBA_TOPK, nb)
    _, idx = lax.top_k(gate, kk)
    nc = S // MOBA_Q_CHUNK
    q_c = qg.reshape(B, nc, MOBA_Q_CHUNK, kvh, G, d).transpose(1, 0, 2, 3, 4, 5)
    idx_c = idx.reshape(B, nc, MOBA_Q_CHUNK, kvh, G, kk).transpose(1, 0, 2, 3, 4, 5)
    bi = jnp.arange(B)[:, None, None, None, None]
    ki = jnp.arange(kvh)[None, None, :, None, None]

    def chunk(args):
        ci, qc, ic = args
        t0 = ci * MOBA_Q_CHUNK
        t = t0 + jnp.arange(MOBA_Q_CHUNK)
        cblk = t0 // MOBA_BLOCK
        ksel = kblk[bi, ki, ic]
        vsel = vblk[bi, ki, ic]
        s_sel = jnp.einsum('bqkgd,bqkgsnd->bqkgsn', qc, ksel).astype(jnp.float32) * scale
        slot_ok = jnp.arange(kk) < cblk
        s_sel = jnp.where(slot_ok[:, None], s_sel, NEG)
        kown = lax.dynamic_index_in_dim(kblk, cblk, axis=2, keepdims=False)
        vown = lax.dynamic_index_in_dim(vblk, cblk, axis=2, keepdims=False)
        s_own = jnp.einsum('bqkgd,bknd->bqkgn', qc, kown).astype(jnp.float32) * scale
        kpos = cblk * MOBA_BLOCK + jnp.arange(MOBA_BLOCK)
        causal = kpos[None, :] <= t[:, None]
        s_own = jnp.where(causal[None, :, None, None, :], s_own, NEG)
        nsel = kk * MOBA_BLOCK
        logits = jnp.concatenate([s_sel.reshape(B, MOBA_Q_CHUNK, kvh, G, nsel), s_own], axis=-1)
        p = jax.nn.softmax(logits, axis=-1).astype(v.dtype)
        o = jnp.einsum('bqkgm,bqkgmd->bqkgd', p[..., :nsel],
                       vsel.reshape(B, MOBA_Q_CHUNK, kvh, G, nsel, d))
        o = o + jnp.einsum('bqkgn,bknd->bqkgd', p[..., nsel:], vown)
        return o

    out = lax.map(chunk, (jnp.arange(nc), q_c, idx_c))
    return out.transpose(1, 0, 2, 3, 4, 5).reshape(B, S, H, d)

def second_inputs(seed: int = 0) -> dict:
    key = jax.random.key(seed)
    ks = jax.random.split(key, 7)
    x = jax.random.normal(ks[0], (BATCH, SEQ, D_MODEL), jnp.float32)
    norm_g = 1.0 + 0.02 * jax.random.normal(ks[1], (DEPTH_2, D_MODEL), jnp.float32)
    w_in_a = jax.random.normal(ks[2], (N_LAYERS_A, D_MODEL, IN_A), jnp.float32) * D_MODEL ** -0.5
    sinks_a = jax.random.normal(ks[3], (N_LAYERS_A, N_HEADS), jnp.float32)
    w_in_b = jax.random.normal(ks[4], (N_LAYERS_B, D_MODEL, IN_B), jnp.float32) * D_MODEL ** -0.5
    w_out = jax.random.normal(ks[5], (DEPTH_2, MIX_WIDTH, D_MODEL), jnp.float32) * MIX_WIDTH ** -0.5
    final_g = 1.0 + 0.02 * jax.random.normal(ks[6], (D_MODEL,), jnp.float32)
    return {"x": x, "norm_g": norm_g, "w_in_a": w_in_a, "sinks_a": sinks_a,
            "w_in_b": w_in_b, "w_out": w_out, "final_g": final_g}

def second_block(x, norm_g, w_in_a, sinks_a, w_in_b, w_out, final_g):
    B, S, _ = x.shape
    cos, sin = rope_tables(S)
    h = x
    for i in range(DEPTH_2):
        hn = rmsnorm_2(h, norm_g[i])
        j = i // N_MIXERS
        if i % N_MIXERS == 0:
            q, k, v, z = split_proj(hn, w_in_a[j], N_KV_A)
            q, k = apply_rope(q, cos, sin), apply_rope(k, cos, sin)
            o = sliding_window_sink_attention(q, k, v, sinks_a[j])
        else:
            q, k, v, z = split_proj(hn, w_in_b[j], N_KV_B)
            q, k = apply_rope(q, cos, sin), apply_rope(k, cos, sin)
            o = moba_attention(q, k, v)
        o = o.reshape(B, S, MIX_WIDTH) * jax.nn.silu(z)
        h = h + o @ w_out[i]
    return rmsnorm_2(h, final_g)


DEPTH_3 = 2

N_A_LAYERS = (DEPTH_3 + 1) // 2
N_B_LAYERS = DEPTH_3 // 2
N_VRES = max(N_B_LAYERS - 1, 0)

D_FF = 2816
CHUNK = 128
D_SGU = 2 * D_MODEL
SGU_GROUPS = 16
SGU_GROUP_DIM = D_SGU // SGU_GROUPS
RWKV_HEAD = 64
RWKV_HEADS = D_MODEL // RWKV_HEAD
DECAY_LORA = 64
AAA_LORA = 64
MV_LORA = 32
GATE_LORA = 160
GN_EPS = 64e-5
LN_EPS = 1e-5
DN_ALPHA = (2 * DEPTH_3) ** 0.25
DN_BETA = (8 * DEPTH_3) ** -0.25


def layer_norm(x, g, b, eps=LN_EPS):
    xf = x.astype(jnp.float32)
    mu = jnp.mean(xf, axis=-1, keepdims=True)
    var = jnp.mean(jnp.square(xf - mu), axis=-1, keepdims=True)
    return ((xf - mu) * lax.rsqrt(var + eps) * g + b).astype(x.dtype)

def swiglu(x, w_in, w_out):
    gate, up = jnp.split(x @ w_in, 2, axis=-1)
    return (jax.nn.silu(gate) * up) @ w_out

def sgu_mixer(x, w_in, b_in, ln_g, ln_b, w_sp, b_sp, w_out):
    bsz, seq, _ = x.shape
    z = jax.nn.gelu(x @ w_in + b_in, approximate=False)
    u, v = jnp.split(z, 2, axis=-1)
    v = layer_norm(v, ln_g, ln_b)
    n_chunks = seq // CHUNK
    v = v.reshape(bsz, n_chunks, CHUNK, SGU_GROUPS, SGU_GROUP_DIM)
    causal = jnp.tril(jnp.ones((CHUNK, CHUNK), dtype=bool))
    w = jnp.where(causal[None], w_sp, 0)
    mixed = jnp.einsum('gts,bcsgd->bctgd', w, v) + b_sp.T[None, None, :, :, None]
    mixed = mixed.reshape(bsz, seq, D_SGU)
    return (u * mixed) @ w_out

def rwkv7_scan(r, decay, k, v, a, b):
    def step(state, inp):
        r_t, w_t, k_t, v_t, a_t, b_t = inp
        sa = jnp.einsum('bhij,bhj->bhi', state, a_t)
        state = (state * w_t[:, :, None, :] + sa[..., None] * b_t[:, :, None, :]
                 + v_t[..., None] * k_t[:, :, None, :])
        y = jnp.einsum('bhij,bhj->bhi', state, r_t)
        return state, y
    s0 = jnp.zeros(r.shape[1:3] + (RWKV_HEAD, RWKV_HEAD), jnp.float32)
    _, y = lax.scan(step, s0, (r, decay, k, v, a, b))
    return y

def rwkv7_mixer(x, v_first, vres, mu, w_rkv, w0, w1, w2, a0, a1, a2,
                g1, g2, k_k, k_a, r_k, gn_g, gn_b, w_o):
    bsz, seq, d = x.shape
    H, N = RWKV_HEADS, RWKV_HEAD
    xx = jnp.pad(x, ((0, 0), (1, 0), (0, 0)))[:, :-1] - x
    x_rkv = x[None] + xx[None] * mu[:3, None, None, :]
    r, k, v = jnp.einsum('nbsd,nde->nbse', x_rkv, w_rkv)
    xw = x + xx * mu[3]
    xa = x + xx * mu[4]
    xg = x + xx * mu[5]
    w = -jax.nn.softplus(-(w0 + jnp.tanh(xw @ w1) @ w2)) - 0.5
    if vres is None:
        v_first = v
    else:
        v0, v1, v2 = vres
        xv = x + xx * mu[2]
        v = v + (v_first - v) * jax.nn.sigmoid(v0 + (xv @ v1) @ v2)
    a = jax.nn.sigmoid(a0 + (xa @ a1) @ a2)
    g = jax.nn.sigmoid(xg @ g1) @ g2
    kk = (k * k_k).reshape(bsz, seq, H, N).astype(jnp.float32)
    kk = kk / jnp.maximum(jnp.linalg.norm(kk, axis=-1, keepdims=True), 1e-12)
    k = k * (1 + (a - 1) * k_a)

    def heads(z):
        return z.reshape(bsz, seq, H, N).astype(jnp.float32)

    def tmaj(z):
        return jnp.moveaxis(z, 1, 0)

    r_h, k_h, v_h, a_h = heads(r), heads(k), heads(v), heads(a)
    decay = jnp.exp(-jnp.exp(heads(w)))
    y = rwkv7_scan(tmaj(r_h), tmaj(decay), tmaj(k_h), tmaj(v_h), tmaj(-kk), tmaj(kk * a_h))
    y = jnp.moveaxis(y, 0, 1)
    mean = jnp.mean(y, axis=-1, keepdims=True)
    var = jnp.mean(jnp.square(y - mean), axis=-1, keepdims=True)
    y = (y - mean) * lax.rsqrt(var + GN_EPS) * gn_g.reshape(H, N) + gn_b.reshape(H, N)
    bonus = jnp.sum(r_h * k_h * r_k, axis=-1, keepdims=True) * v_h
    out = ((y + bonus).reshape(bsz, seq, d).astype(x.dtype) * g) @ w_o
    return out, v_first

def third_inputs(seed: int = 0) -> dict:
    key = jax.random.key(seed)
    ks = iter(jax.random.split(key, 40))
    f32 = jnp.float32

    def nrm(shape, scale):
        return jax.random.normal(next(ks), shape, f32) * scale

    def unif(shape, lo, hi):
        return jax.random.uniform(next(ks), shape, f32, lo, hi)

    D = D_MODEL
    NA, NB, NV = N_A_LAYERS, N_B_LAYERS, N_VRES
    return {
        "x": nrm((BATCH, SEQ, D), 1.0),
        "ln_g": 1.0 + nrm((DEPTH_3, 3, D), 0.02),
        "ln_b": nrm((DEPTH_3, 3, D), 0.02),
        "ffn_w_in": nrm((DEPTH_3, 2, D, 2 * D_FF), D ** -0.5),
        "ffn_w_out": nrm((DEPTH_3, 2, D_FF, D), D_FF ** -0.5 * DN_BETA),
        "sgu_w_in": nrm((NA, D, 2 * D_SGU), D ** -0.5),
        "sgu_b_in": nrm((NA, 2 * D_SGU), 0.02),
        "sgu_ln_g": 1.0 + nrm((NA, D_SGU), 0.02),
        "sgu_ln_b": nrm((NA, D_SGU), 0.02),
        "sgu_w_sp": nrm((NA, SGU_GROUPS, CHUNK, CHUNK), CHUNK ** -0.5),
        "sgu_b_sp": 1.0 + nrm((NA, SGU_GROUPS, CHUNK), 0.02),
        "sgu_w_out": nrm((NA, D_SGU, D), D_SGU ** -0.5 * DN_BETA),
        "rwkv_mu": unif((NB, 6, D), 0.0, 1.0),
        "rwkv_w_rkv": nrm((NB, 3, D, D), D ** -0.5),
        "rwkv_w0": unif((NB, D), -6.0, -1.0),
        "rwkv_w1": nrm((NB, D, DECAY_LORA), D ** -0.5),
        "rwkv_w2": nrm((NB, DECAY_LORA, D), 0.1 * DECAY_LORA ** -0.5),
        "rwkv_a0": nrm((NB, D), 0.1),
        "rwkv_a1": nrm((NB, D, AAA_LORA), D ** -0.5),
        "rwkv_a2": nrm((NB, AAA_LORA, D), 0.5 * AAA_LORA ** -0.5),
        "rwkv_v0": nrm((NV, D), 0.1),
        "rwkv_v1": nrm((NV, D, MV_LORA), D ** -0.5),
        "rwkv_v2": nrm((NV, MV_LORA, D), 0.5 * MV_LORA ** -0.5),
        "rwkv_g1": nrm((NB, D, GATE_LORA), D ** -0.5),
        "rwkv_g2": nrm((NB, GATE_LORA, D), GATE_LORA ** -0.5),
        "rwkv_k_k": 0.85 + nrm((NB, D), 0.02),
        "rwkv_k_a": 1.0 + nrm((NB, D), 0.02),
        "rwkv_r_k": nrm((NB, RWKV_HEADS, RWKV_HEAD), 0.1),
        "rwkv_gn_g": 1.0 + nrm((NB, D), 0.02),
        "rwkv_gn_b": nrm((NB, D), 0.02),
        "rwkv_w_o": nrm((NB, D, D), D ** -0.5 * DN_BETA),
    }

def third_block(x, ln_g, ln_b, ffn_w_in, ffn_w_out, sgu_w_in, sgu_b_in, sgu_ln_g, sgu_ln_b,
              sgu_w_sp, sgu_b_sp, sgu_w_out, rwkv_mu, rwkv_w_rkv, rwkv_w0, rwkv_w1, rwkv_w2,
              rwkv_a0, rwkv_a1, rwkv_a2, rwkv_v0, rwkv_v1, rwkv_v2, rwkv_g1, rwkv_g2,
              rwkv_k_k, rwkv_k_a, rwkv_r_k, rwkv_gn_g, rwkv_gn_b, rwkv_w_o):
    v_first = None
    for i in range(DEPTH_3):
        x = layer_norm(DN_ALPHA * x + 0.5 * swiglu(x, ffn_w_in[i, 0], ffn_w_out[i, 0]),
                       ln_g[i, 0], ln_b[i, 0])
        j = i // N_MIXERS
        if i % N_MIXERS == 0:
            mix = sgu_mixer(x, sgu_w_in[j], sgu_b_in[j], sgu_ln_g[j], sgu_ln_b[j],
                            sgu_w_sp[j], sgu_b_sp[j], sgu_w_out[j])
        else:
            vres = None if v_first is None else (rwkv_v0[j - 1], rwkv_v1[j - 1], rwkv_v2[j - 1])
            mix, v_first = rwkv7_mixer(x, v_first, vres, rwkv_mu[j], rwkv_w_rkv[j], rwkv_w0[j],
                                       rwkv_w1[j], rwkv_w2[j], rwkv_a0[j], rwkv_a1[j], rwkv_a2[j],
                                       rwkv_g1[j], rwkv_g2[j], rwkv_k_k[j], rwkv_k_a[j],
                                       rwkv_r_k[j], rwkv_gn_g[j], rwkv_gn_b[j], rwkv_w_o[j])
        x = layer_norm(DN_ALPHA * x + mix, ln_g[i, 1], ln_b[i, 1])
        x = layer_norm(DN_ALPHA * x + 0.5 * swiglu(x, ffn_w_in[i, 1], ffn_w_out[i, 1]),
                       ln_g[i, 2], ln_b[i, 2])
    return x


_first_inputs = third_inputs


def third_inputs(seed=0):
    import zlib

    import numpy as np

    out = dict(_first_inputs(seed))
    spreads = {}
    factors = {'sgu_b_in': 7.761,
     'sgu_ln_g': 29.046,
     'sgu_ln_b': 29.849,
     'sgu_b_sp': 8.0,
     'rwkv_w1': 8.0,
     'rwkv_w2': 8.0,
     'rwkv_a0': 7.104,
     'rwkv_k_k': 24.541,
     'rwkv_k_a': 8.0,
     'rwkv_gn_g': 27.253,
     'rwkv_gn_b': 29.537}
    for name, (base, spread) in spreads.items():
        noise = np.random.default_rng([zlib.crc32(name.encode()), seed]).standard_normal(out[name].shape)
        drawn = base * np.exp(spread * noise) if base else spread * noise
        out[name] = __import__('jax').numpy.asarray(drawn.astype(out[name].dtype))
    for name, factor in factors.items():
        out[name] = (out[name] * factor).astype(out[name].dtype)
    return out


_narrow_inputs = third_inputs


def third_inputs(seed=0):

    out = dict(_narrow_inputs(seed))
    wider = {'sgu_b_sp': 3.8, 'rwkv_k_k': 4.03, 'rwkv_gn_g': 3.25, 'rwkv_gn_b': 3.17}
    for name, times in wider.items():
        mean = out[name].mean()
        out[name] = (mean + times * (out[name] - mean)).astype(out[name].dtype)
    return out


def setup_inputs(seed=0):
    out = dict(first_inputs(seed))
    for name, value in second_inputs(seed + 1).items():
        if name != "x":
            out[name + "_2"] = value
    for name, value in third_inputs(seed + 2).items():
        if name != "x":
            out[name + "_3"] = value
    return out


def reference(
    x, mem, attn_norm_g, mem_norm_g, w_in, w_mem_kv, da_lambda_q1, da_lambda_k1, da_lambda_q2,
    da_lambda_k2, da_subln_g, wa_sink, w_da_o, w_wa_o, w_xa_o, w_out, ffn_norm_g, w_router,
    w_exp_gate, w_exp_up, w_exp_down, final_norm_g, norm_g_2, w_in_a_2, sinks_a_2, w_in_b_2,
    w_out_2, final_g_2, ln_g_3, ln_b_3, ffn_w_in_3, ffn_w_out_3, sgu_w_in_3, sgu_b_in_3,
    sgu_ln_g_3, sgu_ln_b_3, sgu_w_sp_3, sgu_b_sp_3, sgu_w_out_3, rwkv_mu_3, rwkv_w_rkv_3,
    rwkv_w0_3, rwkv_w1_3, rwkv_w2_3, rwkv_a0_3, rwkv_a1_3, rwkv_a2_3, rwkv_v0_3, rwkv_v1_3,
    rwkv_v2_3, rwkv_g1_3, rwkv_g2_3, rwkv_k_k_3, rwkv_k_a_3, rwkv_r_k_3, rwkv_gn_g_3,
    rwkv_gn_b_3, rwkv_w_o_3,
):
    x = first_block(
        x, mem, attn_norm_g, mem_norm_g, w_in, w_mem_kv, da_lambda_q1, da_lambda_k1,
        da_lambda_q2, da_lambda_k2, da_subln_g, wa_sink, w_da_o, w_wa_o, w_xa_o, w_out,
        ffn_norm_g, w_router, w_exp_gate, w_exp_up, w_exp_down, final_norm_g,
    )
    x = second_block(
        x, norm_g_2, w_in_a_2, sinks_a_2, w_in_b_2, w_out_2, final_g_2,
    )
    return third_block(
        x, ln_g_3, ln_b_3, ffn_w_in_3, ffn_w_out_3, sgu_w_in_3, sgu_b_in_3, sgu_ln_g_3,
        sgu_ln_b_3, sgu_w_sp_3, sgu_b_sp_3, sgu_w_out_3, rwkv_mu_3, rwkv_w_rkv_3, rwkv_w0_3,
        rwkv_w1_3, rwkv_w2_3, rwkv_a0_3, rwkv_a1_3, rwkv_a2_3, rwkv_v0_3, rwkv_v1_3, rwkv_v2_3,
        rwkv_g1_3, rwkv_g2_3, rwkv_k_k_3, rwkv_k_a_3, rwkv_r_k_3, rwkv_gn_g_3, rwkv_gn_b_3,
        rwkv_w_o_3,
    )


_drawn_inputs = setup_inputs


def setup_inputs(seed=0):
    import zlib

    import numpy as np

    out = dict(_drawn_inputs(seed))
    spreads = {}
    factors = {'mem_norm_g': 2.672, 'da_lambda_k2': 4.067}
    for name, (base, spread) in spreads.items():
        noise = np.random.default_rng([zlib.crc32(name.encode()), seed]).standard_normal(out[name].shape)
        drawn = base * np.exp(spread * noise) if base else spread * noise
        out[name] = __import__('jax').numpy.asarray(drawn.astype(out[name].dtype))
    for name, factor in factors.items():
        out[name] = (out[name] * factor).astype(out[name].dtype)
    return out
```

```python
from contextlib import ExitStack

import numpy as np
import concourse.bass as bass
from concourse import mybir

F32 = mybir.dt.float32
ALU = mybir.AluOpType
ACT = mybir.ActivationFunctionType
AX = mybir.AxisListType
P = 128
T = 256
D = 1024
STOP = 99

NSLOT = 5
SLOT = 4096
BIG = 2048
NBIG = 10

VEC = {}
for _n, _c in (("attn_norm_g", 8), ("mem_norm_g", 8), ("ffn_norm_g", 8), ("final_norm_g", 8), ("norm_g_2", 16),
               ("final_g_2", 8), ("ln_g_3", 48), ("ln_b_3", 48), ("rwkv_mu_3", 48), ("rwkv_w0_3", 8),
               ("rwkv_a0_3", 8), ("rwkv_k_k_3", 8), ("rwkv_k_a_3", 8), ("rwkv_r_k_3", 8), ("sgu_b_in_3", 32),
               ("da_subln_g", 1)):
    VEC[_n] = (sum(c for _, c in VEC.values()), _c)
NVEC = sum(c for _, c in VEC.values())


def const_tables():
    p = np.arange(P)
    q = (np.arange(2)[None, :, None] * P + p[:, None, None]).astype(np.int64)
    k = np.arange(T)[None, None, :]
    dist = np.abs(q - k)
    out = {}
    out["ident"] = np.eye(P)
    out["d1"] = dist.reshape(P, -1)
    out["d2"] = np.where(dist <= 128, dist, 1e32).reshape(P, -1)
    out["ma"] = np.where((q - k >= 0) & (q - k < 128), 0.0, -1e30).reshape(P, -1)
    out["mb"] = np.where(q - k >= 0, 0.0, -1e30).reshape(P, -1)
    inv = np.float32(10000.0) ** (-np.arange(0, 64, 2, dtype=np.float32) / np.float32(64))
    ang = np.arange(T, dtype=np.float32)[None, :] * inv[p % 32][:, None].astype(np.float32)
    out["cos"] = np.cos(ang)
    out["sin"] = np.sin(ang)
    r = np.zeros((P, P))
    for m in range(P):
        if m % 64 < 32:
            r[m + 32, m] = -1.0
        else:
            r[m - 32, m] = 1.0
    out["rot"] = r
    out["ones"] = np.full((P, P), 1.0 / 1024)
    out["iota32"] = np.tile(np.arange(32), (P, 1))
    tt = p % 64
    s = np.arange(64)[None, :]
    t = tt[:, None]
    out["low"] = (s < t) * 1.0
    out["upp"] = (t < s) * 1.0
    out["uppi"] = (t <= s) * 1.0
    out["eye64"] = (t == s) * 1.0
    for i, b in enumerate((1, 2, 4, 8, 16, 32)):
        same = (t // (2 * b)) == (s // (2 * b))
        out["ml%d" % i] = (same & (t % (2 * b) >= b) & (s % (2 * b) < b)) * 1.0
        out["mu%d" % i] = (same & (t % (2 * b) < b) & (s % (2 * b) >= b)) * 1.0
    out["reset"] = np.tile((np.arange(T) % 64 != 0) * 1.0, (P, 1))
    sel = np.zeros((P, 8, 16))
    selt = np.zeros((P, 8, P))
    for f in range(8):
        for h in range(2):
            sel[64 * h:64 * h + 64, f, 2 * f + h] = 1.0
            selt[2 * f + h, f, 64 * h:64 * h + 64] = 1.0
    out["sel"] = sel.reshape(P, -1)
    out["selt"] = selt.reshape(P, -1)
    return {n: a.astype(np.float32) for n, a in out.items()}


CT = {n: a.shape[1] for n, a in const_tables().items()}
LATE = [n for n in CT if n in ("low", "upp", "uppi", "eye64", "reset", "sel", "selt") or n[:2] in ("ml", "mu")]
EARLY = [n for n in CT if n not in LATE]
COFF = {}
for _l in (EARLY, LATE):
    _o = 0
    for _n in _l:
        COFF[_n] = _o
        _o += CT[_n]
NCONST = sum(CT[n] for n in EARLY)


class Queue:

    def __init__(self, sem):
        self.sem = sem
        self.n = 0
        self.ops = []
        self.seen = {}

    def wait(self, toks):
        for t in toks:
            if t is None:
                continue
            if isinstance(t, list):
                self.wait(t)
                continue
            key, sem, v = t
            if self.seen.get(key, 0) < v:
                self.seen[key] = v
                self.ops.append(lambda e, sem=sem, v=v: e.wait_ge(sem, v))

    def do(self, fn, *toks, inc=True):
        self.wait(toks)
        if not inc:
            self.ops.append(fn)
            return None
        self.n += 1
        self.ops.append(lambda e, fn=fn: fn(e).then_inc(self.sem, 1))
        return (id(self), self.sem, self.n)

    def now(self):
        return (id(self), self.sem, self.n) if self.n else None

    def play(self, e):
        for op in self.ops:
            op(e)


def MM(o, l, r, start, stop, skip=False):
    return lambda e: e.matmul(o, l, r, start=start, stop=stop, skip_group_check=skip)


def TR(o, i, ident):
    return lambda e: e.transpose(o, i, ident)


def TT(o, a, b, op):
    return lambda e: e.tensor_tensor(o, a, b, op)


def TS(o, a, s1, s2, op0, op1=None):
    if op1 is None:
        return lambda e: e.tensor_scalar(o, a, s1, None, op0)
    return lambda e: e.tensor_scalar(o, a, s1, s2, op0, op1)


def STT(o, a, s, b, op0, op1):
    return lambda e: e.scalar_tensor_tensor(out=o, in0=a, scalar=s, in1=b, op0=op0, op1=op1)


def CP(o, i):
    return lambda e: e.tensor_copy(o, i)


def RCP(o, i):
    return lambda e: e.reciprocal(o, i)


def RED(o, i, op, neg=False):
    if neg:
        return lambda e: e.tensor_reduce(o, i, AX.X, op, negate=True)
    return lambda e: e.tensor_reduce(o, i, AX.X, op)


def AC(o, i, f, **kw):
    return lambda e: e.activation(o, i, f, **kw)


def build(nc, A, out):
    ctx = ExitStack()
    with ctx:
        def sb(name, cols):
            return ctx.enter_context(nc.sbuf_tensor(name, [P, cols], F32))

        def sem(name):
            return ctx.enter_context(nc.semaphore(name))

        ring = sb("ring", NSLOT * SLOT)
        big = sb("big", NBIG * BIG)
        cst = sb("cst", NCONST)
        vec = sb("vec", NVEC)
        xw = sb("xw", 3 * 1024)
        ptw = sb("ptw", 1024)
        tw = sb("tw", 4 * 512)
        sm = sb("sm", 1024)
        ps = ctx.enter_context(nc.psum_tensor("ps", [P, 8, 512], F32))

        PE, DV, AT, PO, SP = (Queue(sem(n)) for n in ("s_pe", "s_dve", "s_act", "s_pool", "s_sp"))
        ld_sem = [sem("s_ld%d" % i) for i in range(NSLOT)]
        ld_n = [0] * NSLOT
        sc_sem = sem("s_small")
        out_sem = sem("s_out")
        side_sem = sem("s_side")
        ldc = [0]

        def C(name):
            return (xw if name in LATE else cst)[:, COFF[name]:COFF[name] + CT[name]]

        def V(name, i=0):
            o = VEC[name][0] + i
            return vec[:, o:o + 1]

        def Vs(name, i, n):
            o = VEC[name][0] + i
            return vec[:, o:o + n]

        def B(i, n=1):
            return big[:, i * BIG:(i + n) * BIG]

        def F(ap, n=8):
            return ap.rearrange("p (f t) -> p f t", f=n)

        IDN = C("ident")

        bank_rel = [[] for _ in range(8)]

        class Banks:
            def __init__(self, ids):
                self.ids, self.i = ids, 0

            def get(self):
                b = self.ids[self.i % len(self.ids)]
                self.i += 1
                w = bank_rel[b]
                bank_rel[b] = []
                return b, w

        def free_bank(b, *toks):
            bank_rel[b] = list(toks)

        slots = list(range(NSLOT))
        slot_i = [0]
        slot_rel = [[] for _ in range(NSLOT)]

        def load(*parts):
            s = slots[slot_i[0] % len(slots)]
            slot_i[0] += 1
            SP.wait(slot_rel[s])
            slot_rel[s] = []
            base = ring[:, s * SLOT:(s + 1) * SLOT]
            for view, src in parts:
                def go(e, dst=view(base), src=src, q=ld_sem[s]):
                    e.dma_start(dst, src).then_inc(q, 16)
                SP.ops.append(go)
                ld_n[s] += 16
            return s, base, ("ld%d" % s, ld_sem[s], ld_n[s])

        def free_slot(s, *toks):
            slot_rel[s] = list(toks)

        def bar():
            return [q.now() for q in (PE, DV, AT, PO) if q.now()]

        def small(dst, src):
            def go(e, dst=dst, src=src):
                e.dma_start(dst, src).then_inc(sc_sem, 16)
            AT.ops.append(go)
            ldc[0] += 16

        small(B(0), A["xT"])
        small(cst[:, :], A["consts"])
        small(vec[:, :], A["vecs"])
        small(B(2), A["memT"])
        SINK = sm[:, 0:32]
        small(sm[:, 0:16], A["wa_sink"].partition_broadcast(P))
        small(sm[:, 16:32], A["sinks_a_2"].partition_broadcast(P))
        LAM = sm[:, 32:288].rearrange("p (a b) -> p a b", a=4)
        for i, n in enumerate(("da_lambda_q1", "da_lambda_k1", "da_lambda_q2", "da_lambda_k2")):
            small(LAM[:, i, :], A[n].partition_broadcast(P))
        CONST = ("const", sc_sem, ldc[0])
        NSINK = sm[:, 288:320]
        LV = sm[:, 320:328]
        ST = sm[:, 384:512].rearrange("p (r c) -> p r c", r=4)
        RSTD = sm[:, 512:768]
        SM2 = sm[:, 768:1024]

        DB = Banks([0, 1])
        KB = Banks([0, 1, 2, 3, 4, 5, 6, 7])

        def fmsum(src, n, bank, w, *toks):
            for f in range(n):
                t = PE.do(MM(ps[:, bank, 0:T], C("ones"), src[:, f, :], f == 0, f == n - 1),
                          *(w + list(toks) if f == 0 else ()), inc=f == n - 1)
            return t

        def rstd_of(src, tmp, eps, banks, *toks):
            t = AT.do(AC(tmp, src, ACT.Square), *toks)
            b, w = banks.get()
            t = fmsum(F(tmp), 8, b, w, t)
            t = DV.do(TS(RSTD, ps[:, b, 0:T], eps, None, ALU.add), t, AT.now())
            free_bank(b, t)
            t = AT.do(AC(RSTD, RSTD, ACT.Sqrt), t)
            return DV.do(RCP(RSTD, RSTD), t)

        def rms(src, tmp, dst, eps, g, banks, *toks):
            t = rstd_of(src, tmp, eps, banks, *toks)
            r = []
            for f in range(8):
                r.append(DV.do(STT(F(dst)[:, f, :], F(src)[:, f, :], g(f), RSTD, ALU.mult, ALU.mult), t))
            return r

        def ln(y, tmp, dst, eps, g, b_, banks, *toks):
            b, w = banks.get()
            t = fmsum(F(y), 8, b, w, *toks)
            mu = ps[:, b, 0:T].unsqueeze(1).broadcast_to((P, 8, T))
            t = DV.do(TT(F(y), F(y), mu, ALU.subtract), t)
            free_bank(b, t)
            t0 = t
            t = rstd_of(y, tmp, eps, banks, t)
            r = []
            for f in range(8):
                a = DV.do(STT(F(tmp)[:, f, :], F(y)[:, f, :], g(f), RSTD, ALU.mult, ALU.mult), t, PE.now())
                r.append(AT.do(AC(F(dst)[:, f, :], F(tmp)[:, f, :], ACT.Identity, bias=b_(f)), a, t0))
            return r

        def fm(x, slot_view, nt, evac, ready, banks):
            last = None
            nk = slot_view.shape[1]
            for j in range((nt + 1) // 2):
                b, w = banks.get()
                m = min(2, nt - 2 * j)
                for i in range(m):
                    for k in range(nk):
                        c = (2 * j + i) * P
                        t = PE.do(MM(ps[:, b, i * T:(i + 1) * T], slot_view[:, k, c:c + P], x[:, k, :],
                                     k == 0, k == nk - 1),
                                  *((w, ready) if i == 0 and k == 0 else ()), inc=(i == m - 1 and k == nk - 1))
                free_bank(b, *evac(j, ps[:, b, 0:m * T].rearrange("p (i t) -> p i t", t=T), t))
                last = t
                yield last

        def run(g):
            last = None
            for last in g:
                pass
            return last

        def wk(src, c0, n=512):
            return (lambda s: s[:, 0:8 * n].rearrange("p (k n) -> p k n", k=8),
                    src.rearrange("(k p) n -> p k n", p=P)[:, :, c0:c0 + n])

        def proj_fm(x, src, c0, ncols, evac, ready, banks):
            for c in range(0, ncols, 512):
                n = min(512, ncols - c)
                s, base, tl = load(wk(src, c0 + c, n))
                v = base[:, 0:8 * n].rearrange("p (k n) -> p k n", k=8)
                last = None
                for last in fm(x, v, n // P, lambda j, bk, t, c=c: evac(c // 256 + j, bk, t), [ready, tl], banks):
                    yield last
                free_slot(s, last)

        def proj_tm(x, src, c0, ncols, evac, ready, banks):
            for c in range(0, ncols, 512):
                n = min(512, ncols - c)
                s, base, tl = load(wk(src, c0 + c, n))
                v = base[:, 0:8 * n].rearrange("p (k n) -> p k n", k=8)
                for tt in range(2):
                    b, w = banks.get()
                    for k in range(8):
                        t = PE.do(MM(ps[:, b, 0:n], x[:, k, tt * P:(tt + 1) * P], v[:, k, :], k == 0, k == 7),
                                  *((w, ready, tl) if k == 0 else ()), inc=k == 7)
                    free_bank(b, *evac(tt, c, ps[:, b, 0:n], t))
                    if tt == 1:
                        free_slot(s, t)
                    yield t

        def proj_dup(x, src, c0, nkv, evac, ready, banks):
            sv = src.rearrange("(k p) n -> p k n", p=P)[:, :, c0:c0 + 64 * nkv].rearrange("p k (j e) -> p k j e", e=64)
            n = 128 * nkv
            def at(s, d):
                return s[:, 0:8 * n].rearrange("p (k j d e) -> p k j d e", k=8, d=2, e=64)[:, :, :, d, :]
            parts = []
            for j in range(nkv):
                for d in range(2):
                    parts.append((lambda s, d=d, j=j: at(s, d)[:, :, j, :], sv[:, :, j, :]))
            s, base, tl = load(*parts)
            v = base[:, 0:8 * n].rearrange("p (k n) -> p k n", k=8)
            last = None
            for last in fm(x, v, nkv, evac, [ready, tl], banks):
                yield last
            free_slot(s, last)

        def acc_fm(x, nk, src, evac, ready, banks4, x_ready=None):
            bk = [banks4.get() for _ in range(4)]
            sv = src.rearrange("(k p) n -> p k n", p=P)
            for k0 in range(0, nk, 4):
                n = min(4, nk - k0)
                s, base, tl = load((lambda q, n=n: q[:, 0:n * 1024].rearrange("p (k n) -> p k n", k=n),
                                    sv[:, k0:k0 + n, :]))
                v = base[:, 0:n * 1024].rearrange("p (k n) -> p k n", k=n)
                for kk in range(n):
                    k = k0 + kk
                    for f in range(8):
                        b, w = bk[f // 2]
                        i = f % 2
                        t = PE.do(MM(ps[:, b, i * T:(i + 1) * T], v[:, kk, f * P:(f + 1) * P], x[:, k, :],
                                     k == 0 and i == 0, k == nk - 1, skip=True),
                                  *((ready, w, tl) if k == 0 else (tl,)), inc=(k == nk - 1 and i == 1) or (kk == n - 1 and f == 7))
                        if k == nk - 1 and i == 1:
                            free_bank(b, *evac(f // 2, ps[:, b, :].rearrange("p (i t) -> p i t", t=T), t))
                free_slot(s, PE.now())
                yield PE.now()

        def cp_act(dst, scale=None):
            def f(j, bk, t):
                n = bk.shape[1]
                kw = {} if scale is None else {"scale": scale}
                return [AT.do(AC(dst[:, 2 * j:2 * j + n, :], bk, ACT.Copy, **kw), t)]
            return f

        def cp_tm(dst):
            def f(tt, c, bk, t):
                return [AT.do(AC(dst[:, tt, c:c + bk.shape[1]], bk, ACT.Copy), t)]
            return f

        def to_tm(src, dst, banks, *toks):
            r = []
            first = True
            for tt in range(2):
                for h in range(2):
                    b, w = banks.get()
                    for i in range(4):
                        f = 4 * h + i
                        t = PE.do(TR(ps[:, b, i * P:(i + 1) * P], src[:, f, tt * P:(tt + 1) * P], IDN),
                                  *((w, *toks) if i == 0 else ()), inc=i == 3)
                    q = DV if h else AT
                    o = dst[:, tt, h * 512:(h + 1) * 512]
                    fn = CP(o, ps[:, b, :]) if h else AC(o, ps[:, b, :], ACT.Copy)
                    t = q.do(fn, t)
                    free_bank(b, t)
                    r.append(t)
            return r

        def to_fm(src, evac, banks, *toks):
            r = []
            for j in range(4):
                b, w = banks.get()
                for i in range(2):
                    for tt in range(2):
                        f = 2 * j + i
                        t = PE.do(TR(ps[:, b, i * T + tt * P:i * T + (tt + 1) * P], src[:, tt, f * P:(f + 1) * P], IDN),
                                  *((w, *toks) if i == 0 and tt == 0 else ()), inc=(i == 1 and tt == 1))
                q = evac(j, ps[:, b, :].rearrange("p (i t) -> p i t", t=T), t)
                free_bank(b, *q)
                r += q
            return r

        S2 = Banks([2])
        PT2 = Banks([4])
        OB = Banks([6, 7])
        xfree = [[], [], []]
        ptfree = [[]]

        def attention(units, ready, done):
            state = []

            def stage_a(i, u):
                X = xw[:, (i % 3) * 1024:(i % 3 + 1) * 1024].rearrange("p (m c) -> p m c", m=2)
                st = ST[:, i % 4, :]
                b0, w0 = S2.get()
                w0 = w0 + bank_rel[b0 + 1]
                for m in range(2):
                    for qt in range(2):
                        t = u["scores"](m, qt, ps[:, b0 + m, qt * T:(qt + 1) * T], [w0, ready] if m + qt == 0 else [], qt == 1 and m == 1)
                S = ps[:, b0:b0 + 2, :]
                wx = xfree[i % 3]
                if u["bias"] is None:
                    tx = DV.do(CP(X, S), t, wx)
                elif len(u["bias"]) == 1:
                    tab, fac = u["bias"][0]
                    tx = DV.do(STT(X, tab.unsqueeze(1).broadcast_to((P, 2, 512)), fac, S, ALU.mult, ALU.add), t, wx)
                else:
                    for m, (tab, fac) in enumerate(u["bias"]):
                        tx = DV.do(STT(X[:, m, :], tab, fac, S[:, m, :], ALU.mult, ALU.add), t, wx)
                free_bank(b0, tx)
                free_bank(b0 + 1, tx)
                X4 = X.rearrange("p m (q k) -> p (m q) k", q=2)
                nm, s, r = st[:, 0:4], st[:, 4:8], st[:, 8:12]
                t = DV.do(RED(nm, X4, ALU.max, neg=True), tx)
                sink = u["sink"]
                if sink is not None:
                    ns = NSINK[:, sink:sink + 2].unsqueeze(2).broadcast_to((P, 2, 2))
                    sk = SINK[:, sink:sink + 2].unsqueeze(2).broadcast_to((P, 2, 2))
                    n3 = nm.rearrange("p (m q) -> p m q", m=2)
                    t = DV.do(TT(n3, n3, ns, ALU.min), t)
                    e3 = st[:, 12:16].rearrange("p (m q) -> p m q", m=2)
                    te = DV.do(TT(e3, n3, sk, ALU.add), t)
                for g in range(4):
                    ta = AT.do(AC(X4[:, g, :], X4[:, g, :], ACT.Exp, bias=nm[:, g:g + 1], accum_out=s[:, g:g + 1]), t)
                if sink is not None:
                    ta = AT.do(AC(st[:, 12:16], st[:, 12:16], ACT.Exp), te)
                return X4, st, ta

            def stage_b(i, u, X4, st, ta):
                s, r = st[:, 4:8], st[:, 8:12]
                if u["sink"] is not None:
                    ta = DV.do(TT(s, s, st[:, 12:16], ALU.add), ta)
                t = DV.do(RCP(r, s), ta)
                if u["lam"] is not None:
                    t = DV.do(TS(r[:, 2:4], r[:, 2:4], u["lam"], None, ALU.mult), t)
                    maps = [0]
                    for qt in range(2):
                        t2 = DV.do(TS(X4[:, 2 + qt, :], X4[:, 2 + qt, :], r[:, 2 + qt:3 + qt], None, ALU.mult), t)
                        tn = DV.do(STT(X4[:, qt, :], X4[:, qt, :], r[:, qt:qt + 1], X4[:, 2 + qt, :], ALU.mult, ALU.add), t2)
                else:
                    maps = [0, 1]
                    for g in range(4):
                        tn = DV.do(TS(X4[:, g, :], X4[:, g, :], r[:, g:g + 1], None, ALU.mult), t)
                PT = ptw[:, :].rearrange("p (m k q) -> p m k q", m=2, k=2)
                tp = []
                for m in maps:
                    b = 4 + m
                    w = bank_rel[b]
                    for kt in range(2):
                        for qt in range(2):
                            t = PE.do(TR(ps[:, b, kt * T + qt * P:kt * T + (qt + 1) * P],
                                         X4[:, 2 * m + qt, kt * P:(kt + 1) * P], IDN),
                                      *((w, tn) if kt + qt == 0 else ()), inc=kt + qt == 2)
                    q = AT.do(AC(PT[:, m, :, :], ps[:, b, :].rearrange("p (k q) -> p k q", k=2), ACT.Copy), t, ptfree[0])
                    free_bank(b, q)
                    tp.append(q)
                xfree[i % 3] = [PE.now()]
                ptfree[0] = u["pv"](PT, tp)
                done.append(ptfree[0])

            prev = None
            for i, u in enumerate(units):
                a = stage_a(i, u)
                yield
                if prev is not None:
                    stage_b(*prev)
                prev = (i, u, *a)
                yield
            stage_b(*prev)
            yield

        def par(a, b, ra=1, rb=1):
            live = [a, b]
            while live:
                for g, n in ((a, ra), (b, rb)):
                    for _ in range(n):
                        if g in live:
                            try:
                                next(g)
                            except StopIteration:
                                live.remove(g)

        def pv_pair(fns, ob=OB):
            v, dst = fns

            def go(PT, tp):
                b, w = ob.get()
                for m in range(2):
                    for kt in range(2):
                        t = PE.do(MM(ps[64 * m:64 * m + 64, b, 0:T], v(m, kt), PT[:, m, kt, :], kt == 0, kt == 1),
                                  *((w, tp) if m + kt == 0 else ()), inc=(m == 1 and kt == 1))
                d = AT.do(AC(dst, ps[:, b, 0:T], ACT.Copy), t)
                free_bank(b, d)
                return [t, d]
            return go

        def score_pair(q, k):
            def go(m, qt, o, w, inc):
                return PE.do(MM(o, q(m)[:, qt * P:(qt + 1) * P], k(m), True, True), *w, inc=inc)
            return go

        DV.wait([CONST])
        PE.wait([CONST])
        AT.wait([CONST])
        PO.wait([CONST])
        DV.do(TS(NSINK, SINK, -1.0, None, ALU.mult))
        lt = tw[:, 0:128].rearrange("p (a b) -> p a b", a=2)
        t = DV.do(TT(lt[:, 0, :], LAM[:, 0, :], LAM[:, 1, :], ALU.mult))
        t = DV.do(TT(lt[:, 1, :], LAM[:, 2, :], LAM[:, 3, :], ALU.mult))
        t = DV.do(RED(LV[:, 0:2], lt, ALU.add), t)
        t = AT.do(AC(LV[:, 2:4], LV[:, 0:2], ACT.Exp), t)
        t = DV.do(TT(LV[:, 4:5], LV[:, 3:4], LV[:, 2:3], ALU.subtract), t)
        lam_init = 0.8 - 0.6 * float(np.exp(-0.3 * 0))
        t = DV.do(TS(LV[:, 5:6], LV[:, 4:5], -lam_init, None, ALU.add), t)
        NLAM = LV[:, 5:6]
        t = DV.do(TS(LV[:, 6:7], V("da_subln_g"), 1.0 - lam_init, None, ALU.mult))
        SUBG = LV[:, 6:7]

        x, ht, mt = B(0), B(1), B(2)
        tm_ = rms(x, B(9), ht, 1e-6, lambda f: V("attn_norm_g", f), KB)
        tm2 = rms(mt, B(9), mt, 1e-6, lambda f: V("mem_norm_g", f), KB, tm_)
        H, M = F(ht), F(mt)
        W1 = A["w_in"]
        daq, dak, dav, waq, wakv, xaq, mk = B(3), B(4), B(5), B(6), B(7), B(8), B(9)
        wak = F(wakv[:, 0:1024], 4)
        wav = wakv[:, 1024:1536].rearrange("p (t n) -> p t n", t=2)
        mv = B(2)
        xtm = lambda b: b.rearrange("p (t n) -> p t n", t=2)
        WK = A["w_mem_kv"]
        for g in (proj_fm(H, W1, 0, 1024, cp_act(F(daq), 0.125), tm_, KB),
                  proj_fm(H, W1, 1024, 1024, cp_act(F(dak)), tm_, KB),
                  proj_tm(H, W1, 2048, 1024, cp_tm(xtm(dav)), tm_, KB)):
            run(g)
        tda = bar()

        oda = []
        OT = xtm(ptw[:, 0:1])if False else None
        odt = B(2)

        run(proj_fm(M, WK, 0, 1024, cp_act(F(mk)), [tm2, bar()], KB))
        run(proj_tm(M, WK, 1024, 1024, cp_tm(xtm(xaq)), tm2, KB))
        mvb, xaqb = xaq, None
        tmv = bar()
        ODT = xtm(odt)

        def da_units():
            for h in range(8):
                def pv(PT, tp, h=h):
                    b, w = OB.get()
                    for qt in range(2):
                        for kt in range(2):
                            t = PE.do(MM(ps[:, b, qt * P:(qt + 1) * P], PT[:, 0, kt, qt * P:(qt + 1) * P],
                                         xtm(dav)[:, kt, h * P:(h + 1) * P], kt == 0, kt == 1),
                                      *((w, tp) if qt + kt == 0 else ()), inc=qt + kt == 2)
                    d = AT.do(AC(ODT[:, :, h * P:(h + 1) * P], ps[:, b, 0:T].rearrange("p (q e) -> p q e", q=2),
                                 ACT.Copy), t, tmv)
                    free_bank(b, d)
                    return [t, d]
                slope = 2.0 ** (-(h + 1))
                yield {"scores": score_pair(lambda m, h=h: F(daq)[64 * m:64 * m + 64, h, :],
                                            lambda m, h=h: F(dak)[64 * m:64 * m + 64, h, :]),
                       "bias": [(C("d1"), -slope)], "sink": None, "lam": NLAM, "pv": pv}

        def dense_a():
            yield from proj_fm(H, W1, 3072, 1024, cp_act(F(waq), 0.125), tm_, DB)
            yield from proj_dup(H, W1, 4096, 4, cp_act(wak), tm_, DB)
            yield from proj_tm(H, W1, 4352, 256, cp_tm(wav), tm_, DB)

        par(attention(da_units(), tda, oda), dense_a(), 2, 1)
        twa = bar()

        def wa_units():
            for j in range(8):
                kv = j // 2
                slopes = [float(np.exp2(np.float32(-8.0) * np.float32(h + 1) / np.float32(16))) for h in (2 * j, 2 * j + 1)]
                yield {"scores": score_pair(lambda m, j=j: F(waq)[64 * m:64 * m + 64, j, :],
                                            lambda m, kv=kv: wak[64 * m:64 * m + 64, kv, :]),
                       "bias": [(C("d2"), -slopes[0]), (C("d2"), -slopes[1])], "sink": 2 * j, "lam": None,
                       "pv": pv_pair((lambda m, kt, kv=kv: wav[:, kt, kv * 64:kv * 64 + 64], F(waq)[:, j, :]))}

        def da_norm():
            sq = B(4)
            o16 = odt.rearrange("p (a e) -> p a e", e=P)
            t = AT.do(AC(sq, odt, ACT.Square), twa)
            r16 = SM2[:, 0:16]
            t = DV.do(RED(r16, sq.rearrange("p (a e) -> p a e", e=P), ALU.add), t)
            t = DV.do(TS(r16, r16, 1.0 / 128, 1e-6, ALU.mult, ALU.add), t)
            t = AT.do(AC(r16, r16, ACT.Sqrt), t)
            t = DV.do(RCP(r16, r16), t)
            t = DV.do(TT(o16, o16, r16.unsqueeze(2).broadcast_to((P, 16, P)), ALU.mult), t)
            return t

        t = da_norm()
        to_fm(ODT, lambda j, bk, t: [AT.do(AC(F(daq)[:, 2 * j:2 * j + 2, :], bk, ACT.Copy, scale=SUBG), t)], DB, t)
        tod = bar()
        ODA = F(daq)
        merged = B(5)
        xq2 = B(4)

        def branch(n, o, wname, ready, banks, add):
            ga = W1
            gi = [0]
            for c in range(0, 1024, 512):
                gt = tw[:, :].rearrange("p (i j t) -> p i j t", i=2, j=4) if False else None
                sg, bg, tg = load(wk(ga, 5632 + n * 1024 + c))
                vg = bg[:, :].rearrange("p (k n) -> p k n", k=8)
                sw, bw, tw_ = load(wk(A[wname], c))
                vw = bw[:, :].rearrange("p (k n) -> p k n", k=8)
                for j in range(2):
                    jj = c // 256 + j
                    G = tw[:, (jj % 2) * 512:(jj % 2 + 1) * 512].rearrange("p (i t) -> p i t", t=T)
                    toks = {}

                    def ev_g(_, bk, t, G=G, toks=toks, jj=jj):
                        toks["g"] = AT.do(AC(G, bk, ACT.Sigmoid), t, gfree[jj % 2])
                        return [toks["g"]]

                    def ev_w(_, bk, t, G=G, toks=toks, jj=jj):
                        dst = F(merged)[:, 2 * jj:2 * jj + 2, :]
                        if not add:
                            q = DV.do(TT(dst, bk, G, ALU.mult), t, toks["g"])
                            gfree[jj % 2] = [q]
                            return [q]
                        q = DV.do(TT(G, bk, G, ALU.mult), t, toks["g"])
                        q2 = PO.do(TT(dst, dst, G, ALU.add), q)
                        gfree[jj % 2] = [q2]
                        return [q]
                    yield from fm(H, vg[:, :, j * 256:(j + 1) * 256], 2, ev_g, tg, banks)
                    if j == 1:
                        free_slot(sg, PE.now())
                    yield from fm(o, vw[:, :, j * 256:(j + 1) * 256], 2, ev_w, [ready, tw_], banks)
                    if j == 1:
                        free_slot(sw, PE.now())

        gfree = [[], []]

        def dense_b():
            yield from proj_fm(H, W1, 4608, 1024, cp_act(F(xq2), 0.0625), tod, DB)
            yield from branch(0, ODA, "w_da_o", tod, DB, False)

        owa = []
        par(attention(wa_units(), twa, owa), dense_b(), 2, 1)
        txa = bar()

        def xa_units():
            for h in range(0, 4, 2):
                def scores(m, qt, o, w, inc, h=h):
                    for kk in range(2):
                        f = 2 * (h + m) + kk
                        t = PE.do(MM(o, F(xq2)[:, f, qt * P:(qt + 1) * P], F(mk)[:, f, :], kk == 0, kk == 1),
                                  *(w if kk == 0 else ()), inc=inc and kk == 1)
                    return t

                def pv(PT, tp, h=h):
                    r = []
                    for m in range(2):
                        b, w = OB.get()
                        for e in range(2):
                            for kt in range(2):
                                c = (h + m) * 256 + e * P
                                t = PE.do(MM(ps[:, b, e * T:(e + 1) * T], xtm(mvb)[:, kt, c:c + P], PT[:, m, kt, :],
                                             kt == 0, kt == 1), *((w, tp) if e + kt == 0 else ()), inc=e + kt == 2)
                        f = 2 * (h + m)
                        d = AT.do(AC(F(xq2)[:, f:f + 2, :], ps[:, b, :].rearrange("p (e t) -> p e t", t=T), ACT.Copy), t)
                        free_bank(b, d)
                        r += [t, d]
                    return r
                yield {"scores": scores, "bias": None, "sink": None, "lam": None, "pv": pv}

        oxa = []
        par(attention(xa_units(), txa, oxa), branch(1, F(waq), "w_wa_o", txa, DB, True), 1, 1)
        txo = bar()
        run(branch(2, F(xq2), "w_xa_o", txo, DB, True))
        tmg = bar()
        X = F(x)

        def resid(j, bk, t, scale=None):
            d = X[:, 2 * j:2 * j + 2, :]
            if scale is None:
                return [DV.do(TT(d, bk, d, ALU.add), t)]
            return [DV.do(STT(d, d, scale, bk, ALU.mult, ALU.add), t)]
        run(proj_fm(F(merged), A["w_out"], 0, 1024, resid, tmg, KB))
        t1 = bar()

        def finish(src):
            SP.wait(bar())

            def go(e, src=src):
                e.dma_start(out, src).then_inc(out_sem, 16)
            SP.ops.append(go)

        def fin():
            blk = ctx.enter_context(nc.Block())

            @blk.sync
            def _(e):
                SP.play(e)
                e.wait_ge(out_sem, 16)

            @blk.tensor
            def _(e):
                PE.play(e)

            @blk.scalar
            def _(e):
                AT.play(e)

            @blk.vector
            def _(e):
                DV.play(e)

            @blk.gpsimd
            def _(e):
                PO.play(e)

        if STOP == 1:
            finish(x)
            return fin()
        sd = [0]

        def side(dst, src, *toks):
            PO.wait(toks)

            def go(e, dst=dst, src=src):
                e.dma_start(dst, src).then_inc(side_sem, 16)
            PO.ops.append(go)
            sd[0] += 16
            return ("side", side_sem, sd[0])

        h2 = B(1)
        th = rms(x, B(9), h2, 1e-6, lambda f: V("ffn_norm_g", f), KB, t1)
        H2T = xtm(B(2))
        s, base, tl = load((lambda q: q[:, 0:128].rearrange("p (k n) -> p k n", k=8),
                            A["w_router"].rearrange("(k p) n -> p k n", p=P)))
        wr = base[:, 0:128].rearrange("p (k n) -> p k n", k=8)
        b, w = KB.get()
        for tt in range(2):
            for k in range(8):
                t = PE.do(MM(ps[:, b, tt * 16:tt * 16 + 16], F(h2)[:, k, tt * P:(tt + 1) * P], wr[:, k, :], k == 0, k == 7),
                          *((w, th, tl) if k + tt == 0 else ()), inc=k == 7)
        free_slot(s, t)
        lg = SM2[:, 0:32].rearrange("p (t e) -> p t e", t=2)
        lmax = SM2[:, 32:34]
        lsum = SM2[:, 34:36]
        l2 = SM2[:, 36:68].rearrange("p (t e) -> p t e", t=2)
        pb = ps[:, b, 0:32].rearrange("p (t e) -> p t e", t=2)
        t = DV.do(RED(lmax, pb, ALU.max, neg=True), t)
        t = DV.do(TT(lg, pb, lmax.unsqueeze(2).broadcast_to((P, 2, 16)), ALU.add), t)
        free_bank(b, t)
        t = AT.do(AC(l2, lg, ACT.Exp), t)
        t = DV.do(RED(lsum, l2, ALU.add), t)
        t = DV.do(RCP(lsum, lsum), t)
        t = DV.do(TT(lg, l2, lsum.unsqueeze(2).broadcast_to((P, 2, 16)), ALU.mult), t)
        taff = t
        b, w = KB.get()
        for tt in range(2):
            t = PE.do(TR(ps[0:16, b, tt * P:(tt + 1) * P], lg[:, tt, :], IDN), *((w, t) if tt == 0 else ()), inc=tt == 1)
        af, wk2, msk, pos = (B(9)[0:16, i * T:(i + 1) * T] for i in range(4))
        m8 = SM2[0:16, 72:80]
        t = DV.do(CP(af, ps[0:16, b, 0:T]), t)
        free_bank(b, t)
        cur, nxt = af, wk2
        for r in range(4):
            t = DV.do(lambda e, o=m8, i=cur: e.max(o, i), t)
            t = DV.do(lambda e, o=nxt, m=m8, i=cur: e.match_replace(o, m, i, -1.0), t)
            cur, nxt = nxt, cur
        t = DV.do(TS(msk, cur, 0.0, None, ALU.is_lt), t)
        t = DV.do(lambda e: e.memset(nxt, 1.0), t)
        t = DV.do(lambda e: e.tensor_tensor_scan(pos, nxt, msk, 0.0, ALU.mult, ALU.add), t)
        t = DV.do(TT(pos, pos, msk, ALU.mult), t)
        t = DV.do(TS(pos, pos, -1.0, None, ALU.add), t)
        b, w = KB.get()
        for tt in range(2):
            t = PE.do(TR(ps[:, b, tt * 16:tt * 16 + 16], pos[:, tt * P:(tt + 1) * P], IDN[0:16, 0:16]),
                      *((w, t) if tt == 0 else ()), inc=tt == 1)
        posT = l2.rearrange("p t e -> p (t e)")
        t = DV.do(CP(posT, ps[:, b, 0:32]), t)
        free_bank(b, t)
        OH = B(5)[:, 0:1024]
        GW = B(5)[:, 1024:2048]
        a32 = lambda v: v.rearrange("p (a j) -> p a j", j=32)
        t = DV.do(TT(a32(OH), posT.unsqueeze(2).broadcast_to((P, 32, 32)),
                     C("iota32").unsqueeze(1).broadcast_to((P, 32, 32)), ALU.is_equal), t)
        toh = t
        t = DV.do(TT(a32(GW), a32(OH), lg.rearrange("p t e -> p (t e)").unsqueeze(2).broadcast_to((P, 32, 32)), ALU.mult), t)
        tgw = t
        tt_ = to_tm(F(h2), H2T, KB, th)
        XE = B(3, 2).rearrange("p (d c) -> p d c", d=8)
        txe = []
        for d in range(8):
            b, w = KB.get()
            for tt in range(2):
                t = PE.do(MM(ps[:, b, :], H2T[:, tt, d * P:(d + 1) * P], OH[:, tt * 512:(tt + 1) * 512], tt == 0, tt == 1),
                          *((w, tt_, toh) if tt == 0 else ()), inc=tt == 1)
            t = AT.do(AC(XE[:, d, :], ps[:, b, :], ACT.Copy), t) if d % 2 else DV.do(CP(XE[:, d, :], ps[:, b, :]), t)
            free_bank(b, t)
            txe.append(t)
        GT = B(7)[:, 0:1024].rearrange("p (g t) -> p g t", g=4)
        for g2 in range(2):
            b, w = KB.get()
            for i in range(2):
                for tt in range(2):
                    g = 2 * g2 + i
                    t = PE.do(TR(ps[:, b, i * T + tt * P:i * T + (tt + 1) * P], GW[:, tt * 512 + g * P:tt * 512 + (g + 1) * P], IDN),
                              *((w, tgw) if i + tt == 0 else ()), inc=i + tt == 2)
            t = DV.do(CP(GT[:, 2 * g2:2 * g2 + 2, :], ps[:, b, :].rearrange("p (g t) -> p g t", g=2)), t)
            free_bank(b, t)
            txe.append(t)
        YE = B(7)[:, 1024:2048]
        AT_ = B(6).rearrange("p (f c) -> p f c", f=16)
        EB, TB, YB = Banks([0, 1, 2, 3]), Banks([4, 5]), Banks([6, 7])
        afree = [[], []]
        tat = []
        tye = []
        for g in range(4):
            for q in range(4):
                ba, wa_ = EB.get()
                bu, wu = EB.get()
                for k in range(8):
                    def vw(s, i):
                        return s[:, i * 2048:(i + 1) * 2048].rearrange("p (e n) -> p e n", e=4)
                    s, base, tl = load(*((lambda s, i=i: vw(s, i),
                                          A[n][4 * g:4 * g + 4, k * P:(k + 1) * P, q * 512:(q + 1) * 512].rearrange("e p n -> p e n"))
                                         for i, n in enumerate(("w_exp_gate", "w_exp_up"))))
                    for i, bb in enumerate((ba, bu)):
                        for e in range(4):
                            c = (4 * g + e) * 32
                            t = PE.do(MM(ps[32 * e:32 * e + 32, bb, :], XE[:, k, c:c + 32], vw(base, i)[:, e, :], k == 0, k == 7),
                                      *((tl, txe, wa_, wu) if k + i + e == 0 else (tl,)), inc=(i == 1 and e == 3))
                    free_slot(s, t)
                S1 = tw[:, (q % 2) * 512:(q % 2 + 1) * 512]
                t1_ = AT.do(AC(S1, ps[:, ba, :], ACT.Silu), t, afree[q % 2])
                free_bank(ba, t1_)
                t = DV.do(TT(S1, S1, ps[:, bu, :], ALU.mult), t1_)
                free_bank(bu, t)
                b, w = TB.get()
                for i in range(4):
                    t = PE.do(TR(ps[:, b, i * P:(i + 1) * P], S1[:, i * P:(i + 1) * P], IDN),
                              *((w, t) if i == 0 else ()), inc=i == 3)
                afree[q % 2] = [t]
                t = DV.do(CP(AT_[:, 4 * q:4 * q + 4, :], ps[:, b, :].rearrange("p (f c) -> p f c", f=4)), t)
                free_bank(b, t)
                tat = [t]
            by = [YB.get() for _ in range(2)]
            for k in range(16):
                v4 = lambda s: s.rearrange("p (e n) -> p e n", e=4)
                s, base, tl = load((v4, A["w_exp_down"][4 * g:4 * g + 4, k * P:(k + 1) * P, :].rearrange("e p n -> p e n")))
                for c in range(2):
                    for e in range(4):
                        t = PE.do(MM(ps[32 * e:32 * e + 32, by[c][0], :], AT_[:, k, 32 * e:32 * e + 32],
                                     v4(base)[:, e, c * 512:(c + 1) * 512], k == 0, k == 15),
                                  *((tl, tat, by[0][1], by[1][1]) if k + c + e == 0 else (tl,)), inc=(c == 1 and e == 3))
                free_slot(s, t)
            ty = [AT.do(AC(YE[:, 0:512], ps[:, by[0][0], :], ACT.Copy), t, tye),
                  DV.do(CP(YE[:, 512:1024], ps[:, by[1][0], :]), t, tye)]
            free_bank(by[0][0], ty[0])
            free_bank(by[1][0], ty[1])
            for j in range(4):
                b, w = TB.get()
                for i in range(2):
                    d = 2 * j + i
                    t = PE.do(MM(ps[:, b, i * T:(i + 1) * T], YE[:, d * P:(d + 1) * P], GT[:, g, :], True, True),
                              *((w, ty) if i == 0 else ()), inc=i == 1)
                free_bank(b, *resid(j, ps[:, b, :].rearrange("p (i t) -> p i t", t=T), t))
            tye = [t]
        if STOP == 2:
            finish(x)
            return fin()
        xb = B(1)
        tx = rms(x, B(9), xb, 1e-6, lambda f: V("final_norm_g", f), KB, bar())
        x = xb
        X = F(x)

        for l in range(2):
            src, nkv = (A["w_in_a_2"], 2) if l == 0 else (A["w_in_b_2"], 4)
            hn = B(2)
            tn = rms(x, B(9), hn, 1e-5, lambda f, l=l: V("norm_g_2", 8 * l + f), KB, tx, bar())
            HN = F(hn)
            qb, kvb, zb = B(3), B(5), B(6)
            kd = F(kvb[:, 0:128 * 2 * nkv], nkv)
            vt = kvb[:, 1024:1024 + 2 * 64 * nkv].rearrange("p (t n) -> p t n", t=2)
            run(proj_fm(HN, src, 0, 1024, cp_act(F(qb), 0.125), tn, DB))
            tq = bar()
            RB = Banks([4, 5])

            def rope(dst, nt, ready):
                for j in range(nt // 2):
                    d = dst[:, 2 * j:2 * j + 2, :]
                    b, w = RB.get()
                    t = PE.do(MM(ps[:, b, :], C("rot"), d, True, True), w, ready)
                    tmp = tw[:, (j % 2) * 512:(j % 2 + 1) * 512].rearrange("p (i t) -> p i t", t=T)
                    cs = C("cos").unsqueeze(1).broadcast_to((P, 2, T))
                    sn = C("sin").unsqueeze(1).broadcast_to((P, 2, T))
                    ta = DV.do(TT(tmp, ps[:, b, :].rearrange("p (i t) -> p i t", t=T), sn, ALU.mult), t)
                    free_bank(b, ta)
                    t = DV.do(TT(d, d, cs, ALU.mult), t)
                    DV.do(TT(d, d, tmp, ALU.add), t, ta)
                    yield

            def kv():
                yield from proj_dup(HN, src, 1024, nkv, cp_act(kd), tn, DB)
                yield from proj_tm(HN, src, 1024 + 64 * nkv, 64 * nkv, cp_tm(vt), tn, DB)
            par(kv(), rope(F(qb), 8, tq))
            run(rope(kd, nkv, bar()))
            trope = bar()

            def units():
                for j in range(8):
                    kv_ = 2 * j // (16 // nkv)
                    yield {"scores": score_pair(lambda m, j=j: F(qb)[64 * m:64 * m + 64, j, :],
                                                lambda m, kv_=kv_: kd[64 * m:64 * m + 64, kv_, :]),
                           "bias": [(C("ma") if l == 0 else C("mb"), 1.0)], "sink": 16 + 2 * j if l == 0 else None,
                           "lam": None,
                           "pv": pv_pair((lambda m, kt, kv_=kv_: vt[:, kt, kv_ * 64:kv_ * 64 + 64], F(qb)[:, j, :]))}

            def silu_z(j, bk, t):
                return [AT.do(AC(F(zb)[:, 2 * j:2 * j + 2, :], bk, ACT.Silu), t)]
            par(attention(units(), trope, []), proj_fm(HN, src, 1024 + 128 * nkv, 1024, silu_z, tn, DB), 4, 1)
            tb = bar()
            tz = [DV.do(TT(F(qb)[:, 2 * j:2 * j + 2, :], F(qb)[:, 2 * j:2 * j + 2, :], F(zb)[:, 2 * j:2 * j + 2, :], ALU.mult), tb)
                  for j in range(4)]
            run(proj_fm(F(qb), A["w_out_2"][l], 0, 1024, resid, tz, KB))
            tx = bar()
            if STOP == 3 and l == 0:
                finish(x)
                return fin()
        x3 = B(0)
        rms(x, B(9), x3, 1e-5, lambda f: V("final_g_2", f), KB, tx)
        x = x3
        X = F(x)
        if STOP == 4:
            finish(x)
            return fin()

        side(xw[:, 0:sum(CT[n] for n in LATE)], A["consts2"], bar())
        TMP, Y = B(1), B(2)
        FB, QB = Banks([0, 1, 2, 3]), Banks([4, 5, 6, 7])
        ALPHA = float((2 * 2) ** 0.25)

        def ynew(scale):
            def f(j, bk, t):
                return [DV.do(STT(F(Y)[:, 2 * j:2 * j + 2, :], X[:, 2 * j:2 * j + 2, :], scale, bk, ALU.mult, ALU.add), t)]
            return f

        def norm3(l, i, eps):
            return ln(Y, TMP, x, eps, lambda f: V("ln_g_3", (3 * l + i) * 8 + f), lambda f: V("ln_b_3", (3 * l + i) * 8 + f),
                      FB, bar())

        def ffn(l, idx, ready):
            src = A["ffn_w_in_3"][l, idx].rearrange("(k p) n -> p k n", p=P)
            act = B(3, 3)[:, 0:22 * T].rearrange("p (f t) -> p f t", t=T)
            ta = []
            for c in range(11):
                def vw(s, i):
                    return s[:, i * 2048:(i + 1) * 2048].rearrange("p (k n) -> p k n", k=8)
                s, base, tl = load(*((lambda s, i=i: vw(s, i), src[:, :, i * 2816 + c * 256:i * 2816 + c * 256 + 256]) for i in range(2)))
                a = act[:, 2 * c:2 * c + 2, :]

                def ev0(j, bk, t):
                    return [AT.do(AC(a, bk, ACT.Silu), t, ready)]

                def ev1(j, bk, t):
                    ta.append(DV.do(TT(a, a, bk, ALU.mult), t, AT.now()))
                    return [ta[-1]]
                run(fm(X, vw(base, 0), 2, ev0, [tl, ready], FB))
                t = run(fm(X, vw(base, 1), 2, ev1, tl, FB))
                free_slot(s, t)
            run(acc_fm(act, 22, A["ffn_w_out_3"][l, idx], ynew(2 * ALPHA), ta, QB))

        def sgu():
            tb = bar()
            VB, UB = B(5, 2), B(3, 2)
            U, Vt = F(UB, 16), VB.rearrange("p (t n) -> p t n", t=2)
            side(B(7), A["b_in_v"].partition_broadcast(P), tb)
            side(B(8), A["sgu_ln_g_3"].partition_broadcast(P))
            ts_ = side(B(9), A["sgu_ln_b_3"].partition_broadcast(P))

            def ev_v(tt, c, bk, t):
                d = Vt[:, tt, c:c + 512]
                t = DV.do(TT(d, bk, B(7)[:, c:c + 512], ALU.add), t, ts_)
                AT.do(AC(d, d, ACT.Gelu), t)
                return [t]

            def ev_u(j, bk, t):
                for i in range(2):
                    r = AT.do(AC(U[:, 2 * j + i, :], bk[:, i, :], ACT.Gelu, bias=V("sgu_b_in_3", 2 * j + i)), t)
                return [r]
            run(proj_tm(X, A["sgu_w_in_3"], 2048, 2048, ev_v, tb, FB))
            tv = bar()
            stt = SM2[:, 0:48].rearrange("p (t c s) -> p t c s", t=2, c=4)
            mvv = SM2[:, 48:52].rearrange("p (t c) -> p t c", t=2)
            for tt in range(2):
                for c in range(4):
                    t = DV.do(lambda e, o=stt[:, tt, c, :], i=Vt[:, tt, c * 512:(c + 1) * 512]: e.bn_stats(o, i), tv)
                t = DV.do(lambda e, o=mvv[:, tt, :], i=stt[:, tt, :, :]: e.bn_aggr(o, i), t)
            rs = SM2[:, 52:54]
            t = DV.do(TS(rs, mvv[:, :, 1], 1e-5, None, ALU.add), t)
            t = AT.do(AC(rs, rs, ACT.Sqrt), t)
            t = DV.do(RCP(rs, rs), t)
            for tt in range(2):
                d = Vt[:, tt, :]
                a = DV.do(TS(d, d, mvv[:, tt, 0:1], rs[:, tt:tt + 1], ALU.subtract, ALU.mult), t)
                a = DV.do(TT(d, d, B(8), ALU.mult), a)
                tv = DV.do(TT(d, d, B(9), ALU.add), a)
            run(proj_fm(X, A["sgu_w_in_3"], 0, 2048, ev_u, tb, FB))
            s, base, tl = load((lambda q: q[:, 0:2048], A["spT"]),
                               (lambda q: q[:, 2048:4096], A["b_sp"].partition_broadcast(P)))
            sp = base[:, 0:2048].rearrange("p (g t) -> p g t", g=16)
            bs = base[:, 2048:4096].rearrange("p (g t) -> p g t", g=16)
            tm = PO.do(lambda e: e.affine_select(out=sp, in_=sp, compare_op=ALU.is_ge, fill=0.0, base=0,
                                                 pattern=[[0, 16], [1, P]], channel_multiplier=-1), tl)
            tu = bar()
            fr = [[], []]
            r = []
            for j in range(8):
                b, w = FB.get()
                for i in range(2):
                    for c in range(2):
                        g = 2 * j + i
                        t = PE.do(MM(ps[:, b, i * T + c * P:i * T + (c + 1) * P], Vt[:, c, g * P:(g + 1) * P], sp[:, g, :], True, True),
                                  *((w, tv, tm) if i + c == 0 else ()), inc=i + c == 2)
                tmp = tw[:, (j % 2) * 512:(j % 2 + 1) * 512].rearrange("p (i c t) -> p i c t", i=2, c=2)
                t = DV.do(TT(tmp, ps[:, b, :].rearrange("p (i c t) -> p i c t", i=2, c=2),
                             bs[:, 2 * j:2 * j + 2, :].unsqueeze(2).broadcast_to((P, 2, 2, P)), ALU.add), t, tl)
                free_bank(b, t)
                u = U[:, 2 * j:2 * j + 2, :]
                r.append(DV.do(TT(u, u, tmp.rearrange("p i c t -> p i (c t)"), ALU.mult), t, tu))
            free_slot(s, r[-1], PE.now())
            run(acc_fm(U, 16, A["sgu_w_out_3"], ynew(ALPHA), r, QB))

        run_l = [None]
        ffn(0, 0, bar())
        norm3(0, 0, 4e-5)
        if STOP == 5:
            finish(x)
            return fin()
        sgu()
        norm3(0, 1, 1e-5)
        if STOP == 6:
            finish(x)
            return fin()
        ffn(0, 1, bar())
        norm3(0, 2, 4e-5)
        ffn(1, 0, bar())
        norm3(1, 0, 4e-5)
        if STOP == 7:
            finish(x)
            return fin()
        def rwkv():
            t0 = bar()
            lent = [slots.pop() for _ in range(2)]
            SB = [ring[:, s * SLOT + i * BIG:s * SLOT + (i + 1) * BIG] for s in lent for i in range(2)]
            for s in lent:
                for t in slot_rel[s]:
                    t0.append(t)
            S0, S1, S2_, S3 = SB
            DT = cst[:, P:P + BIG]
            XX = B(1)
            R_, K_, SG, A_, G_, VV = B(3), B(4), B(5), B(6), B(7), B(8)
            ta = DV.do(TT(F(XX)[:, :, 1:T], X[:, :, 0:T - 1], X[:, :, 1:T], ALU.subtract), t0)
            tb = DV.do(TS(F(XX)[:, :, 0:1], X[:, :, 0:1], -1.0, None, ALU.mult), t0)
            txx = [ta, tb]
            xm_free = [list(t0), list(t0)]
            nxm = [0]

            def mixed(m):
                i = nxm[0] % 2
                nxm[0] += 1
                d = (B(2), B(9))[i]
                for f in range(8):
                    t = DV.do(STT(F(d)[:, f, :], F(XX)[:, f, :], V("rwkv_mu_3", 8 * m + f), X[:, f, :], ALU.mult, ALU.add),
                              txx, xm_free[i])
                return i, F(d), t

            def lora(xm, t, wv, tl, n, func, dst):
                b, w = FB.get()
                for k in range(8):
                    t = PE.do(MM(ps[0:n, b, 0:T], wv[:, k, :], xm[:, k, :], k == 0, k == 7),
                              *((w, t, tl) if k == 0 else ()), inc=k == 7)
                q = AT.do(AC(dst, ps[0:n, b, 0:T], func), t)
                free_bank(b, q)
                return t, q

            i, xm, t = mixed(2)
            run(proj_tm(xm, A["rwkv_w_rkv_3"][2], 0, 1024, cp_tm(xtm(VV)), t, FB))
            xm_free[i] = [PE.now()]
            i, xm, t = mixed(0)
            run(proj_fm(xm, A["rwkv_w_rkv_3"][0], 0, 1024, cp_act(F(R_)), t, FB))
            xm_free[i] = [PE.now()]
            i, xm, t = mixed(1)
            run(proj_fm(xm, A["rwkv_w_rkv_3"][1], 0, 1024, cp_act(F(K_)), t, FB))
            xm_free[i] = [PE.now()]
            s1, b1, tl1 = load((lambda q: q[:, 0:512].rearrange("p (k n) -> p k n", k=8), A["rwkv_w1_3"].rearrange("(k p) n -> p k n", p=P)),
                               (lambda q: q[:, 512:1024].rearrange("p (k n) -> p k n", k=8), A["rwkv_a1_3"].rearrange("(k p) n -> p k n", p=P)),
                               (lambda q: q[:, 1024:2304].rearrange("p (k n) -> p k n", k=8), A["rwkv_g1_3"].rearrange("(k p) n -> p k n", p=P)))
            s2, b2, tl2 = load((lambda q: q[0:64, 0:1024], A["rwkv_w2_3"]), (lambda q: q[0:64, 1024:2048], A["rwkv_a2_3"]),
                               (lambda q: q[:, 2048:3072], A["rwkv_g2_3"][0:P, :]), (lambda q: q[0:32, 3072:4096], A["rwkv_g2_3"][P:160, :]))
            k8 = lambda v: v.rearrange("p (k n) -> p k n", k=8)
            z1, z2 = tw[0:64, 0:T], tw[0:64, T:2 * T]
            z3, z4 = tw[:, 2 * T:3 * T], tw[0:32, 3 * T:4 * T]

            def second(parts, j):
                b, w = FB.get()
                for i in range(2):
                    f = 2 * j + i
                    for n, (wv, z, t) in enumerate(parts):
                        t = PE.do(MM(ps[:, b, i * T:(i + 1) * T], wv[:, f * P:(f + 1) * P], z, n == 0, n == len(parts) - 1),
                                  w, t, tl2, inc=n == len(parts) - 1)
                return b, t
            for m, wv, z, func, w2, bias, dst in ((3, b1[:, 0:512], z1, ACT.Tanh, b2[0:64, 0:1024], "rwkv_w0_3", SG),
                                                  (4, b1[:, 512:1024], z2, ACT.Copy, b2[0:64, 1024:2048], "rwkv_a0_3", A_)):
                i, xm, t = mixed(m)
                tp, t = lora(xm, t, k8(wv), tl1, 64, func, z)
                xm_free[i] = [tp]
                for j in range(4):
                    b, t2 = second([(w2, z, t)], j)
                    for i in range(2):
                        r = AT.do(AC(F(dst)[:, 2 * j + i, :], ps[:, b, i * T:(i + 1) * T], ACT.Sigmoid, bias=V(bias, 2 * j + i)), t2)
                    free_bank(b, r)
            i, xm, t = mixed(5)
            g1 = k8(b1[:, 1024:2304])
            tp, ta = lora(xm, t, g1[:, :, 0:P], tl1, P, ACT.Sigmoid, z3)
            tp, tb = lora(xm, t, g1[:, :, P:160], tl1, 32, ACT.Sigmoid, z4)
            for j in range(4):
                b, t2 = second([(b2[:, 2048:3072], z3, ta), (b2[0:32, 3072:4096], z4, tb)], j)
                r = AT.do(AC(F(G_)[:, 2 * j:2 * j + 2, :], ps[:, b, :].rearrange("p (i t) -> p i t", t=T), ACT.Copy), t2)
                free_bank(b, r)
            free_slot(s1, PE.now())
            free_slot(s2, PE.now())
            tc = bar() + [("side", side_sem, sd[0])]

            KK, BV = B(2), B(9)
            for f in range(8):
                t = DV.do(TS(F(KK)[:, f, :], F(K_)[:, f, :], V("rwkv_k_k_3", f), None, ALU.mult), tc)
            t = AT.do(AC(BV, KK, ACT.Square), t, tc)
            sel = C("sel").rearrange("p (f h) -> p f h", f=8)
            selt = C("selt").rearrange("p (f m) -> p f m", f=8)
            b, w = FB.get()
            for f in range(8):
                t = PE.do(MM(ps[0:16, b, 0:T], sel[:, f, :], F(BV)[:, f, :], f == 0, f == 7), w, t, tc, inc=f == 7)
            n16 = SM2[0:16, 0:T]
            t = AT.do(AC(n16, ps[0:16, b, 0:T], ACT.Sqrt), t)
            free_bank(b, t)
            t = DV.do(TS(n16, n16, 1e-12, None, ALU.max), t)
            t = DV.do(RCP(n16, n16), t)
            tk = []
            for j in range(4):
                b, w = FB.get()
                for i in range(2):
                    t2 = PE.do(MM(ps[:, b, i * T:(i + 1) * T], selt[0:16, 2 * j + i, :], n16, True, True), w, t, inc=i == 1)
                d = F(KK)[:, 2 * j:2 * j + 2, :]
                t2 = DV.do(TT(d, d, ps[:, b, :].rearrange("p (i t) -> p i t", t=T), ALU.mult), t2)
                free_bank(b, t2)
                tk.append(t2)
            t = DV.do(TT(BV, KK, A_, ALU.mult), tk, PE.now())
            for f in range(8):
                t = DV.do(TS(F(A_)[:, f, :], F(A_)[:, f, :], -1.0, V("rwkv_k_a_3", f), ALU.add, ALU.mult), t)
            tK = DV.do(STT(K_, A_, 1.0, K_, ALU.add, ALU.mult), t)
            for f in range(8):
                t = DV.do(STT(F(S0)[:, f, :], F(R_)[:, f, :], V("rwkv_r_k_3", f), F(K_)[:, f, :], ALU.mult, ALU.mult), tK)
            b, w = FB.get()
            for tt in range(2):
                for f in range(8):
                    t = PE.do(MM(ps[:, b, tt * 16:tt * 16 + 16], F(S0)[:, f, tt * P:(tt + 1) * P], sel[:, f, :], f == 0, f == 7),
                              w, t, inc=f == 7)
            BON = RSTD[:, 0:32]
            t = DV.do(CP(BON, ps[:, b, 0:32]), t)
            free_bank(b, t)
            t = DV.do(TS(SG, SG, -float(np.exp(-0.5)), None, ALU.mult), tK)
            for f in range(8):
                t2 = DV.do(lambda e, o=F(S1)[:, f, :], i=F(SG)[:, f, :]: e.tensor_tensor_scan(o, C("reset"), i, 0.0, ALU.mult, ALU.add), t)
            t = DV.do(TT(SG, S1, SG, ALU.subtract), t2)
            a = AT.do(AC(SG, SG, ACT.Exp), t)
            c = AT.do(AC(S2_, S1, ACT.Exp, scale=-1.0), t)
            e_ = AT.do(AC(S1, S1, ACT.Exp), t2)
            t1 = DV.do(STT(KK, KK, -1.0, SG, ALU.mult, ALU.mult), a)
            t2 = DV.do(TT(BV, BV, S2_, ALU.mult), c)
            t3 = DV.do(TT(K_, K_, S2_, ALU.mult), tK)
            t4 = DV.do(TT(R_, R_, S1, ALU.mult), e_, PE.now())
            PC = RSTD[:, 32:64].rearrange("p (f c) -> p f c", f=8)
            t5 = DV.do(CP(PC, S1.rearrange("p (f c t) -> p f c t", f=8, c=4)[:, :, :, 63]), e_)
            tall = [t1, t2, t3, t4, t5]
            AT_m, BT_m, KT_m = xtm(S0), xtm(S1), xtm(S2_)
            ttm = to_tm(F(KK), AT_m, QB, tall) + to_tm(F(BV), BT_m, QB, tall) + to_tm(F(K_), KT_m, QB, tall)

            def v4(m):
                return m.rearrange("p (t h i s) -> p t h i s", t=2, h=2, i=8)

            def pairs(left, right, mask, dst, banks):
                for tt in range(2):
                    for par_ in range(2):
                        b, w = banks.get()
                        for i in range(8):
                            for cp in range(2):
                                c0 = tt * P + cp * 64
                                rows = slice(64 * par_, 64 * par_ + 64)
                                t = PE.do(MM(ps[64 * cp:64 * cp + 64, b, i * 64:(i + 1) * 64], F(left)[rows, i, c0:c0 + 64],
                                             F(right)[rows, i, c0:c0 + 64], True, True),
                                          w, tall, inc=(i == 7 and cp == 1))
                        o = v4(dst)[:, tt, par_, :, :]
                        t = DV.do(TT(o, ps[:, b, :].rearrange("p (i s) -> p i s", i=8),
                                     C(mask).unsqueeze(1).broadcast_to((P, 8, 64)), ALU.mult), t, pairs_w)
                        free_bank(b, t)
                return t
            pairs_w = bar()
            N_, NT, A2T, RBT, RKT = S3, DT, B(1), B(5), B(6)
            pairs(KK, BV, "low", N_, FB)
            pairs(BV, KK, "upp", NT, FB)
            pairs(K_, KK, "upp", A2T, FB)
            pairs(BV, R_, "uppi", RBT, FB)
            pairs(K_, R_, "uppi", RKT, FB)
            tp = bar()
            T_, G, XS = B(2), B(4), B(9)
            bc = lambda n: C(n).unsqueeze(1).broadcast_to((P, 32, 64))
            m3 = lambda v: v.rearrange("p (a s) -> p a s", s=64)
            t = DV.do(TT(m3(T_), m3(N_), bc("ml0"), ALU.mult), tp, ttm)
            t2 = DV.do(TT(m3(G), m3(NT), bc("mu0"), ALU.mult), tp, ttm)
            tT = DV.do(TT(m3(T_), m3(T_), bc("eye64"), ALU.add), t)
            tG = DV.do(TT(m3(G), m3(G), bc("eye64"), ALU.add), t2)

            def blk(left, right, banks, fn, *toks):
                r = []
                for tt in range(2):
                    for h in range(2):
                        b, w = banks.get()
                        for i in range(8):
                            for cp in range(2):
                                rows = slice(64 * cp, 64 * cp + 64)
                                t = PE.do(MM(ps[rows, b, i * 64:(i + 1) * 64], left(tt, h, i)[rows, :], right(tt, h, i)[rows, :], True, True),
                                          w, *toks, inc=(i == 7 and cp == 1))
                        t = fn(tt, h, ps[:, b, :].rearrange("p (i s) -> p i s", i=8), t)
                        free_bank(b, t)
                        r.append(t)
                return r

            def at4(m):
                return lambda tt, h, i: v4(m)[:, tt, h, i, :]

            def vat(m):
                return lambda tt, h, i: m[:, tt, (2 * i + h) * 64:(2 * i + h) * 64 + 64]
            NM = tw
            for lev in range(1, 6):
                tn = DV.do(TT(m3(NM[:, :]), m3(NT), bc("mu%d" % lev), ALU.mult), PE.now(), t)
                before = PE.now()

                def to_x(tt, h, bk, t, before=before):
                    return AT.do(AC(v4(XS)[:, tt, h, :, :], bk, ACT.Copy), t, before)
                tX = blk(at4(NM), at4(T_), FB, to_x, tn, tT)
                if lev < 5:
                    bks = []
                    for tt in range(2):
                        for h in range(2):
                            b, w = QB.get()
                            for i in range(8):
                                for cp in range(2):
                                    rows = slice(64 * cp, 64 * cp + 64)
                                    t = PE.do(MM(ps[rows, b, i * 64:(i + 1) * 64], at4(G)(tt, h, i)[rows, :], at4(XS)(tt, h, i)[rows, :], True, True),
                                              w, tX, tG, inc=(i == 7 and cp == 1))
                            bks.append((tt, h, b, t))
                else:
                    bks = []

                def add_g(tt, h, bk, t, m=G):
                    o = v4(m)[:, tt, h, :, :]
                    return DV.do(TT(o, o, bk, ALU.add), t)
                tG = blk(at4(XS), at4(G), FB, add_g, tX, tG)
                r = []
                for tt, h, b, t in bks:
                    t = add_g(tt, h, ps[:, b, :].rearrange("p (i s) -> p i s", i=8), t, T_)
                    free_bank(b, t)
                    r.append(t)
                tT = r
            tinv = bar()
            tgn = side(tw[:, 0:1024], A["rwkv_gn_g_3"].partition_broadcast(P), tinv)
            tgn = side(tw[:, 1024:2048], A["rwkv_gn_b_3"].partition_broadcast(P))
            W1 = S3.rearrange("p (i c t) -> p i c t", i=8, c=4)
            tw1 = []
            for c in range(4):
                tt, cp = c // 2, c % 2
                b, w = QB.get()
                rows = slice(64 * cp, 64 * cp + 64)
                for i in range(8):
                    for h in range(2):
                        t = PE.do(MM(ps[64 * h:64 * h + 64, b, i * 64:(i + 1) * 64], vat(AT_m)(tt, h, i)[rows, :], at4(G)(tt, h, i)[rows, :], True, True),
                                  w, tinv, inc=(i == 7 and h == 1))
                t = AT.do(AC(W1[:, :, c, :], ps[:, b, :].rearrange("p (i t) -> p i t", i=8), ACT.Copy), t, tinv)
                free_bank(b, t)
                tw1.append(t)
            Vm = xtm(VV)
            Z, W2, YI = B(9), B(2), DT
            tz = blk(at4(A2T), vat(Vm), FB, lambda tt, h, bk, t: AT.do(AC(v4(Z)[:, tt, h, :, :], bk, ACT.Copy), t), tinv)
            tyi = blk(at4(RKT), vat(Vm), FB, lambda tt, h, bk, t: AT.do(AC(v4(YI)[:, tt, h, :, :], bk, ACT.Copy), t), tinv)
            tw2 = blk(at4(G), at4(Z), QB, lambda tt, h, bk, t: DV.do(CP(v4(W2)[:, tt, h, :, :], bk), t), tz)
            ST_ = ptw[:, 0:512].rearrange("p (i v) -> p i v", i=8)
            SX = ptw[:, 512:1024].rearrange("p (i v) -> p i v", i=8)
            Us = B(1)[:, 0:1024].rearrange("p (h i v) -> p h i v", h=2, i=8)
            ts = DV.do(lambda e: e.memset(ptw[:, 0:512], 0.0), tinv)
            tw_all = tw1 + tw2 + tyi
            b3 = lambda b, rows: ps[rows, b, :].rearrange("p (i v) -> p i v", i=8)
            for c in range(4):
                tt, cp = c // 2, c % 2
                rows = slice(64 * cp, 64 * cp + 64)
                tu, ty = [], []
                for h in range(2):
                    hr = slice(64 * h, 64 * h + 64)
                    w = bank_rel[h]
                    for i in range(8):
                        t = PE.do(MM(ps[rows, h, i * 64:(i + 1) * 64], W1[hr, i, c, :], ST_[hr, i, :], True, True),
                                  w, ts, tw_all, inc=i == 7)
                    t = DV.do(TT(Us[rows, h, :, :], b3(h, rows), v4(W2)[rows, tt, h, :, :], ALU.add), t)
                    free_bank(h, t)
                    tu.append(t)
                for h in range(2):
                    hr = slice(64 * h, 64 * h + 64)
                    w = bank_rel[2 + h]
                    for i in range(8):
                        t = PE.do(MM(ps[rows, 2 + h, i * 64:(i + 1) * 64], F(R_)[hr, i, c * 64:(c + 1) * 64], ST_[hr, i, :], True, True),
                                  w, ts, inc=i == 7)
                    ty.append(t)
                w = bank_rel[6]
                for i in range(8):
                    for h in range(2):
                        hr = slice(64 * h, 64 * h + 64)
                        o = ps[hr, 6, i * 64:(i + 1) * 64]
                        PE.do(MM(o, vat(KT_m)(tt, h, i)[rows, :], vat(Vm)(tt, h, i)[rows, :], True, False), w, inc=False)
                        t = PE.do(MM(o, vat(BT_m)(tt, h, i)[rows, :], Us[rows, h, i, :], False, True), tu, inc=(i == 7 and h == 1))
                tsx = DV.do(TT(SX, ST_, ps[:, 6, :].rearrange("p (i v) -> p i v", i=8), ALU.add), t)
                free_bank(6, tsx)
                ts = DV.do(TT(ST_, SX, PC[:, :, c:c + 1].broadcast_to((P, 8, 64)), ALU.mult), tsx, ty)
                for h in range(2):
                    w = bank_rel[4 + h]
                    for i in range(8):
                        t = PE.do(MM(ps[rows, 4 + h, i * 64:(i + 1) * 64], at4(RBT)(tt, h, i)[rows, :], Us[rows, h, i, :], True, True),
                                  w, tu, inc=i == 7)
                    y = v4(YI)[rows, tt, h, :, :]
                    a = DV.do(TT(y, y, b3(2 + h, rows), ALU.add), ty[h])
                    free_bank(2 + h, a)
                    a = DV.do(TT(y, y, b3(4 + h, rows), ALU.add), t, a)
                    free_bank(4 + h, a)
            tc = bar()
            st = SM2[:, 0:32]
            sv = SM2[:, 32:64]
            y3 = m3(YI)
            t = DV.do(RED(st, y3, ALU.add), tc)
            t = DV.do(TS(st, st, 1.0 / 64, None, ALU.mult), t)
            t = DV.do(TT(y3, y3, st.unsqueeze(2).broadcast_to((P, 32, 64)), ALU.subtract), t)
            t = AT.do(AC(Z, YI, ACT.Square), t)
            t = DV.do(RED(sv, m3(Z), ALU.add), t)
            t = DV.do(TS(sv, sv, 1.0 / 64, 64e-5, ALU.mult, ALU.add), t)
            t = AT.do(AC(sv, sv, ACT.Sqrt), t)
            t = DV.do(RCP(sv, sv), t)
            t = DV.do(TT(y3, y3, sv.unsqueeze(2).broadcast_to((P, 32, 64)), ALU.mult), t)
            YN = B(4)
            yn5 = YN.rearrange("p (t i h v) -> p t i h v", t=2, i=8, h=2)
            gg = tw[:, 0:1024].rearrange("p (i h v) -> p i h v", i=8, h=2)
            r = []
            for tt in range(2):
                for h in range(2):
                    r.append(DV.do(TT(yn5[:, tt, :, h, :], v4(YI)[:, tt, h, :, :], gg[:, :, h, :], ALU.mult), t, tgn))
            gb = tw[:, 1024:2048].unsqueeze(1).broadcast_to((P, 2, 1024))
            t = DV.do(TT(xtm(YN), xtm(YN), gb, ALU.add), r)
            t2 = DV.do(TT(m3(VV), m3(VV), BON.unsqueeze(2).broadcast_to((P, 32, 64)), ALU.mult), tc)
            t = DV.do(TT(YN, YN, VV, ALU.add), t, t2)
            r = to_fm(xtm(YN), lambda j, bk, t: [DV.do(TT(F(R_)[:, 2 * j:2 * j + 2, :], bk, F(G_)[:, 2 * j:2 * j + 2, :], ALU.mult), t)], QB, t)
            run(proj_fm(F(R_), A["rwkv_w_o_3"], 0, 1024, ynew(ALPHA), r, FB))
            for s in lent:
                slots.append(s)
                free_slot(s, *bar())

        rwkv()
        norm3(1, 1, 1e-5)
        if STOP == 8:
            finish(x)
            return fin()
        ffn(1, 1, bar())
        norm3(1, 2, 4e-5)
        finish(x)
        return fin()


_VEC_SRC = list(VEC)


def kernel(**inputs):
    import concourse.bacc as _bacc
    from concourse.bass_utils import run_bass_kernel_spmd as _run

    I = {n: np.asarray(a) for n, a in inputs.items()}
    nc = _bacc.Bacc("TRN2", target_bir_lowering=False, num_devices=1)
    arrays, A = {}, {}

    def give(name, a):
        a = np.ascontiguousarray(a)
        arrays["in_" + name] = a
        A[name] = nc.dram_tensor("in_" + name, a.shape, mybir.dt.from_np(a.dtype), kind="ExternalInput").ap()

    def fmaj(a):
        return a.reshape(T, 8, P).transpose(2, 1, 0).reshape(P, 8 * T)

    give("xT", fmaj(I["x"]))
    give("memT", fmaj(I["mem"]))
    tabs = const_tables()
    give("consts", np.concatenate([tabs[n] for n in EARLY], axis=1))
    give("consts2", np.concatenate([tabs[n] for n in LATE], axis=1))
    give("vecs", np.concatenate([I[n].reshape(-1, P).T for n in _VEC_SRC], axis=1))
    for n in ("wa_sink", "sinks_a_2", "da_lambda_q1", "da_lambda_k1", "da_lambda_q2", "da_lambda_k2"):
        give(n, I[n].reshape(-1))
    for n in ("w_in", "w_mem_kv", "w_da_o", "w_wa_o", "w_xa_o", "w_out", "w_router", "w_exp_gate", "w_exp_up",
              "w_exp_down", "w_in_a_2", "w_in_b_2", "w_out_2", "ffn_w_in_3", "ffn_w_out_3", "sgu_w_in_3",
              "sgu_w_out_3", "rwkv_w_rkv_3", "rwkv_w1_3", "rwkv_w2_3", "rwkv_a1_3", "rwkv_a2_3", "rwkv_g1_3",
              "rwkv_g2_3", "rwkv_w_o_3"):
        a = I[n]
        give(n, a[0] if a.shape[0] == 1 else a)
    give("spT", I["sgu_w_sp_3"][0].transpose(2, 0, 1).reshape(P, 16 * P))
    give("b_sp", I["sgu_b_sp_3"][0].reshape(-1))
    for n in ("sgu_ln_g_3", "sgu_ln_b_3", "rwkv_gn_g_3", "rwkv_gn_b_3"):
        give(n, I[n].reshape(-1))
    give("b_in_v", I["sgu_b_in_3"].reshape(-1)[2048:])
    o = nc.dram_tensor("out_0_dram", (P, 8 * T), F32, kind="ExternalOutput").ap()
    build(nc, A, o)
    r = _run(nc, [arrays], core_ids=[0])
    y = r.results[0]["out_0_dram"]
    return np.ascontiguousarray(y.reshape(P, 8, T).transpose(2, 1, 0)).reshape(1, T, D)
```

```python
from contextlib import ExitStack

import numpy as np
import concourse.bass as bass
from concourse import mybir

F32 = mybir.dt.float32
FR = mybir.dt.float32r
ALU = mybir.AluOpType
ACT = mybir.ActivationFunctionType
AX = mybir.AxisListType
P = 128
T = 256
D = 1024
STOP = 99

U = 1024
PARTS = (0, 12, 32, 41)
SLOT_UNIT = {0: 32, 1: 34, 2: 36, 3: 38, 4: 0, 5: 2, 6: 4, 7: 6, 8: 8, 9: 10, 10: 28, 11: 30}
NSLOT = len(SLOT_UNIT)
BIG = 2048

VEC = {}
for _n, _c in (("attn_norm_g", 8), ("mem_norm_g", 8), ("ffn_norm_g", 8), ("final_norm_g", 8), ("norm_g_2", 16),
               ("final_g_2", 8), ("ln_g_3", 48), ("ln_b_3", 48), ("rwkv_mu_3", 48), ("rwkv_w0_3", 8),
               ("rwkv_a0_3", 8), ("rwkv_k_k_3", 8), ("rwkv_k_a_3", 8), ("rwkv_r_k_3", 8), ("sgu_b_in_3", 32),
               ("da_subln_g", 1)):
    VEC[_n] = (sum(c for _, c in VEC.values()), _c)
NVEC = sum(c for _, c in VEC.values())


def const_tables():
    p = np.arange(P)
    q = (np.arange(2)[None, :, None] * P + p[:, None, None]).astype(np.int64)
    k = np.arange(T)[None, None, :]
    dist = np.abs(q - k)
    out = {}
    out["ident"] = np.eye(P)
    out["d1"] = dist.reshape(P, -1)
    out["d2"] = np.where(dist <= 128, dist, 1e32).reshape(P, -1)
    out["ma"] = np.where((q - k >= 0) & (q - k < 128), 0.0, -1e30).reshape(P, -1)
    out["mb"] = np.where(q - k >= 0, 0.0, -1e30).reshape(P, -1)
    inv = np.float32(10000.0) ** (-np.arange(0, 64, 2, dtype=np.float32) / np.float32(64))
    ang = np.arange(T, dtype=np.float32)[None, :] * inv[p % 32][:, None].astype(np.float32)
    out["cos"] = np.cos(ang)
    out["sin"] = np.sin(ang)
    r = np.zeros((P, P))
    for m in range(P):
        if m % 64 < 32:
            r[m + 32, m] = -1.0
        else:
            r[m - 32, m] = 1.0
    out["rot"] = r
    out["ones"] = np.full((P, P), 1.0 / 1024)
    out["iota32"] = np.tile(np.arange(32), (P, 1))
    tt = p % 64
    s = np.arange(64)[None, :]
    t = tt[:, None]
    out["low"] = (s < t) * 1.0
    out["upp"] = (t < s) * 1.0
    out["uppi"] = (t <= s) * 1.0
    out["eye64"] = (t == s) * 1.0
    for i, b in enumerate((1, 2, 4, 8, 16, 32)):
        same = (t // (2 * b)) == (s // (2 * b))
        out["ml%d" % i] = (same & (t % (2 * b) >= b) & (s % (2 * b) < b)) * 1.0
        out["mu%d" % i] = (same & (t % (2 * b) < b) & (s % (2 * b) >= b)) * 1.0
    out["reset"] = np.tile((np.arange(T) % 64 != 0) * 1.0, (P, 1))
    sel = np.zeros((P, 8, 16))
    selt = np.zeros((P, 8, P))
    for f in range(8):
        for h in range(2):
            sel[64 * h:64 * h + 64, f, 2 * f + h] = 1.0
            selt[2 * f + h, f, 64 * h:64 * h + 64] = 1.0
    out["sel"] = sel.reshape(P, -1)
    out["selt"] = selt.reshape(P, -1)
    return {n: a.astype(np.float32) for n, a in out.items()}


CT = {n: a.shape[1] for n, a in const_tables().items()}
LATE = [n for n in CT if n in ("low", "upp", "uppi", "eye64", "reset", "sel", "selt") or n[:2] in ("ml", "mu")]
EARLY = [n for n in CT if n not in LATE]
COFF = {}
for _l in (EARLY, LATE):
    _o = 0
    for _n in _l:
        COFF[_n] = _o
        _o += CT[_n]
NCONST = sum(CT[n] for n in EARLY)


class Queue:

    def __init__(self, sem):
        self.sem = sem
        self.n = 0
        self.ops = []
        self.seen = {}

    def wait(self, toks):
        for t in toks:
            if t is None:
                continue
            if isinstance(t, list):
                self.wait(t)
                continue
            key, sem, v = t
            if self.seen.get(key, 0) < v:
                self.seen[key] = v
                self.ops.append(lambda e, sem=sem, v=v: e.wait_ge(sem, v))

    def do(self, fn, *toks, inc=True):
        self.wait(toks)
        if not inc:
            self.ops.append(fn)
            return None
        self.n += 1
        self.ops.append(lambda e, fn=fn: fn(e).then_inc(self.sem, 1))
        return (id(self), self.sem, self.n)

    def now(self):
        return (id(self), self.sem, self.n) if self.n else None

    def play(self, e):
        for op in self.ops:
            op(e)


def MM(o, l, r, start, stop, skip=False):
    return lambda e: e.matmul(o, l, r, start=start, stop=stop, skip_group_check=skip)


def TR(o, i, ident):
    return lambda e: e.transpose(o, i, ident)


def TT(o, a, b, op):
    return lambda e: e.tensor_tensor(o, a, b, op)


def TS(o, a, s1, s2, op0, op1=None):
    if op1 is None:
        return lambda e: e.tensor_scalar(o, a, s1, None, op0)
    return lambda e: e.tensor_scalar(o, a, s1, s2, op0, op1)


def STT(o, a, s, b, op0, op1):
    return lambda e: e.scalar_tensor_tensor(out=o, in0=a, scalar=s, in1=b, op0=op0, op1=op1)


def CP(o, i):
    return lambda e: e.tensor_copy(o, i)


def RCP(o, i):
    return lambda e: e.reciprocal(o, i)


def RED(o, i, op, neg=False):
    if neg:
        return lambda e: e.tensor_reduce(o, i, AX.X, op, negate=True)
    return lambda e: e.tensor_reduce(o, i, AX.X, op)


def AC(o, i, f, **kw):
    return lambda e: e.activation(o, i, f, **kw)


def build(nc, A, out):
    with ExitStack() as ctx:
        def sb(name, cols):
            return ctx.enter_context(nc.sbuf_tensor(name, [P, cols], F32))

        def sem(name):
            return ctx.enter_context(nc.semaphore(name))

        af, ar = [], []
        for i in range(len(PARTS) - 1):
            n = (PARTS[i + 1] - PARTS[i]) * U
            with nc.sbuf_tensor("af%d" % i, [P, n], F32) as a:
                pass
            af.append(a)
            ar.append(ctx.enter_context(nc.sbuf_tensor("ar%d" % i, [P, n], FR)))
        mem = dict(af=af, ar=ar, cst=sb("cst", NCONST), vec=sb("vec", NVEC), xw=sb("xw", 3 * 1024),
                   ptw=sb("ptw", 1024), tw=sb("tw", 4 * 512), sm=sb("sm", 1024),
                   ps=ctx.enter_context(nc.psum_tensor("ps", [P, 8, 512], F32)))
        sems = {n: sem(n) for n in ("s_pe", "s_dve", "s_act", "s_pool", "s_sp", "s_small", "s_small2", "s_out", "s_side")}
        ld_sem = [sem("s_ld%d" % i) for i in range(NSLOT)]
        plan = []
        emit(nc, A, out, mem, sems, ld_sem, None, plan)
        queues, n_out = emit(nc, A, out, mem, sems, ld_sem, plan, [])
        PE, DV, AT, PO, SP = queues
        blk = ctx.enter_context(nc.Block())

        @blk.sync
        def _(e):
            SP.play(e)
            e.wait_ge(sems["s_out"], n_out)

        @blk.tensor
        def _(e):
            PE.play(e)

        @blk.scalar
        def _(e):
            AT.play(e)

        @blk.vector
        def _(e):
            DV.play(e)

        @blk.gpsimd
        def _(e):
            PO.play(e)


def emit(nc, A, out, mem, sems, ld_sem, plan, seen_loads):
    if True:
        af, ar, cst, vec, xw, ptw, tw, sm, ps = (mem[n] for n in ("af", "ar", "cst", "vec", "xw", "ptw", "tw", "sm", "ps"))
        PE, DV, AT, PO, SP = (Queue(sems[n]) for n in ("s_pe", "s_dve", "s_act", "s_pool", "s_sp"))
        ld_n = [0] * NSLOT
        out_sem, side_sem = sems["s_out"], sems["s_side"]
        ldc = [0, 0]

        def C(name):
            return (xw if name in LATE else cst)[:, COFF[name]:COFF[name] + CT[name]]

        def V(name, i=0):
            o = VEC[name][0] + i
            return vec[:, o:o + 1]

        def Vs(name, i, n):
            o = VEC[name][0] + i
            return vec[:, o:o + n]

        def units_of(tensors, u, n):
            i = 0
            while u >= PARTS[i + 1]:
                i += 1
            assert u + n <= PARTS[i + 1]
            return tensors[i][:, (u - PARTS[i]) * U:(u + n - PARTS[i]) * U]

        def unit_f(u, n):
            return units_of(af, u, n)

        def unit_r(u, n):
            return units_of(ar, u, n)

        def B(i, n=1):
            return unit_f(12 + 2 * i, 2 * n)

        def R(i, n=1):
            return unit_r(12 + 2 * i, 2 * n)

        WH = [unit_r(0, 2), unit_r(4, 2)]
        WL = [unit_r(2, 2), unit_r(6, 2)]
        XP = (unit_r(8, 2), unit_r(10, 2))

        def f_(ap):
            return ap.bitcast(F32)

        def F(ap, n=8):
            return ap.rearrange("p (f t) -> p f t", f=n)

        IDN = C("ident")

        bank_rel = [[] for _ in range(8)]

        class Banks:
            def __init__(self, ids):
                self.ids, self.i = ids, 0

            def get(self):
                b = self.ids[self.i % len(self.ids)]
                self.i += 1
                w = bank_rel[b]
                bank_rel[b] = []
                return b, w

        def free_bank(b, *toks):
            bank_rel[b] = list(toks)

        slots = [0, 1, 2, 3]
        slot_i = [0]
        slot_rel = [[] for _ in range(NSLOT)]
        rq = [0]
        issued = {}
        wcnt = [0]
        wfree = [[[], []], [[], []]]

        def fill(parts):
            s = slots[slot_i[0] % len(slots)]
            slot_i[0] += 1
            SP.wait(slot_rel[s])
            slot_rel[s] = []
            base = unit_f(SLOT_UNIT[s], 2)
            for view, src in parts:
                def go(e, dst=view(base), src=src, q=ld_sem[s]):
                    e.dma_start(dst, src).then_inc(q, 16)
                SP.ops.append(go)
                ld_n[s] += 16
            return s, base, ("ld%d" % s, ld_sem[s], ld_n[s])

        def load(*parts):
            seen_loads.append(None)
            rq[0] += 1
            return fill(parts)

        def free_slot(s, *toks):
            slot_rel[s] = list(toks)

        def issue(i, n, parts):
            s, base, tl = fill(parts)
            j = wcnt[0] % 2
            wcnt[0] += 1
            ends = []
            step = n // 2
            for h in range(2):
                c = h * step
                hi, lo, src = WH[j][:, c:c + step], WL[j][:, c:c + step], base[:, c:c + step]
                a = AT.do(AC(hi, src, ACT.Copy), tl, wfree[j][h])
                d = DV.do(TT(lo, src, f_(hi), ALU.subtract), a, tl, wfree[j][h])
                ends.append(d)
            free_slot(s, a, *ends)
            issued[i] = (j, ends)

        def split_load(n, *parts):
            i = rq[0]
            rq[0] += 1
            seen_loads.append((n, parts))
            if i not in issued:
                issue(i, n, parts)
            if plan is not None and i + 1 < len(plan) and plan[i + 1] is not None:
                issue(i + 1, *plan[i + 1])
            j, ends = issued.pop(i)
            return (WH[j][:, 0:n], WL[j][:, 0:n]), ends, j

        def fence():
            seen_loads.append(None)
            rq[0] += 1

        def bar():
            return [q.now() for q in (PE, DV, AT, PO) if q.now()]

        def small(dst, src, g=0):
            def go(e, dst=dst, src=src, q=sems[("s_small", "s_small2")[g]]):
                e.dma_start(dst, src).then_inc(q, 16)
            AT.ops.append(go)
            ldc[g] += 16

        small(B(0), A["xT"])
        small(vec[:, :], A["vecs"])
        small(cst[:, :], A["consts"])
        CONST = ("const", sems["s_small"], ldc[0])
        SINK = sm[:, 0:32]
        LAM = sm[:, 32:288].rearrange("p (a b) -> p a b", a=4)
        small(B(2), A["memT"], 1)
        small(sm[:, 0:16], A["wa_sink"].partition_broadcast(P), 1)
        small(sm[:, 16:32], A["sinks_a_2"].partition_broadcast(P), 1)
        for i, n in enumerate(("da_lambda_q1", "da_lambda_k1", "da_lambda_q2", "da_lambda_k2")):
            small(LAM[:, i, :], A[n].partition_broadcast(P), 1)
        CONST2 = ("const2", sems["s_small2"], ldc[1])
        NSINK = sm[:, 288:320]
        LV = sm[:, 320:328]
        ST = sm[:, 384:512].rearrange("p (r c) -> p r c", r=4)
        RSTD = sm[:, 512:768]
        SM2 = sm[:, 768:1024]

        DB = Banks([0, 1])
        KB = Banks([0, 1, 2, 3, 4, 5, 6, 7])

        def fmsum(src, n, bank, w, *toks):
            for f in range(n):
                t = PE.do(MM(ps[:, bank, 0:T], C("ones"), src[:, f, :], f == 0, f == n - 1),
                          *(w + list(toks) if f == 0 else ()), inc=f == n - 1)
            return t

        def rstd_of(src, tmp, eps, banks, *toks):
            t = AT.do(AC(tmp, src, ACT.Square), *toks)
            b, w = banks.get()
            t = fmsum(F(tmp), 8, b, w, t)
            t = DV.do(TS(RSTD, ps[:, b, 0:T], eps, None, ALU.add), t, AT.now())
            free_bank(b, t)
            t = AT.do(AC(RSTD, RSTD, ACT.Sqrt), t)
            return DV.do(RCP(RSTD, RSTD), t)

        def split(src, pair, k, *toks):
            hi, lo = (F(v, v.shape[1] // T)[:, k, :] for v in pair)
            a = AT.do(AC(hi, src, ACT.Copy), *toks)
            return [a, DV.do(TT(lo, src, f_(hi), ALU.subtract), a)]

        def rms(src, tmp, dst, eps, g, banks, *toks, pair=None, pair_w=()):
            t = rstd_of(src, tmp, eps, banks, *toks)
            r = []
            for f in range(8):
                d = DV.do(STT(F(dst)[:, f, :], F(src)[:, f, :], g(f), RSTD, ALU.mult, ALU.mult), t, PE.now())
                r.append([d] if pair is None else split(F(dst)[:, f, :], pair, f, d, list(pair_w)))
            return r

        def ln(y, tmp, dst, eps, g, b_, banks, *toks, pair=None):
            b, w = banks.get()
            t = fmsum(F(y), 8, b, w, *toks)
            mu = ps[:, b, 0:T].unsqueeze(1).broadcast_to((P, 8, T))
            t = DV.do(TT(F(y), F(y), mu, ALU.subtract), t)
            free_bank(b, t)
            t0 = t
            t = rstd_of(y, tmp, eps, banks, t)
            r = []
            for f in range(8):
                a = DV.do(STT(F(tmp)[:, f, :], F(y)[:, f, :], g(f), RSTD, ALU.mult, ALU.mult), t, PE.now())
                c = AT.do(AC(F(dst)[:, f, :], F(tmp)[:, f, :], ACT.Identity, bias=b_(f)), a, t0)
                if pair is None:
                    r.append([c])
                    continue
                hi, lo = (F(v)[:, f, :] for v in pair)
                h = AT.do(AC(hi, F(tmp)[:, f, :], ACT.Identity, bias=b_(f)), a)
                r.append([c, h, DV.do(TT(lo, F(dst)[:, f, :], f_(hi), ALU.subtract), c, h)])
            return r

        def MM3(o, left, right, start, stop, *toks, inc=False, skip=False):
            (lh, ll), (rh, rl) = left, right
            PE.do(MM(o, lh, rh, start, False, skip), *toks, inc=False)
            PE.do(MM(o, lh, rl, False, False, skip), inc=False)
            return PE.do(MM(o, ll, rh, False, stop, skip), inc=inc)

        def both(pair, fn):
            return fn(pair[0]), fn(pair[1])

        def rdy(ready, k):
            return ready[k] if isinstance(ready, tuple) else ready

        def fm(x, wl, evac, ready, banks):
            wp, ends, jb = wl
            wp = both(wp, k_)
            b, w = banks.get()
            for h in range(2):
                for i in range(2):
                    for k in range(4 * h, 4 * h + 4):
                        t = MM3(ps[:, b, i * T:(i + 1) * T], both(wp, lambda v: v[:, k, i * P:(i + 1) * P]),
                                both(x, lambda v: v[:, k, :]), k == 0 and i == 0, k == 7,
                                w, ends[h], rdy(ready, k), inc=(i == 1 and k % 4 == 3), skip=True)
                wfree[jb][h] = [t]
                if h == 1:
                    free_bank(b, *evac(ps[:, b, :].rearrange("p (i t) -> p i t", t=T), t))
                yield t

        def run(g):
            last = None
            for last in g:
                pass
            return last

        def k_(ap, k=8):
            return ap.rearrange("p (k n) -> p k n", k=k)

        def wk(src, c0, n=256):
            return (lambda s: k_(s[:, 0:8 * n]), src.rearrange("(k p) n -> p k n", p=P)[:, :, c0:c0 + n])

        def proj_fm(x, src, c0, ncols, evac, ready, banks):
            for c in range(0, ncols, 256):
                yield from fm(x, split_load(2048, wk(src, c0 + c)), lambda bk, t, c=c: evac(c // 256, bk, t), ready, banks)

        def proj_tm(x, src, c0, ncols, evac, ready, banks):
            for c in range(0, ncols, 256):
                n = min(256, ncols - c)
                wp, ends, j = split_load(8 * n, wk(src, c0 + c, n))
                v = both(wp, k_)
                b, w = banks.get()
                for h in range(2):
                    for tt in range(2):
                        for k in range(4 * h, 4 * h + 4):
                            t = MM3(ps[:, b, tt * n:(tt + 1) * n], both(x, lambda u: u[:, k, tt * P:(tt + 1) * P]),
                                    both(v, lambda u: u[:, k, :]), k == 0 and tt == 0, k == 7, w, rdy(ready, k), ends[h],
                                    inc=(tt == 1 and k % 4 == 3), skip=True)
                    wfree[j][h] = [t]
                    if h == 1:
                        free_bank(b, *evac(c, ps[:, b, 0:2 * n].rearrange("p (t n) -> p t n", t=2), t))
                    yield t

        def proj_dup(x, src, c0, nkv, evac, ready, banks):
            sv = src.rearrange("(k p) n -> p k n", p=P)
            for j0 in range(0, nkv, 2):
                def at(s, jj, d):
                    return s.rearrange("p (k j d e) -> p k j d e", k=8, j=2, d=2)[:, :, jj, d, :]
                parts = []
                for jj in range(2):
                    c = c0 + 64 * (j0 + jj)
                    for d in range(2):
                        parts.append((lambda s, d=d, jj=jj: at(s, jj, d), sv[:, :, c:c + 64]))
                yield from fm(x, split_load(2048, *parts), lambda bk, t, j0=j0: evac(j0 // 2, bk, t), ready, banks)

        def acc_fm(x, nk, src, evac, ready, banks4):
            bk = [banks4.get() for _ in range(4)]
            sv = src.rearrange("(k p) n -> p k n", p=P)
            for k0 in range(0, nk, 2):
                wp, ends, j = split_load(2048, (lambda q: k_(q, 2), sv[:, k0:k0 + 2, :]))
                v = both(wp, lambda u: k_(u, 2))
                for kk in range(2):
                    k = k0 + kk
                    for f in range(8):
                        b, w = bk[f // 2]
                        i = f % 2
                        t = MM3(ps[:, b, i * T:(i + 1) * T], both(v, lambda u: u[:, kk, f * P:(f + 1) * P]),
                                both(x, lambda u: u[:, k, :]), k == 0 and i == 0, k == nk - 1,
                                rdy(ready, k), w, ends[kk], inc=f == 7 or (k == nk - 1 and i == 1), skip=True)
                        if k == nk - 1 and i == 1:
                            free_bank(b, *evac(f // 2, ps[:, b, :].rearrange("p (i t) -> p i t", t=T), t))
                    wfree[j][kk] = [t]
                    yield t

        def cp_act(dst, scale=None):
            def f(j, bk, t):
                n = bk.shape[1]
                kw = {} if scale is None else {"scale": scale}
                return [AT.do(AC(dst[:, 2 * j:2 * j + n, :], bk, ACT.Copy, **kw), t)]
            return f

        def cp_tm(dst):
            def f(c, bk, t):
                return [AT.do(AC(dst[:, :, c:c + bk.shape[2]], bk, ACT.Copy), t)]
            return f

        def to_tm(src, dst, banks, *toks):
            r = []
            first = True
            for tt in range(2):
                for h in range(2):
                    b, w = banks.get()
                    for i in range(4):
                        f = 4 * h + i
                        t = PE.do(TR(ps[:, b, i * P:(i + 1) * P], src[:, f, tt * P:(tt + 1) * P], IDN),
                                  *((w, *toks) if i == 0 else ()), inc=i == 3)
                    q = DV if h else AT
                    o = dst[:, tt, h * 512:(h + 1) * 512]
                    fn = CP(o, ps[:, b, :]) if h else AC(o, ps[:, b, :], ACT.Copy)
                    t = q.do(fn, t)
                    free_bank(b, t)
                    r.append(t)
            return r

        def to_fm(src, evac, banks, *toks):
            r = []
            for j in range(4):
                b, w = banks.get()
                for i in range(2):
                    for tt in range(2):
                        f = 2 * j + i
                        t = PE.do(TR(ps[:, b, i * T + tt * P:i * T + (tt + 1) * P], src[:, tt, f * P:(f + 1) * P], IDN),
                                  *((w, *toks) if i == 0 and tt == 0 else ()), inc=(i == 1 and tt == 1))
                q = evac(j, ps[:, b, :].rearrange("p (i t) -> p i t", t=T), t)
                free_bank(b, *q)
                r += q
            return r

        S2 = Banks([2])
        PT2 = Banks([4])
        OB = Banks([6, 7])
        xfree = [[], [], []]
        ptfree = [[]]

        def attention(units, ready, done):
            state = []

            def stage_a(i, u):
                X = xw[:, (i % 3) * 1024:(i % 3 + 1) * 1024].rearrange("p (m c) -> p m c", m=2)
                st = ST[:, i % 4, :]
                b0, w0 = S2.get()
                w0 = w0 + bank_rel[b0 + 1]
                for qt in range(2):
                    for m in range(2):
                        t = u["scores"](m, qt, ps[:, b0 + m, qt * T:(qt + 1) * T], [w0, ready, u.get("ready")] if m + qt == 0 else [], qt == 1 and m == 1)
                S = ps[:, b0:b0 + 2, :]
                wx = xfree[i % 3]
                if u["bias"] is None:
                    tx = DV.do(CP(X, S), t, wx)
                elif len(u["bias"]) == 1:
                    tab, fac = u["bias"][0]
                    tx = DV.do(STT(X, tab.unsqueeze(1).broadcast_to((P, 2, 512)), fac, S, ALU.mult, ALU.add), t, wx)
                else:
                    for m, (tab, fac) in enumerate(u["bias"]):
                        tx = DV.do(STT(X[:, m, :], tab, fac, S[:, m, :], ALU.mult, ALU.add), t, wx)
                free_bank(b0, tx)
                free_bank(b0 + 1, tx)
                X4 = X.rearrange("p m (q k) -> p (m q) k", q=2)
                nm, s, r = st[:, 0:4], st[:, 4:8], st[:, 8:12]
                t = DV.do(RED(nm, X4, ALU.max, neg=True), tx)
                sink = u["sink"]
                if sink is not None:
                    ns = NSINK[:, sink:sink + 2].unsqueeze(2).broadcast_to((P, 2, 2))
                    sk = SINK[:, sink:sink + 2].unsqueeze(2).broadcast_to((P, 2, 2))
                    n3 = nm.rearrange("p (m q) -> p m q", m=2)
                    t = DV.do(TT(n3, n3, ns, ALU.min), t)
                    e3 = st[:, 12:16].rearrange("p (m q) -> p m q", m=2)
                    te = DV.do(TT(e3, n3, sk, ALU.add), t)
                return X4, st, t, te if sink is not None else None

            def stage_e(u, X4, st, t, te):
                nm, s = st[:, 0:4], st[:, 4:8]
                for g in range(4):
                    ta = AT.do(AC(X4[:, g, :], X4[:, g, :], ACT.Exp, bias=nm[:, g:g + 1], accum_out=s[:, g:g + 1]), t)
                if u["sink"] is not None:
                    ta = AT.do(AC(st[:, 12:16], st[:, 12:16], ACT.Exp), te)
                return X4, st, ta

            def stage_n(i, u, X4, st, ta):
                s, r = st[:, 4:8], st[:, 8:12]
                if u["sink"] is not None:
                    ta = DV.do(TT(s, s, st[:, 12:16], ALU.add), ta)
                t = DV.do(RCP(r, s), ta)
                if u["lam"] is not None:
                    t = DV.do(TS(r[:, 2:4], r[:, 2:4], u["lam"], None, ALU.mult), t)
                    maps = [0]
                    for qt in range(2):
                        t2 = DV.do(TS(X4[:, 2 + qt, :], X4[:, 2 + qt, :], r[:, 2 + qt:3 + qt], None, ALU.mult), t)
                        tn = DV.do(STT(X4[:, qt, :], X4[:, qt, :], r[:, qt:qt + 1], X4[:, 2 + qt, :], ALU.mult, ALU.add), t2)
                else:
                    maps = [0, 1]
                    for g in range(4):
                        tn = DV.do(TS(X4[:, g, :], X4[:, g, :], r[:, g:g + 1], None, ALU.mult), t)
                return i, X4, maps, tn

            def stage_b(u, i, X4, maps, tn):
                PT = ptw[:, :].rearrange("p (m k q) -> p m k q", m=2, k=2)
                tp = []
                for m in maps:
                    b = 4 + m
                    w = bank_rel[b]
                    for kt in range(2):
                        for qt in range(2):
                            t = PE.do(TR(ps[:, b, kt * T + qt * P:kt * T + (qt + 1) * P],
                                         X4[:, 2 * m + qt, kt * P:(kt + 1) * P], IDN),
                                      *((w, tn) if kt + qt == 0 else ()), inc=kt + qt == 2)
                    q = AT.do(AC(PT[:, m, :, :], ps[:, b, :].rearrange("p (k q) -> p k q", k=2), ACT.Copy), t, ptfree[0])
                    free_bank(b, q)
                    tp.append(q)
                xfree[i % 3] = [PE.now()]
                return u, PT, tp

            def stage_c(u, PT, tp):
                ptfree[0] = u["pv"](PT, tp)
                done.append(ptfree[0])

            prev = None
            for i, u in enumerate(units):
                if prev is not None:
                    n = stage_n(*prev)
                a = stage_a(i, u)
                yield
                if prev is not None:
                    c = stage_b(prev[1], *n)
                a = stage_e(u, *a)
                yield
                if prev is not None:
                    stage_c(*c)
                    yield
                prev = (i, u, *a)
            n = stage_n(*prev)
            yield
            c = stage_b(prev[1], *n)
            yield
            stage_c(*c)
            yield

        def par(a, b, ra=1, rb=1):
            live, at = {0: a, 1: b}, [0, 0]
            while live:
                i = min(live, key=lambda i: (at[i] + 1) / (ra, rb)[i])
                at[i] += 1
                try:
                    next(live[i])
                except StopIteration:
                    del live[i]

        def pv_pair(fns, ob=OB):
            v, dst = fns

            def go(PT, tp):
                b, w = ob.get()
                for kt in range(2):
                    for m in range(2):
                        t = PE.do(MM(ps[64 * m:64 * m + 64, b, 0:T], v(m, kt), PT[:, m, kt, :], kt == 0, kt == 1),
                                  *((w, tp) if m + kt == 0 else ()), inc=(m == 1 and kt == 1))
                d = AT.do(AC(dst, ps[:, b, 0:T], ACT.Copy), t)
                free_bank(b, d)
                return [t, d]
            return go

        def score_pair(q, k):
            def go(m, qt, o, w, inc):
                return PE.do(MM(o, q(m)[:, qt * P:(qt + 1) * P], k(m), True, True), *w, inc=inc)
            return go

        for q in (DV, PE, AT, PO):
            q.wait([CONST])
        x = B(0)
        H = both(XP, F)
        pr = lambda i, j: (R(i), R(j))
        t_h = tuple(rms(x, B(9), B(8), 1e-6, lambda f: V("attn_norm_g", f), KB, pair=XP))
        W1 = A["w_in"]
        daq, dak, dav, waq, wakv, xaq, mk = B(3), B(4), B(5), B(6), B(7), B(8), B(9)
        wak = F(wakv[:, 0:1024], 4)
        wav = wakv[:, 1024:1536].rearrange("p (t n) -> p t n", t=2)
        xtm = lambda b: b.rearrange("p (t n) -> p t n", t=2)
        WK = A["w_mem_kv"]
        mp = pr(4, 5)

        mp = pr(6, 7)

        def first():
            yield from proj_fm(H, W1, 0, 1024, cp_act(F(daq), 0.125), t_h, DB)

        tm2 = []

        def memory_norm():
            for q in (DV, AT):
                q.wait([CONST2])
            DV.do(TS(NSINK, SINK, -1.0, None, ALU.mult))
            lt = tw[:, 0:128].rearrange("p (a b) -> p a b", a=2)
            t = DV.do(TT(lt[:, 0, :], LAM[:, 0, :], LAM[:, 1, :], ALU.mult))
            t = DV.do(TT(lt[:, 1, :], LAM[:, 2, :], LAM[:, 3, :], ALU.mult))
            t = DV.do(RED(LV[:, 0:2], lt, ALU.add), t)
            t = AT.do(AC(LV[:, 2:4], LV[:, 0:2], ACT.Exp), t)
            t = DV.do(TT(LV[:, 4:5], LV[:, 3:4], LV[:, 2:3], ALU.subtract), t)
            lam_init = 0.8 - 0.6 * float(np.exp(-0.3 * 0))
            t = DV.do(TS(LV[:, 5:6], LV[:, 4:5], -lam_init, None, ALU.add), t)
            t = DV.do(TS(LV[:, 6:7], V("da_subln_g"), 1.0 - lam_init, None, ALU.mult))
            yield
            tm2.extend(rms(B(2), B(9), B(8), 1e-6, lambda f: V("mem_norm_g", f), Banks([2, 3]), bar(), pair=mp))
            yield
        NLAM, SUBG = LV[:, 5:6], LV[:, 6:7]
        par(first(), memory_norm(), 2, 1)
        tmv = tm2
        run(proj_fm(H, W1, 1024, 1024, cp_act(F(dak)), t_h, KB))
        run(proj_tm(H, W1, 2048, 1024, cp_tm(xtm(dav)), t_h, KB))
        mvb = xaq
        odt = B(2)
        tda = bar()
        oda = []
        ODT = xtm(odt)

        def da_units():
            for h in range(8):
                def pv(PT, tp, h=h):
                    b, w = OB.get()
                    for qt in range(2):
                        for kt in range(2):
                            t = PE.do(MM(ps[:, b, qt * P:(qt + 1) * P], PT[:, 0, kt, qt * P:(qt + 1) * P],
                                         xtm(dav)[:, kt, h * P:(h + 1) * P], kt == 0, kt == 1),
                                      *((w, tp) if qt + kt == 0 else ()), inc=qt + kt == 2)
                    d = AT.do(AC(ODT[:, :, h * P:(h + 1) * P], ps[:, b, 0:T].rearrange("p (q e) -> p q e", q=2),
                                 ACT.Copy), t, tmv)
                    free_bank(b, d)
                    return [t, d]
                slope = 2.0 ** (-(h + 1))
                yield {"scores": score_pair(lambda m, h=h: F(daq)[64 * m:64 * m + 64, h, :],
                                            lambda m, h=h: F(dak)[64 * m:64 * m + 64, h, :]),
                       "bias": [(C("d1"), -slope)], "sink": None, "lam": NLAM, "pv": pv}

        def dense_a():
            yield from proj_fm(both(mp, F), WK, 0, 1024, cp_act(F(mk)), tm2, DB)
            yield from proj_tm(both(mp, F), WK, 1024, 1024, cp_tm(xtm(xaq)), tm2, DB)
            AT.wait([PE.now()])
            yield from proj_fm(H, W1, 3072, 1024, cp_act(F(waq), 0.125), t_h, DB)
            yield from proj_dup(H, W1, 4096, 4, cp_act(wak), t_h, DB)
            yield from proj_tm(H, W1, 4352, 256, cp_tm(wav), t_h, DB)
            yield from proj_fm(H, W1, 4608, 1024, cp_act(F(xq2), 0.0625), t_h, DB)

        xq2 = B(1)
        par(attention(da_units(), tda, oda), dense_a(), 26, 39)
        twa = bar()

        def wa_units():
            for j in range(8):
                kv = j // 2
                slopes = [float(np.exp2(np.float32(-8.0) * np.float32(h + 1) / np.float32(16))) for h in (2 * j, 2 * j + 1)]
                yield {"scores": score_pair(lambda m, j=j: F(waq)[64 * m:64 * m + 64, j, :],
                                            lambda m, kv=kv: wak[64 * m:64 * m + 64, kv, :]),
                       "bias": [(C("d2"), -slopes[0]), (C("d2"), -slopes[1])], "sink": 2 * j, "lam": None,
                       "pv": pv_pair((lambda m, kt, kv=kv: wav[:, kt, kv * 64:kv * 64 + 64], F(waq)[:, j, :]))}

        def da_norm():
            sq = B(4)
            o16 = odt.rearrange("p (a e) -> p a e", e=P)
            t = AT.do(AC(sq, odt, ACT.Square), twa)
            r16 = SM2[:, 0:16]
            t = DV.do(RED(r16, sq.rearrange("p (a e) -> p a e", e=P), ALU.add), t)
            t = DV.do(TS(r16, r16, 1.0 / 128, 1e-6, ALU.mult, ALU.add), t)
            t = AT.do(AC(r16, r16, ACT.Sqrt), t)
            t = DV.do(RCP(r16, r16), t)
            t = DV.do(TT(o16, o16, r16.unsqueeze(2).broadcast_to((P, 16, P)), ALU.mult), t)
            return t

        t = da_norm()
        op = pr(3, 4)

        def oda_split(j, bk, t):
            hi, lo = (F(v)[:, 2 * j:2 * j + 2, :] for v in op)
            a = AT.do(AC(hi, bk, ACT.Copy, scale=SUBG), t)
            return [a, DV.do(STT(lo, bk, SUBG, f_(hi), ALU.mult, ALU.subtract), a)]
        to_fm(ODT, oda_split, DB, t)
        tod = bar()
        merged = B(5)

        def gate(n, dst):
            def ev(j, bk, t):
                return [AT.do(AC(F(dst)[:, 2 * j:2 * j + 2, :], bk, ACT.Sigmoid), t)]
            return proj_fm(H, W1, 5632 + n * 1024, 1024, ev, t_h, DB)

        def branch(o, wname, ready, G, add):
            def ev(j, bk, t):
                g, dst = (F(v)[:, 2 * j:2 * j + 2, :] for v in (G, merged))
                if not add:
                    return [DV.do(TT(dst, bk, g, ALU.mult), t, AT.now())]
                q = DV.do(TT(g, bk, g, ALU.mult), t, AT.now())
                PO.do(TT(dst, dst, g, ALU.add), q)
                return [q]
            return proj_fm(o, A[wname], 0, 1024, ev, ready, DB)

        def dense_b():
            yield from gate(0, B(2))
            yield from branch(both(op, F), "w_da_o", tod, B(2), False)
            AT.wait([DV.now()])
            yield from gate(1, B(2))

        owa = []
        par(attention(wa_units(), twa, owa), dense_b(), 26, 25)
        txa = bar()
        wp2 = pr(3, 4)
        tsp = tuple(split(F(waq)[:, f, :], wp2, f, txa) for f in range(8))

        def xa_units():
            for h in range(0, 4, 2):
                def scores(m, qt, o, w, inc, h=h):
                    for kk in range(2):
                        f = 2 * (h + m) + kk
                        t = PE.do(MM(o, F(xq2)[:, f, qt * P:(qt + 1) * P], F(mk)[:, f, :], kk == 0, kk == 1),
                                  *(w if kk == 0 else ()), inc=inc and kk == 1)
                    return t

                def pv(PT, tp, h=h):
                    r = []
                    for m in range(2):
                        b, w = OB.get()
                        for e in range(2):
                            for kt in range(2):
                                c = (h + m) * 256 + e * P
                                t = PE.do(MM(ps[:, b, e * T:(e + 1) * T], xtm(mvb)[:, kt, c:c + P], PT[:, m, kt, :],
                                             kt == 0, kt == 1), *((w, tp) if e + kt == 0 else ()), inc=e + kt == 2)
                        f = 2 * (h + m)
                        d = AT.do(AC(F(xq2)[:, f:f + 2, :], ps[:, b, :].rearrange("p (e t) -> p e t", t=T), ACT.Copy), t)
                        free_bank(b, d)
                        r += [t, d]
                    return r
                yield {"scores": scores, "bias": None, "sink": None, "lam": None, "pv": pv}

        oxa = []
        
        def dense_c():
            yield from gate(2, B(7))
            yield from branch(both(wp2, F), "w_wa_o", tsp, B(2), True)
        par(attention(xa_units(), txa, oxa), dense_c(), 8, 17)
        txo = bar()
        xp2 = pr(6, 2)
        tsp = tuple(split(F(xq2)[:, f, :], xp2, f, txo) for f in range(8))
        run(branch(both(xp2, F), "w_xa_o", tsp, B(7), True))
        tmg = bar()
        mgp = pr(8, 9)
        tmg = tuple(split(F(merged)[:, f, :], mgp, f, tmg) for f in range(8))
        X = F(x)

        def resid(j, bk, t, scale=None):
            d = X[:, 2 * j:2 * j + 2, :]
            if scale is None:
                return [DV.do(TT(d, bk, d, ALU.add), t)]
            return [DV.do(STT(d, d, scale, bk, ALU.mult, ALU.add), t)]
        run(proj_fm(both(mgp, F), A["w_out"], 0, 1024, resid, tmg, KB))
        t1 = bar()

        def finish(src):
            SP.wait(bar())

            def go(e, src=src):
                e.dma_start(out, src).then_inc(out_sem, 16)
            SP.ops.append(go)

        def fin():
            return (PE, DV, AT, PO, SP), 16

        if STOP == 1:
            finish(x)
            return fin()
        sd = [0]

        def side(dst, src, *toks):
            PO.wait(toks)

            def go(e, dst=dst, src=src):
                e.dma_start(dst, src).then_inc(side_sem, 16)
            PO.ops.append(go)
            sd[0] += 16
            return ("side", side_sem, sd[0])

        fence()
        tx4 = bar()
        for i in range(4, 11):
            slots.append(i)
            free_slot(i, *tx4)
        h2 = B(1)
        th = rms(x, B(9), h2, 1e-6, lambda f: V("ffn_norm_g", f), KB, t1)
        H2T = xtm(B(2))
        s, base, tl = load((lambda q: q[:, 0:128].rearrange("p (k n) -> p k n", k=8),
                            A["w_router"].rearrange("(k p) n -> p k n", p=P)))
        wr = base[:, 0:128].rearrange("p (k n) -> p k n", k=8)
        b, w = KB.get()
        for tt in range(2):
            for k in range(8):
                t = PE.do(MM(ps[:, b, tt * 16:tt * 16 + 16], F(h2)[:, k, tt * P:(tt + 1) * P], wr[:, k, :], k == 0, k == 7),
                          *((w, th, tl) if k + tt == 0 else ()), inc=k == 7)
        free_slot(s, t)
        trt = t
        tt_ = to_tm(F(h2), H2T, Banks([(b + i) % 8 for i in range(1, 5)]), th)
        t = trt
        lg = SM2[:, 0:32].rearrange("p (t e) -> p t e", t=2)
        lmax = SM2[:, 32:34]
        lsum = SM2[:, 34:36]
        l2 = SM2[:, 36:68].rearrange("p (t e) -> p t e", t=2)
        pb = ps[:, b, 0:32].rearrange("p (t e) -> p t e", t=2)
        t = DV.do(RED(lmax, pb, ALU.max, neg=True), t)
        t = DV.do(TT(lg, pb, lmax.unsqueeze(2).broadcast_to((P, 2, 16)), ALU.add), t)
        free_bank(b, t)
        t = AT.do(AC(l2, lg, ACT.Exp), t)
        t = DV.do(RED(lsum, l2, ALU.add), t)
        t = DV.do(RCP(lsum, lsum), t)
        t = DV.do(TT(lg, l2, lsum.unsqueeze(2).broadcast_to((P, 2, 16)), ALU.mult), t)
        taff = t
        b, w = KB.get()
        for tt in range(2):
            t = PE.do(TR(ps[0:16, b, tt * P:(tt + 1) * P], lg[:, tt, :], IDN), *((w, t) if tt == 0 else ()), inc=tt == 1)
        aff_, wk2, msk, pos = (B(9)[0:16, i * T:(i + 1) * T] for i in range(4))
        m8 = SM2[0:16, 72:80]
        t = DV.do(CP(aff_, ps[0:16, b, 0:T]), t)
        free_bank(b, t)
        cur, nxt = aff_, wk2
        for r in range(4):
            t = DV.do(lambda e, o=m8, i=cur: e.max(o, i), t)
            t = DV.do(lambda e, o=nxt, m=m8, i=cur: e.match_replace(o, m, i, -1.0), t)
            cur, nxt = nxt, cur
        t = DV.do(TS(msk, cur, 0.0, None, ALU.is_lt), t)
        t = DV.do(lambda e: e.memset(nxt, 1.0), t)
        t = DV.do(lambda e: e.tensor_tensor_scan(pos, nxt, msk, 0.0, ALU.mult, ALU.add), t)
        t = DV.do(TT(pos, pos, msk, ALU.mult), t)
        t = DV.do(TS(pos, pos, -1.0, None, ALU.add), t)
        b, w = KB.get()
        for tt in range(2):
            t = PE.do(TR(ps[:, b, tt * 16:tt * 16 + 16], pos[:, tt * P:(tt + 1) * P], IDN[0:16, 0:16]),
                      *((w, t) if tt == 0 else ()), inc=tt == 1)
        posT = l2.rearrange("p t e -> p (t e)")
        t = DV.do(CP(posT, ps[:, b, 0:32]), t)
        free_bank(b, t)
        OH = B(5)[:, 0:1024]
        GW = B(5)[:, 1024:2048]
        a32 = lambda v: v.rearrange("p (a j) -> p a j", j=32)
        t = DV.do(TT(a32(OH), posT.unsqueeze(2).broadcast_to((P, 32, 32)),
                     C("iota32").unsqueeze(1).broadcast_to((P, 32, 32)), ALU.is_equal), t)
        toh = t
        t = DV.do(TT(a32(GW), a32(OH), lg.rearrange("p t e -> p (t e)").unsqueeze(2).broadcast_to((P, 32, 32)), ALU.mult), t)
        tgw = t
        XE = B(3, 2).rearrange("p (d c) -> p d c", d=8)
        txe = []
        for d in range(8):
            b, w = KB.get()
            for tt in range(2):
                t = PE.do(MM(ps[:, b, :], H2T[:, tt, d * P:(d + 1) * P], OH[:, tt * 512:(tt + 1) * 512], tt == 0, tt == 1),
                          *((w, tt_, toh) if tt == 0 else ()), inc=tt == 1)
            t = AT.do(AC(XE[:, d, :], ps[:, b, :], ACT.Copy), t) if d % 2 else DV.do(CP(XE[:, d, :], ps[:, b, :]), t)
            free_bank(b, t)
            txe.append(t)
        GT = B(7)[:, 0:1024].rearrange("p (g t) -> p g t", g=4)
        for g2 in range(2):
            b, w = KB.get()
            for i in range(2):
                for tt in range(2):
                    g = 2 * g2 + i
                    t = PE.do(TR(ps[:, b, i * T + tt * P:i * T + (tt + 1) * P], GW[:, tt * 512 + g * P:tt * 512 + (g + 1) * P], IDN),
                              *((w, tgw) if i + tt == 0 else ()), inc=i + tt == 2)
            t = DV.do(CP(GT[:, 2 * g2:2 * g2 + 2, :], ps[:, b, :].rearrange("p (g t) -> p g t", g=2)), t)
            free_bank(b, t)
            txe.append(t)
        YE = B(7)[:, 1024:2048]
        AT_ = B(6).rearrange("p (f c) -> p f c", f=16)
        EB, TB, YB = Banks([0, 1, 2, 3]), Banks([4, 5]), Banks([6, 7])
        afree = [[], []]
        tat = []
        tye = []
        for g in range(4):
            for q in range(4):
                ba, wa_ = EB.get()
                bu, wu = EB.get()
                for k in range(8):
                    for n, bb in (("w_exp_gate", ba), ("w_exp_up", bu)):
                        s, base, tl = load((lambda s: k_(s, 4),
                                            A[n][4 * g:4 * g + 4, k * P:(k + 1) * P, q * 512:(q + 1) * 512].rearrange("e p n -> p e n")))
                        for e in range(4):
                            c = (4 * g + e) * 32
                            t = PE.do(MM(ps[32 * e:32 * e + 32, bb, :], XE[:, k, c:c + 32], k_(base, 4)[:, e, :], k == 0, k == 7),
                                      tl, txe, wa_, wu, inc=e == 3)
                        free_slot(s, t)
                S1 = tw[:, (q % 2) * 512:(q % 2 + 1) * 512]
                t1_ = AT.do(AC(S1, ps[:, ba, :], ACT.Silu), t, afree[q % 2])
                free_bank(ba, t1_)
                t = DV.do(TT(S1, S1, ps[:, bu, :], ALU.mult), t1_)
                free_bank(bu, t)
                b, w = TB.get()
                for i in range(4):
                    t = PE.do(TR(ps[:, b, i * P:(i + 1) * P], S1[:, i * P:(i + 1) * P], IDN),
                              *((w, t) if i == 0 else ()), inc=i == 3)
                afree[q % 2] = [t]
                t = DV.do(CP(AT_[:, 4 * q:4 * q + 4, :], ps[:, b, :].rearrange("p (f c) -> p f c", f=4)), t)
                free_bank(b, t)
                tat = [t]
            by = [YB.get() for _ in range(2)]
            for k in range(16):
                for c in range(2):
                    s, base, tl = load((lambda s: k_(s, 4),
                                        A["w_exp_down"][4 * g:4 * g + 4, k * P:(k + 1) * P, c * 512:(c + 1) * 512].rearrange("e p n -> p e n")))
                    for e in range(4):
                        t = PE.do(MM(ps[32 * e:32 * e + 32, by[c][0], :], AT_[:, k, 32 * e:32 * e + 32],
                                     k_(base, 4)[:, e, :], k == 0, k == 15),
                                  tl, tat, by[0][1], by[1][1], inc=e == 3)
                    free_slot(s, t)
            ty = [AT.do(AC(YE[:, 0:512], ps[:, by[0][0], :], ACT.Copy), t, tye),
                  DV.do(CP(YE[:, 512:1024], ps[:, by[1][0], :]), t, tye)]
            free_bank(by[0][0], ty[0])
            free_bank(by[1][0], ty[1])
            for j in range(4):
                b, w = TB.get()
                for i in range(2):
                    d = 2 * j + i
                    t = PE.do(MM(ps[:, b, i * T:(i + 1) * T], YE[:, d * P:(d + 1) * P], GT[:, g, :], True, True),
                              *((w, ty) if i == 0 else ()), inc=i == 1)
                free_bank(b, *resid(j, ps[:, b, :].rearrange("p (i t) -> p i t", t=T), t))
            tye = [t]
        del slots[4:]
        tx4 = bar()
        wfree[0], wfree[1] = [tx4, tx4], [tx4, tx4]
        fence()
        if STOP == 2:
            finish(x)
            return fin()
        xb = B(1)
        tx = rms(x, B(9), xb, 1e-6, lambda f: V("final_norm_g", f), KB, bar())
        x = xb
        X = F(x)

        for l in range(2):
            src, nkv = (A["w_in_a_2"], 2) if l == 0 else (A["w_in_b_2"], 4)
            tn = tuple(rms(x, B(9), B(2), 1e-5, lambda f, l=l: V("norm_g_2", 8 * l + f), KB, tx, bar(), pair=XP, pair_w=bar()))
            HN = H
            qb, kvb, zb = B(3), B(5), B(6)
            kd = F(kvb[:, 0:128 * 2 * nkv], nkv)
            vt = kvb[:, 1024:1024 + 2 * 64 * nkv].rearrange("p (t n) -> p t n", t=2)
            RB = Banks([4, 5])

            def rope(dst, j, ready, *toks):
                d = dst[:, 2 * j:2 * j + 2, :]
                b, w = RB.get()
                t = PE.do(MM(ps[:, b, :], C("rot"), d, True, True), w, *toks)
                tmp = tw[:, (j % 2) * 512:(j % 2 + 1) * 512].rearrange("p (i t) -> p i t", t=T)
                cs = C("cos").unsqueeze(1).broadcast_to((P, 2, T))
                sn = C("sin").unsqueeze(1).broadcast_to((P, 2, T))
                ta = DV.do(TT(tmp, ps[:, b, :].rearrange("p (i t) -> p i t", t=T), sn, ALU.mult), t)
                free_bank(b, ta)
                t = DV.do(TT(d, d, cs, ALU.mult), t)
                ready.append(DV.do(TT(d, d, tmp, ALU.add), t, ta))

            kr, qr, qtok = [], [], []

            def dense_q(j0, j1):
                for j in range(j0, j1):
                    def ev(_, bk, t, j=j):
                        qtok.append(cp_act(F(qb), 0.125)(j, bk, t))
                        return qtok[j]
                    yield from proj_fm(HN, src, 256 * j, 256, ev, tn, DB)
                    if j >= 1:
                        rope(F(qb), j - 1, qr, qtok[j - 1])
                        yield
            run(proj_dup(HN, src, 1024, nkv, cp_act(kd), tn, DB))
            run(proj_tm(HN, src, 1024 + 64 * nkv, 64 * nkv, cp_tm(vt), tn, DB))
            for j in range(nkv // 2):
                rope(kd, j, kr, AT.now())
            run(dense_q(0, 2))
            trope = [kr, bar()]

            def units():
                for j in range(8):
                    kv_ = 2 * j // (16 // nkv)
                    yield {"ready": qr[j // 2], "scores": score_pair(lambda m, j=j: F(qb)[64 * m:64 * m + 64, j, :],
                                                lambda m, kv_=kv_: kd[64 * m:64 * m + 64, kv_, :]),
                           "bias": [(C("ma") if l == 0 else C("mb"), 1.0)], "sink": 16 + 2 * j if l == 0 else None,
                           "lam": None,
                           "pv": pv_pair((lambda m, kt, kv_=kv_: vt[:, kt, kv_ * 64:kv_ * 64 + 64], F(qb)[:, j, :]))}

            def silu_z(j, bk, t):
                return [AT.do(AC(F(zb)[:, 2 * j:2 * j + 2, :], bk, ACT.Silu), t)]
            
            def dense_z():
                yield from dense_q(2, 4)
                rope(F(qb), 3, qr, qtok[3])
                yield
                yield from proj_fm(HN, src, 1024 + 128 * nkv, 1024, silu_z, tn, DB)
            par(attention(units(), trope, []), dense_z(), 26, 16)
            tb = bar()
            tz = []
            zp = pr(7, 8)
            for f in range(8):
                q_ = F(qb)[:, f, :]
                t = DV.do(TT(q_, q_, F(zb)[:, f, :], ALU.mult), tb)
                tz.append(split(q_, zp, f, t))
            run(proj_fm(both(zp, F), A["w_out_2"][l], 0, 1024, resid, tuple(tz), KB))
            tx = bar()
            if STOP == 3 and l == 0:
                finish(x)
                return fin()
        x3 = B(0)
        tx = rms(x, B(9), x3, 1e-5, lambda f: V("final_g_2", f), KB, tx, pair=XP, pair_w=bar())
        x = x3
        X = F(x)
        if STOP == 4:
            finish(x)
            return fin()

        side(xw[:, 0:sum(CT[n] for n in LATE)], A["consts2"], bar())
        TMP, Y = B(1), B(2)
        FB, QB = Banks([0, 1, 2, 3]), Banks([4, 5, 6, 7])
        ALPHA = float((2 * 2) ** 0.25)

        def ynew(scale):
            def f(j, bk, t):
                return [DV.do(STT(F(Y)[:, 2 * j:2 * j + 2, :], X[:, 2 * j:2 * j + 2, :], scale, bk, ALU.mult, ALU.add), t)]
            return f

        def norm3(l, i, eps):
            return ln(Y, TMP, x, eps, lambda f: V("ln_g_3", (3 * l + i) * 8 + f), lambda f: V("ln_b_3", (3 * l + i) * 8 + f),
                      FB, bar(), pair=XP)

        def ffn(l, idx, ready):
            ready = tuple(ready)
            src = A["ffn_w_in_3"][l, idx]
            ap_ = (unit_r(18, 6)[:, 0:22 * T], unit_r(24, 6)[:, 0:22 * T])
            act = both(ap_, lambda v: F(v, 22))
            tfree = [[] for _ in range(4)]
            tst = bar()
            ta = []
            for c in range(11):
                G = tw[:, (c % 4) * 512:(c % 4 + 1) * 512].rearrange("p (i t) -> p i t", t=T)
                tk = []

                def ev0(bk, t):
                    tk.append(AT.do(AC(G, bk, ACT.Silu), t, tfree[c % 4]))
                    return tk

                def ev1(bk, t):
                    d = DV.do(TT(G, G, bk, ALU.mult), t, tk)
                    hi, lo = (v[:, 2 * c:2 * c + 2, :] for v in act)
                    a = AT.do(AC(hi, G, ACT.Copy), d, tst)
                    tfree[c % 4] = [a, DV.do(TT(lo, G, f_(hi), ALU.subtract), a)]
                    ta.extend([tfree[c % 4]] * 2)
                    return [d]
                for i, ev in enumerate((ev0, ev1)):
                    run(fm(H, split_load(2048, wk(src, i * 2816 + c * 256)), ev, ready, FB))
            run(acc_fm(act, 22, A["ffn_w_out_3"][l, idx], ynew(2 * ALPHA), tuple(ta), QB))

        def sgu(ready):
            ready = tuple(ready)
            tb = bar()
            VB, UB = B(5, 2), B(3, 2)
            U_, Vt = F(UB, 16), VB.rearrange("p (t n) -> p t n", t=2)
            side(B(7), A["b_in_v"].partition_broadcast(P), tb)
            side(B(8), A["sgu_ln_g_3"].partition_broadcast(P))
            ts_ = side(B(9), A["sgu_ln_b_3"].partition_broadcast(P))

            def ev_v(c, bk, t):
                d = Vt[:, :, c:c + 256]
                t = DV.do(TT(d, bk, B(7)[:, c:c + 256].unsqueeze(1).broadcast_to((P, 2, 256)), ALU.add), t, ts_)
                AT.do(AC(d, d, ACT.Gelu), t)
                return [t]

            def ev_u(j, bk, t):
                for i in range(2):
                    r = AT.do(AC(U_[:, 2 * j + i, :], bk[:, i, :], ACT.Gelu, bias=V("sgu_b_in_3", 2 * j + i)), t)
                return [r]
            run(proj_tm(H, A["sgu_w_in_3"], 2048, 2048, ev_v, ready, FB))
            tv = bar()
            stt = SM2[:, 0:48].rearrange("p (t c s) -> p t c s", t=2, c=4)
            mvv = SM2[:, 48:52].rearrange("p (t c) -> p t c", t=2)
            for tt in range(2):
                for c in range(4):
                    t = DV.do(lambda e, o=stt[:, tt, c, :], i=Vt[:, tt, c * 512:(c + 1) * 512]: e.bn_stats(o, i), tv)
                t = DV.do(lambda e, o=mvv[:, tt, :], i=stt[:, tt, :, :]: e.bn_aggr(o, i), t)
            rs = SM2[:, 52:54]
            t = DV.do(TS(rs, mvv[:, :, 1], 1e-5, None, ALU.add), t)
            t = AT.do(AC(rs, rs, ACT.Sqrt), t)
            t = DV.do(RCP(rs, rs), t)
            for tt in range(2):
                d = Vt[:, tt, :]
                a = DV.do(TS(d, d, mvv[:, tt, 0:1], rs[:, tt:tt + 1], ALU.subtract, ALU.mult), t)
                a = DV.do(TT(d, d, B(8), ALU.mult), a)
                tv = DV.do(TT(d, d, B(9), ALU.add), a)
            run(proj_fm(H, A["sgu_w_in_3"], 0, 2048, ev_u, ready, FB))
            s, base, tl = load((lambda q: q, A["spT"]))
            sb_, base2, tl2 = load((lambda q: q, A["b_sp"].partition_broadcast(P)))
            sp = base.rearrange("p (g t) -> p g t", g=16)
            bs = base2.rearrange("p (g t) -> p g t", g=16)
            uh, ul = F(R(7, 2), 16), F(R(3, 2), 16)
            tm = PO.do(lambda e: e.affine_select(out=sp, in_=sp, compare_op=ALU.is_ge, fill=0.0, base=0,
                                                 pattern=[[0, 16], [1, P]], channel_multiplier=-1), tl)
            tu = bar()
            fr = [[], []]
            r = []
            for j in range(8):
                b, w = FB.get()
                for i in range(2):
                    for c in range(2):
                        g = 2 * j + i
                        t = PE.do(MM(ps[:, b, i * T + c * P:i * T + (c + 1) * P], Vt[:, c, g * P:(g + 1) * P], sp[:, g, :], True, True),
                                  *((w, tv, tm) if i + c == 0 else ()), inc=i + c == 2)
                tmp = tw[:, (j % 2) * 512:(j % 2 + 1) * 512].rearrange("p (i c t) -> p i c t", i=2, c=2)
                t = DV.do(TT(tmp, ps[:, b, :].rearrange("p (i c t) -> p i c t", i=2, c=2),
                             bs[:, 2 * j:2 * j + 2, :].unsqueeze(2).broadcast_to((P, 2, 2, P)), ALU.add), t, tl2, fr[j % 2])
                free_bank(b, t)
                u = U_[:, 2 * j:2 * j + 2, :]
                g_ = tmp.rearrange("p i c t -> p i (c t)")
                t = DV.do(TT(g_, u, g_, ALU.mult), t, tu)
                a = AT.do(AC(uh[:, 2 * j:2 * j + 2, :], g_, ACT.Copy), t)
                fr[j % 2] = [a, DV.do(TT(ul[:, 2 * j:2 * j + 2, :], g_, f_(uh[:, 2 * j:2 * j + 2, :]), ALU.subtract), a)]
                r += [fr[j % 2]] * 2
            free_slot(s, *bar())
            free_slot(sb_, *bar())
            run(acc_fm((uh, ul), 16, A["sgu_w_out_3"], ynew(ALPHA), tuple(r), QB))

        ffn(0, 0, tx)
        tx = norm3(0, 0, 4e-5)
        if STOP == 5:
            finish(x)
            return fin()
        sgu(tx)
        tx = norm3(0, 1, 1e-5)
        if STOP == 6:
            finish(x)
            return fin()
        ffn(0, 1, tx)
        tx = norm3(0, 2, 4e-5)
        ffn(1, 0, tx)
        norm3(1, 0, 4e-5)
        if STOP == 7:
            finish(x)
            return fin()
        def rwkv():
            t0 = bar()
            S0, S1, S2_, S3 = (unit_f(u, 2) for u in (0, 2, 4, 6))
            DT = cst[:, P:P + BIG]
            XX = B(1)
            R_, K_, SG, A_, G_, VV = B(3), B(4), B(5), B(6), B(7), B(8)
            ta = DV.do(TT(F(XX)[:, :, 1:T], X[:, :, 0:T - 1], X[:, :, 1:T], ALU.subtract), t0)
            tb = DV.do(TS(F(XX)[:, :, 0:1], X[:, :, 0:1], -1.0, None, ALU.mult), t0)
            txx = [ta, tb]
            nxm = [0]
            xm_free = [list(t0), list(t0)]

            def mixed(m, two=True):
                i = nxm[0] % 2
                nxm[0] += 1
                d = (B(2), B(9))[i]
                r = []
                pe = PE.now()
                for f in range(8):
                    t = DV.do(STT(F(d)[:, f, :], F(XX)[:, f, :], V("rwkv_mu_3", 8 * m + f), X[:, f, :], ALU.mult, ALU.add),
                              txx, xm_free[i])
                    r.append(split(F(d)[:, f, :], XP, f, t, pe) if two else t)
                xm_free[i] = list(r[-1]) if two else []
                return (i, F(d), t) if not two else tuple(r)

            def lora(xm, t, wv, tl, n, func, dst):
                b, w = FB.get()
                for k in range(8):
                    t = PE.do(MM(ps[0:n, b, 0:T], wv[:, k, :], xm[:, k, :], k == 0, k == 7),
                              *((w, t, tl) if k == 0 else ()), inc=k == 7)
                q = AT.do(AC(dst, ps[0:n, b, 0:T], func), t)
                free_bank(b, q)
                return t, q

            run(proj_tm(H, A["rwkv_w_rkv_3"][2], 0, 1024, cp_tm(xtm(VV)), mixed(2), FB))
            run(proj_fm(H, A["rwkv_w_rkv_3"][0], 0, 1024, cp_act(F(R_)), mixed(0), FB))
            run(proj_fm(H, A["rwkv_w_rkv_3"][1], 0, 1024, cp_act(F(K_)), mixed(1), FB))
            tdn = bar()
            xm_free = [tdn, tdn]
            kv_ = lambda n: A[n].rearrange("(k p) n -> p k n", p=P)
            s1, b1, tl1 = load((lambda q: k_(q[:, 0:512]), kv_("rwkv_w1_3")), (lambda q: k_(q[:, 512:1024]), kv_("rwkv_a1_3")))
            s3, b3_, tl3 = load((lambda q: k_(q[:, 0:1280]), kv_("rwkv_g1_3")))
            s2, b2, tl2 = load((lambda q: q[0:64, 0:1024], A["rwkv_w2_3"]), (lambda q: q[0:64, 1024:2048], A["rwkv_a2_3"]))
            s4, b4, tl4 = load((lambda q: q[:, 0:1024], A["rwkv_g2_3"][0:P, :]), (lambda q: q[0:32, 1024:2048], A["rwkv_g2_3"][P:160, :]))
            fence()
            k8 = lambda v: v.rearrange("p (k n) -> p k n", k=8)
            z1, z2 = tw[0:64, 0:T], tw[0:64, T:2 * T]
            z3, z4 = tw[:, 2 * T:3 * T], tw[0:32, 3 * T:4 * T]

            def second(parts, j):
                b, w = FB.get()
                for i in range(2):
                    f = 2 * j + i
                    for n, (wv, z, t) in enumerate(parts):
                        t = PE.do(MM(ps[:, b, i * T:(i + 1) * T], wv[:, f * P:(f + 1) * P], z, n == 0, n == len(parts) - 1),
                                  w, t, tl2, tl4, inc=n == len(parts) - 1)
                return b, t
            for m, wv, z, func, w2, bias, dst in ((3, b1[:, 0:512], z1, ACT.Tanh, b2[0:64, 0:1024], "rwkv_w0_3", SG),
                                                  (4, b1[:, 512:1024], z2, ACT.Copy, b2[0:64, 1024:2048], "rwkv_a0_3", A_)):
                i, xm, t = mixed(m, False)
                tp, t = lora(xm, t, k8(wv), tl1, 64, func, z)
                xm_free[i] = [tp]
                for j in range(4):
                    b, t2 = second([(w2, z, t)], j)
                    for i in range(2):
                        r = AT.do(AC(F(dst)[:, 2 * j + i, :], ps[:, b, i * T:(i + 1) * T], ACT.Sigmoid, bias=V(bias, 2 * j + i)), t2)
                    free_bank(b, r)
            i, xm, t = mixed(5, False)
            g1 = k8(b3_[:, 0:1280])
            tp, ta = lora(xm, t, g1[:, :, 0:P], tl3, P, ACT.Sigmoid, z3)
            tp, tb = lora(xm, t, g1[:, :, P:160], tl3, 32, ACT.Sigmoid, z4)
            for j in range(4):
                b, t2 = second([(b4[:, 0:1024], z3, ta), (b4[0:32, 1024:2048], z4, tb)], j)
                r = AT.do(AC(F(G_)[:, 2 * j:2 * j + 2, :], ps[:, b, :].rearrange("p (i t) -> p i t", t=T), ACT.Copy), t2)
                free_bank(b, r)
            free_slot(s1, PE.now())
            for s_ in (s2, s3, s4):
                free_slot(s_, PE.now())
            tc = bar() + [("side", side_sem, sd[0])]

            KK, BV = B(2), B(9)
            for f in range(8):
                t = DV.do(TS(F(KK)[:, f, :], F(K_)[:, f, :], V("rwkv_k_k_3", f), None, ALU.mult), tc)
            t = AT.do(AC(BV, KK, ACT.Square), t, tc)
            sel = C("sel").rearrange("p (f h) -> p f h", f=8)
            selt = C("selt").rearrange("p (f m) -> p f m", f=8)
            b, w = FB.get()
            for f in range(8):
                t = PE.do(MM(ps[0:16, b, 0:T], sel[:, f, :], F(BV)[:, f, :], f == 0, f == 7), w, t, tc, inc=f == 7)
            n16 = SM2[0:16, 0:T]
            t = AT.do(AC(n16, ps[0:16, b, 0:T], ACT.Sqrt), t)
            free_bank(b, t)
            t = DV.do(TS(n16, n16, 1e-12, None, ALU.max), t)
            t = DV.do(RCP(n16, n16), t)
            tk = []
            for j in range(4):
                b, w = FB.get()
                for i in range(2):
                    t2 = PE.do(MM(ps[:, b, i * T:(i + 1) * T], selt[0:16, 2 * j + i, :], n16, True, True), w, t, inc=i == 1)
                d = F(KK)[:, 2 * j:2 * j + 2, :]
                t2 = DV.do(TT(d, d, ps[:, b, :].rearrange("p (i t) -> p i t", t=T), ALU.mult), t2)
                free_bank(b, t2)
                tk.append(t2)
            t = DV.do(TT(BV, KK, A_, ALU.mult), tk, PE.now())
            for f in range(8):
                t = DV.do(TS(F(A_)[:, f, :], F(A_)[:, f, :], -1.0, V("rwkv_k_a_3", f), ALU.add, ALU.mult), t)
            tK = DV.do(STT(K_, A_, 1.0, K_, ALU.add, ALU.mult), t)
            for f in range(8):
                t = DV.do(STT(F(S0)[:, f, :], F(R_)[:, f, :], V("rwkv_r_k_3", f), F(K_)[:, f, :], ALU.mult, ALU.mult), tK)
            b, w = FB.get()
            for tt in range(2):
                for f in range(8):
                    t = PE.do(MM(ps[:, b, tt * 16:tt * 16 + 16], F(S0)[:, f, tt * P:(tt + 1) * P], sel[:, f, :], f == 0, f == 7),
                              w, t, inc=f == 7)
            BON = RSTD[:, 0:32]
            BON_t = DV.do(CP(BON, ps[:, b, 0:32]), t)
            free_bank(b, BON_t)
            cd = -float(np.exp(-0.5))
            for f in range(8):
                t2 = DV.do(lambda e, o=F(S1)[:, f, :], i=F(SG)[:, f, :]: e.tensor_tensor_scan(o, C("reset"), i, 0.0, ALU.mult, ALU.add), tK)
            t = DV.do(TT(SG, S1, SG, ALU.subtract), t2)
            c = AT.do(AC(S2_, S1, ACT.Exp, scale=-cd), t2)
            a = AT.do(AC(SG, SG, ACT.Exp, scale=cd), t)
            e_ = AT.do(AC(S1, S1, ACT.Exp, scale=cd), t)
            t2 = DV.do(TT(BV, BV, S2_, ALU.mult), c)
            t3 = DV.do(TT(K_, K_, S2_, ALU.mult), c, tK)
            t1 = DV.do(STT(KK, KK, -1.0, SG, ALU.mult, ALU.mult), a)
            t4 = DV.do(TT(R_, R_, S1, ALU.mult), e_, PE.now())
            PC = RSTD[:, 32:64].rearrange("p (f c) -> p f c", f=8)
            t5 = DV.do(CP(PC, S1.rearrange("p (f c t) -> p f c t", f=8, c=4)[:, :, :, 63]), e_)
            tall = [t1, t2, t3, t4, t5]
            AT_m, BT_m, KT_m = xtm(S0), xtm(S1), xtm(S2_)
            ttm = to_tm(F(KK), AT_m, QB, tall) + to_tm(F(BV), BT_m, QB, tall) + to_tm(F(K_), KT_m, QB, tall)

            def v4(m):
                return m.rearrange("p (t h i s) -> p t h i s", t=2, h=2, i=8)

            def pairs(left, right, mask, dst, banks):
                for tt in range(2):
                    for par_ in range(2):
                        b, w = banks.get()
                        for i in range(8):
                            for cp in range(2):
                                c0 = tt * P + cp * 64
                                rows = slice(64 * par_, 64 * par_ + 64)
                                t = PE.do(MM(ps[64 * cp:64 * cp + 64, b, i * 64:(i + 1) * 64], F(left)[rows, i, c0:c0 + 64],
                                             F(right)[rows, i, c0:c0 + 64], True, True),
                                          w, tall, inc=(i == 7 and cp == 1))
                        o = v4(dst)[:, tt, par_, :, :]
                        t = DV.do(TT(o, ps[:, b, :].rearrange("p (i s) -> p i s", i=8),
                                     C(mask).unsqueeze(1).broadcast_to((P, 8, 64)), ALU.mult), t, pairs_w)
                        free_bank(b, t)
                return t
            pairs_w = bar()
            N_, NT, A2T, RBT, RKT = S3, DT, B(1), B(5), B(6)
            pairs(KK, BV, "low", N_, FB)
            pairs(BV, KK, "upp", NT, FB)
            pairs(K_, KK, "upp", A2T, FB)
            pairs(BV, R_, "uppi", RBT, FB)
            pairs(K_, R_, "uppi", RKT, FB)
            tp = bar()
            T_, G, XS = B(2), B(4), B(9)
            bc = lambda n: C(n).unsqueeze(1).broadcast_to((P, 32, 64))
            m3 = lambda v: v.rearrange("p (a s) -> p a s", s=64)
            NM = tw
            t = DV.do(TT(m3(T_), m3(N_), bc("ml0"), ALU.mult), tp, ttm)
            t2 = DV.do(TT(m3(G), m3(NT), bc("mu0"), ALU.mult), tp, ttm)
            tn = DV.do(TT(m3(NM[:, :]), m3(NT), bc("mu1"), ALU.mult), tp)
            tT = [DV.do(TT(m3(T_), m3(T_), bc("eye64"), ALU.add), t)] * 4
            tG = [DV.do(TT(m3(G), m3(G), bc("eye64"), ALU.add), t2)] * 4

            def blk(left, right, banks, fn, *toks, q=None):
                r = []
                for tt in range(2):
                    for h in range(2):
                        b, w = banks.get()
                        for i in range(8):
                            for cp in range(2):
                                rows = slice(64 * cp, 64 * cp + 64)
                                t = PE.do(MM(ps[rows, b, i * 64:(i + 1) * 64], left(tt, h, i)[rows, :], right(tt, h, i)[rows, :], True, True),
                                          w, *toks, q(tt, h) if q else [], inc=(i == 7 and cp == 1))
                        t = fn(tt, h, ps[:, b, :].rearrange("p (i s) -> p i s", i=8), t)
                        free_bank(b, t)
                        r.append(t)
                return r

            def at4(m):
                return lambda tt, h, i: v4(m)[:, tt, h, i, :]

            def vat(m):
                return lambda tt, h, i: m[:, tt, (2 * i + h) * 64:(2 * i + h) * 64 + 64]
            def of(*lists):
                return lambda tt, h: [v[2 * tt + h] for v in lists]
            gread = []
            for lev in range(1, 6):
                tX = blk(at4(NM), at4(T_), KB,
                         lambda tt, h, bk, t: AT.do(AC(v4(XS)[:, tt, h, :, :], bk, ACT.Copy), t, gread), tn, q=of(tT))
                nmdone = PE.now()
                if lev < 5:
                    tn = DV.do(TT(m3(NM[:, :]), m3(NT), bc("mu%d" % (lev + 1)), ALU.mult), nmdone)

                def add_to(m, *toks):
                    def f(tt, h, bk, t):
                        o = v4(m)[:, tt, h, :, :]
                        return DV.do(TT(o, o, bk, ALU.add), t, *toks)
                    return f
                if lev < 5:
                    tT = blk(at4(G), at4(XS), KB, add_to(T_, nmdone), q=of(tG, tX))
                tG = blk(at4(XS), at4(G), KB, add_to(G), q=of(tG, tX))
                gread = PE.now()
            tgn = side(tw[:, 0:1024], A["rwkv_gn_g_3"].partition_broadcast(P), nmdone)
            tgn = side(tw[:, 1024:2048], A["rwkv_gn_b_3"].partition_broadcast(P))
            tinv = [nmdone]
            W1 = S3.rearrange("p (i c t) -> p i c t", i=8, c=4)
            tw1 = []
            for c in range(4):
                tt, cp = c // 2, c % 2
                b, w = QB.get()
                rows = slice(64 * cp, 64 * cp + 64)
                for i in range(8):
                    for h in range(2):
                        t = PE.do(MM(ps[64 * h:64 * h + 64, b, i * 64:(i + 1) * 64], vat(AT_m)(tt, h, i)[rows, :], at4(G)(tt, h, i)[rows, :], True, True),
                                  w, tG[2 * tt], tG[2 * tt + 1], inc=(i == 7 and h == 1))
                t = AT.do(AC(W1[:, :, c, :], ps[:, b, :].rearrange("p (i t) -> p i t", i=8), ACT.Copy), t, tinv)
                free_bank(b, t)
                tw1.append(t)
            Vm = xtm(VV)
            Z, W2, YI = B(9), B(2), DT
            tz = blk(at4(A2T), vat(Vm), FB, lambda tt, h, bk, t: AT.do(AC(v4(Z)[:, tt, h, :, :], bk, ACT.Copy), t, gread))
            tyi = blk(at4(RKT), vat(Vm), FB, lambda tt, h, bk, t: AT.do(AC(v4(YI)[:, tt, h, :, :], bk, ACT.Copy), t, tn))
            tw2 = blk(at4(G), at4(Z), QB, lambda tt, h, bk, t: DV.do(CP(v4(W2)[:, tt, h, :, :], bk), t, tinv), q=of(tz, tG))
            tz_read = PE.now()
            ST_ = ptw[:, 0:512].rearrange("p (i v) -> p i v", i=8)
            SX = ptw[:, 512:1024].rearrange("p (i v) -> p i v", i=8)
            Us = B(1)[:, 0:1024].rearrange("p (h i v) -> p h i v", h=2, i=8)
            ts = DV.do(lambda e: e.memset(ptw[:, 0:512], 0.0))
            SQ, YN, VB = Z, B(4), B(6)
            st, sv = SM2[:, 0:32], SM2[:, 32:64]
            gg = tw[:, 0:1024].rearrange("p (i h v) -> p i h v", i=8, h=2)
            gb = tw[:, 1024:2048].unsqueeze(1).broadcast_to((P, 2, 1024))
            vb = PO.do(TT(m3(VB), m3(VV), BON.unsqueeze(2).broadcast_to((P, 32, 64)), ALU.mult), tz_read, BON_t)
            vb = PO.do(TT(xtm(VB), xtm(VB), gb, ALU.add), vb, tgn)

            def group_norm(tt, *toks):
                half = slice(tt * 1024, tt * 1024 + 1024)
                y3 = YI[:, half].rearrange("p (a s) -> p a s", s=64)
                z3_ = SQ[:, half].rearrange("p (a s) -> p a s", s=64)
                s_, v_ = st[:, 16 * tt:16 * tt + 16], sv[:, 16 * tt:16 * tt + 16]
                t = DV.do(RED(s_, y3, ALU.add), *toks)
                t = DV.do(TS(s_, s_, 1.0 / 64, None, ALU.mult), t)
                t = DV.do(TT(y3, y3, s_.unsqueeze(2).broadcast_to((P, 16, 64)), ALU.subtract), t)
                t = AT.do(AC(SQ[:, half], YI[:, half], ACT.Square), t, tz_read)
                yield
                t = DV.do(RED(v_, z3_, ALU.add), t)
                t = DV.do(TS(v_, v_, 1.0 / 64, 64e-5, ALU.mult, ALU.add), t)
                t = AT.do(AC(v_, v_, ACT.Sqrt), t)
                yield
                t = DV.do(RCP(v_, v_), t)
                t = DV.do(TT(y3, y3, v_.unsqueeze(2).broadcast_to((P, 16, 64)), ALU.mult), t)
                yield
                yn = YN[:, half].rearrange("p (i h v) -> p i h v", i=8, h=2)
                r = [DV.do(TT(yn[:, :, h, :], v4(YI)[:, tt, h, :, :], gg[:, :, h, :], ALU.mult), t, tgn, tz_read) for h in range(2)]
                yield
                tgn_done.append(DV.do(TT(YN[:, half], YN[:, half], VB[:, half], ALU.add), r, vb))
            tgn_done = []
            side_work = None
            tw_all = tw1 + tw2 + tyi
            b3 = lambda b, rows: ps[rows, b, :].rearrange("p (i v) -> p i v", i=8)
            for c in range(4):
                tt, cp = c // 2, c % 2
                rows = slice(64 * cp, 64 * cp + 64)
                tu, ty = [], []
                for h in range(2):
                    hr = slice(64 * h, 64 * h + 64)
                    w = bank_rel[h]
                    for i in range(8):
                        t = PE.do(MM(ps[rows, h, i * 64:(i + 1) * 64], W1[hr, i, c, :], ST_[hr, i, :], True, True),
                                  w, ts, tw_all, inc=i == 7)
                    t = DV.do(TT(Us[rows, h, :, :], b3(h, rows), v4(W2)[rows, tt, h, :, :], ALU.add), t)
                    free_bank(h, t)
                    tu.append(t)
                for h in range(2):
                    hr = slice(64 * h, 64 * h + 64)
                    w = bank_rel[2 + h]
                    for i in range(8):
                        t = PE.do(MM(ps[rows, 2 + h, i * 64:(i + 1) * 64], F(R_)[hr, i, c * 64:(c + 1) * 64], ST_[hr, i, :], True, True),
                                  w, ts, inc=i == 7)
                    ty.append(t)
                w = bank_rel[6]
                for i in range(8):
                    for h in range(2):
                        hr = slice(64 * h, 64 * h + 64)
                        o = ps[hr, 6, i * 64:(i + 1) * 64]
                        PE.do(MM(o, vat(KT_m)(tt, h, i)[rows, :], vat(Vm)(tt, h, i)[rows, :], True, False), w, inc=False)
                        t = PE.do(MM(o, vat(BT_m)(tt, h, i)[rows, :], Us[rows, h, i, :], False, True), tu, inc=(i == 7 and h == 1))
                tsx = DV.do(TT(SX, ST_, ps[:, 6, :].rearrange("p (i v) -> p i v", i=8), ALU.add), t)
                free_bank(6, tsx)
                ts = DV.do(TT(ST_, SX, PC[:, :, c:c + 1].broadcast_to((P, 8, 64)), ALU.mult), tsx, ty)
                for h in range(2):
                    w = bank_rel[4 + h]
                    for i in range(8):
                        t = PE.do(MM(ps[rows, 4 + h, i * 64:(i + 1) * 64], at4(RBT)(tt, h, i)[rows, :], Us[rows, h, i, :], True, True),
                                  w, tu, inc=i == 7)
                    y = v4(YI)[rows, tt, h, :, :]
                    a = DV.do(TT(y, y, b3(2 + h, rows), ALU.add), ty[h])
                    free_bank(2 + h, a)
                    a = DV.do(TT(y, y, b3(4 + h, rows), ALU.add), t, a)
                    free_bank(4 + h, a)
                    if side_work:
                        next(side_work, None)
                if c == 1:
                    side_work = group_norm(0, a)
            run(side_work)
            run(group_norm(1, a))
            r = []

            def gated(j, bk, t):
                t = DV.do(TT(F(R_)[:, 2 * j:2 * j + 2, :], bk, F(G_)[:, 2 * j:2 * j + 2, :], ALU.mult), t)
                q = split(F(R_)[:, 2 * j:2 * j + 2, :], XP, slice(2 * j, 2 * j + 2), t)
                r.extend([q, q])
                return [t]
            tw0 = bar()
            wfree[0], wfree[1] = [tw0, tw0], [tw0, tw0]
            to_fm(xtm(YN), gated, QB, tgn_done)
            run(proj_fm(H, A["rwkv_w_o_3"], 0, 1024, ynew(ALPHA), tuple(r), FB))

        rwkv()
        tx = norm3(1, 1, 1e-5)
        if STOP == 8:
            finish(x)
            return fin()
        ffn(1, 1, tx)
        norm3(1, 2, 4e-5)
        finish(x)
        return fin()


_VEC_SRC = list(VEC)


def kernel(**inputs):
    import concourse.bacc as _bacc
    from concourse.bass_utils import run_bass_kernel_spmd as _run

    I = {n: np.asarray(a) for n, a in inputs.items()}
    nc = _bacc.Bacc("TRN2", target_bir_lowering=False, num_devices=1)
    arrays, A = {}, {}

    def give(name, a):
        a = np.ascontiguousarray(a)
        arrays["in_" + name] = a
        A[name] = nc.dram_tensor("in_" + name, a.shape, mybir.dt.from_np(a.dtype), kind="ExternalInput").ap()

    def fmaj(a):
        return a.reshape(T, 8, P).transpose(2, 1, 0).reshape(P, 8 * T)

    give("xT", fmaj(I["x"]))
    give("memT", fmaj(I["mem"]))
    tabs = const_tables()
    give("consts", np.concatenate([tabs[n] for n in EARLY], axis=1))
    give("consts2", np.concatenate([tabs[n] for n in LATE], axis=1))
    give("vecs", np.concatenate([I[n].reshape(-1, P).T for n in _VEC_SRC], axis=1))
    for n in ("wa_sink", "sinks_a_2", "da_lambda_q1", "da_lambda_k1", "da_lambda_q2", "da_lambda_k2"):
        give(n, I[n].reshape(-1))
    for n in ("w_in", "w_mem_kv", "w_da_o", "w_wa_o", "w_xa_o", "w_out", "w_router", "w_exp_gate", "w_exp_up",
              "w_exp_down", "w_in_a_2", "w_in_b_2", "w_out_2", "ffn_w_in_3", "ffn_w_out_3", "sgu_w_in_3",
              "sgu_w_out_3", "rwkv_w_rkv_3", "rwkv_w1_3", "rwkv_w2_3", "rwkv_a1_3", "rwkv_a2_3", "rwkv_g1_3",
              "rwkv_g2_3", "rwkv_w_o_3"):
        a = I[n]
        give(n, a[0] if a.shape[0] == 1 else a)
    give("spT", I["sgu_w_sp_3"][0].transpose(2, 0, 1).reshape(P, 16 * P))
    give("b_sp", I["sgu_b_sp_3"][0].reshape(-1))
    for n in ("sgu_ln_g_3", "sgu_ln_b_3", "rwkv_gn_g_3", "rwkv_gn_b_3"):
        give(n, I[n].reshape(-1))
    give("b_in_v", I["sgu_b_in_3"].reshape(-1)[2048:])
    o = nc.dram_tensor("out_0_dram", (P, 8 * T), F32, kind="ExternalOutput").ap()
    build(nc, A, o)
    r = _run(nc, [arrays], core_ids=[0])
    y = r.results[0]["out_0_dram"]
    return np.ascontiguousarray(y.reshape(P, 8, T).transpose(2, 1, 0)).reshape(1, T, D)
```

```python
from contextlib import ExitStack

import numpy as np
import concourse.bass as bass
from concourse import mybir

F32 = mybir.dt.float32
FR = mybir.dt.float32r
ALU = mybir.AluOpType
ACT = mybir.ActivationFunctionType
AX = mybir.AxisListType
P = 128
T = 256
D = 1024

U = 1024
PARTS = (0, 12, 32, 41)
SLOT_UNIT = {0: 32, 1: 34, 2: 36, 3: 38, 4: 0, 5: 2, 6: 4, 7: 6, 8: 8, 9: 10, 10: 28, 11: 30}
NSLOT = len(SLOT_UNIT)
BIG = 2048

VEC = {}
for _n, _c in (("attn_norm_g", 8), ("mem_norm_g", 8), ("ffn_norm_g", 8), ("final_norm_g", 8), ("norm_g_2", 16),
               ("final_g_2", 8), ("ln_g_3", 48), ("ln_b_3", 48), ("rwkv_mu_3", 48), ("rwkv_w0_3", 8),
               ("rwkv_a0_3", 8), ("rwkv_k_k_3", 8), ("rwkv_k_a_3", 8), ("rwkv_r_k_3", 8), ("sgu_b_in_3", 32),
               ("da_subln_g", 1)):
    VEC[_n] = (sum(c for _, c in VEC.values()), _c)
NVEC = sum(c for _, c in VEC.values())


def const_tables():
    p = np.arange(P)
    q = (np.arange(2)[None, :, None] * P + p[:, None, None]).astype(np.int64)
    k = np.arange(T)[None, None, :]
    dist = np.abs(q - k)
    out = {}
    out["ident"] = np.eye(P)
    out["d1"] = dist.reshape(P, -1)
    out["d2"] = np.where(dist <= 128, dist, 1e32).reshape(P, -1)
    out["ma"] = np.where((q - k >= 0) & (q - k < 128), 0.0, -1e30).reshape(P, -1)
    out["mb"] = np.where(q - k >= 0, 0.0, -1e30).reshape(P, -1)
    inv = np.float32(10000.0) ** (-np.arange(0, 64, 2, dtype=np.float32) / np.float32(64))
    ang = np.arange(T, dtype=np.float32)[None, :] * inv[p % 32][:, None].astype(np.float32)
    out["cos"] = np.cos(ang)
    out["sin"] = np.sin(ang)
    r = np.zeros((P, P))
    for m in range(P):
        if m % 64 < 32:
            r[m + 32, m] = -1.0
        else:
            r[m - 32, m] = 1.0
    out["rot"] = r
    out["ones"] = np.full((P, P), 1.0 / 1024)
    out["iota32"] = np.tile(np.arange(32), (P, 1))
    tt = p % 64
    s = np.arange(64)[None, :]
    t = tt[:, None]
    out["low"] = (s < t) * 1.0
    out["upp"] = (t < s) * 1.0
    out["uppi"] = (t <= s) * 1.0
    out["eye64"] = (t == s) * 1.0
    for i, b in enumerate((1, 2, 4, 8, 16, 32)):
        same = (t // (2 * b)) == (s // (2 * b))
        out["ml%d" % i] = (same & (t % (2 * b) >= b) & (s % (2 * b) < b)) * 1.0
        out["mu%d" % i] = (same & (t % (2 * b) < b) & (s % (2 * b) >= b)) * 1.0
    out["reset"] = np.tile((np.arange(T) % 64 != 0) * 1.0, (P, 1))
    sel = np.zeros((P, 8, 16))
    selt = np.zeros((P, 8, P))
    for f in range(8):
        for h in range(2):
            sel[64 * h:64 * h + 64, f, 2 * f + h] = 1.0
            selt[2 * f + h, f, 64 * h:64 * h + 64] = 1.0
    out["sel"] = sel.reshape(P, -1)
    out["selt"] = selt.reshape(P, -1)
    return {n: a.astype(np.float32) for n, a in out.items()}


CT = {n: a.shape[1] for n, a in const_tables().items()}
LATE = [n for n in CT if n in ("low", "upp", "uppi", "eye64", "reset", "sel", "selt") or n[:2] in ("ml", "mu")]
FIRST = ["ident", "ones"]
EARLY = FIRST + [n for n in CT if n not in LATE and n not in FIRST]
NFIRST = sum(CT[n] for n in FIRST)
COFF = {}
for _l in (EARLY, LATE):
    _o = 0
    for _n in _l:
        COFF[_n] = _o
        _o += CT[_n]
NCONST = sum(CT[n] for n in EARLY)


class Queue:

    def __init__(self, sem):
        self.sem = sem
        self.n = 0
        self.ops = []
        self.seen = {}

    def wait(self, toks):
        for t in toks:
            if t is None:
                continue
            if isinstance(t, list):
                self.wait(t)
                continue
            key, sem, v = t
            if self.seen.get(key, 0) < v:
                self.seen[key] = v
                self.ops.append(lambda e, sem=sem, v=v: e.wait_ge(sem, v))

    def do(self, fn, *toks, inc=True):
        self.wait(toks)
        if not inc:
            self.ops.append(fn)
            return None
        self.n += 1
        self.ops.append(lambda e, fn=fn: fn(e).then_inc(self.sem, 1))
        return (id(self), self.sem, self.n)

    def now(self):
        return (id(self), self.sem, self.n) if self.n else None

    def play(self, e):
        for op in self.ops:
            op(e)


def MM(o, l, r, start, stop, skip=False):
    return lambda e: e.matmul(o, l, r, start=start, stop=stop, skip_group_check=skip)


def TR(o, i, ident):
    return lambda e: e.transpose(o, i, ident)


def TT(o, a, b, op):
    return lambda e: e.tensor_tensor(o, a, b, op)


def TS(o, a, s1, s2, op0, op1=None):
    if op1 is None:
        return lambda e: e.tensor_scalar(o, a, s1, None, op0)
    return lambda e: e.tensor_scalar(o, a, s1, s2, op0, op1)


def STT(o, a, s, b, op0, op1):
    return lambda e: e.scalar_tensor_tensor(out=o, in0=a, scalar=s, in1=b, op0=op0, op1=op1)


def CP(o, i):
    return lambda e: e.tensor_copy(o, i)


def RCP(o, i):
    return lambda e: e.reciprocal(o, i)


def RED(o, i, op, neg=False):
    if neg:
        return lambda e: e.tensor_reduce(o, i, AX.X, op, negate=True)
    return lambda e: e.tensor_reduce(o, i, AX.X, op)


def AC(o, i, f, **kw):
    return lambda e: e.activation(o, i, f, **kw)


def build(nc, A, out):
    with ExitStack() as ctx:
        def sb(name, cols):
            return ctx.enter_context(nc.sbuf_tensor(name, [P, cols], F32))

        def sem(name):
            return ctx.enter_context(nc.semaphore(name))

        af, ar = [], []
        for i in range(len(PARTS) - 1):
            n = (PARTS[i + 1] - PARTS[i]) * U
            with nc.sbuf_tensor("af%d" % i, [P, n], F32) as a:
                pass
            af.append(a)
            ar.append(ctx.enter_context(nc.sbuf_tensor("ar%d" % i, [P, n], FR)))
        mem = dict(af=af, ar=ar, cst=sb("cst", NCONST), vec=sb("vec", NVEC), xw=sb("xw", 3 * 1024),
                   ptw=sb("ptw", 1024), tw=sb("tw", 4 * 512), sm=sb("sm", 1024),
                   ps=ctx.enter_context(nc.psum_tensor("ps", [P, 8, 512], F32)))
        sems = {n: sem(n) for n in ("s_pe", "s_dve", "s_act", "s_pool", "s_sp", "s_small", "s_small2", "s_out", "s_side", "s_side2")}
        ld_sem = [sem("s_ld%d" % i) for i in range(NSLOT)]
        plan = []
        emit(nc, A, out, mem, sems, ld_sem, None, plan)
        queues, n_out = emit(nc, A, out, mem, sems, ld_sem, plan, [])
        PE, DV, AT, PO, SP = queues
        blk = ctx.enter_context(nc.Block())

        @blk.sync
        def _(e):
            SP.play(e)
            e.wait_ge(sems["s_out"], n_out)

        @blk.tensor
        def _(e):
            PE.play(e)

        @blk.scalar
        def _(e):
            AT.play(e)

        @blk.vector
        def _(e):
            DV.play(e)

        @blk.gpsimd
        def _(e):
            PO.play(e)


def emit(nc, A, out, mem, sems, ld_sem, plan, seen_loads):
    af, ar, cst, vec, xw, ptw, tw, sm, ps = (mem[n] for n in ("af", "ar", "cst", "vec", "xw", "ptw", "tw", "sm", "ps"))
    PE, DV, AT, PO, SP = (Queue(sems[n]) for n in ("s_pe", "s_dve", "s_act", "s_pool", "s_sp"))
    ld_n = [0] * NSLOT
    out_sem, side_sem = sems["s_out"], (sems["s_side"], sems["s_side2"])
    ldc = [0, 0]

    def C(name):
        return (xw if name in LATE else cst)[:, COFF[name]:COFF[name] + CT[name]]

    def V(name, i=0):
        o = VEC[name][0] + i
        return vec[:, o:o + 1]

    def Vs(name, i, n):
        o = VEC[name][0] + i
        return vec[:, o:o + n]

    def units_of(tensors, u, n):
        i = 0
        while u >= PARTS[i + 1]:
            i += 1
        assert u + n <= PARTS[i + 1]
        return tensors[i][:, (u - PARTS[i]) * U:(u + n - PARTS[i]) * U]

    def unit_f(u, n):
        return units_of(af, u, n)

    def unit_r(u, n):
        return units_of(ar, u, n)

    def B(i, n=1):
        return unit_f(12 + 2 * i, 2 * n)

    def R(i, n=1):
        return unit_r(12 + 2 * i, 2 * n)

    WH = [unit_r(0, 2), unit_r(4, 2)]
    WL = [unit_r(2, 2), unit_r(6, 2)]
    XP = (unit_r(8, 2), unit_r(10, 2))

    def f_(ap):
        return ap.bitcast(F32)

    def F(ap, n=8):
        return ap.rearrange("p (f t) -> p f t", f=n)

    IDN = C("ident")

    bank_rel = [[] for _ in range(8)]

    class Banks:
        def __init__(self, ids):
            self.ids, self.i = ids, 0

        def get(self):
            b = self.ids[self.i % len(self.ids)]
            self.i += 1
            w = bank_rel[b]
            bank_rel[b] = []
            return b, w

    def free_bank(b, *toks):
        bank_rel[b] = list(toks)

    slots = [0, 1, 2, 3]
    slot_i = [0]
    slot_rel = [[] for _ in range(NSLOT)]
    rq = [0]
    issued = {}
    wcnt = [0]
    wfree = [[[], []], [[], []]]

    def fill(parts):
        s = slots[slot_i[0] % len(slots)]
        slot_i[0] += 1
        SP.wait(slot_rel[s])
        slot_rel[s] = []
        base = unit_f(SLOT_UNIT[s], 2)
        for view, src in parts:
            def go(e, dst=view(base), src=src, q=ld_sem[s]):
                e.dma_start(dst, src).then_inc(q, 16)
            SP.ops.append(go)
            ld_n[s] += 16
        return s, base, ("ld%d" % s, ld_sem[s], ld_n[s])

    def load(*parts):
        seen_loads.append(None)
        rq[0] += 1
        return fill(parts)

    def free_slot(s, *toks):
        slot_rel[s] = list(toks)

    def issue(i, n, parts):
        s, base, tl = fill(parts)
        j = wcnt[0] % 2
        wcnt[0] += 1
        ends = []
        step = n // 2
        for h in range(2):
            c = h * step
            hi, lo, src = WH[j][:, c:c + step], WL[j][:, c:c + step], base[:, c:c + step]
            a = AT.do(AC(hi, src, ACT.Copy), tl, wfree[j][h])
            d = DV.do(TT(lo, src, f_(hi), ALU.subtract), a, tl, wfree[j][h])
            ends.append(d)
        free_slot(s, a, *ends)
        issued[i] = (j, ends)

    def split_load(n, *parts):
        i = rq[0]
        rq[0] += 1
        seen_loads.append((n, parts))
        if i not in issued:
            issue(i, n, parts)
        if plan is not None and i + 1 < len(plan) and plan[i + 1] is not None:
            issue(i + 1, *plan[i + 1])
        j, ends = issued.pop(i)
        return (WH[j][:, 0:n], WL[j][:, 0:n]), ends, j

    def fence():
        seen_loads.append(None)
        rq[0] += 1

    def bar():
        return [q.now() for q in (PE, DV, AT, PO) if q.now()]

    def small(dst, src, g=0):
        def go(e, dst=dst, src=src, q=sems[("s_small", "s_small2")[g]]):
            e.dma_start(dst, src).then_inc(q, 16)
        AT.ops.append(go)
        ldc[g] += 16

    def first_x(e):
        e.dma_start(B(0), A["xT"]).then_inc(sems["s_small"], 16)
    SP.ops.append(first_x)
    ldc[0] += 16
    small(vec[:, :], A["vecs"])
    small(cst[:, 0:NFIRST], A["consts"][:, 0:NFIRST])
    CONST = ("const", sems["s_small"], ldc[0])
    SINK = sm[:, 0:32]
    LAM = sm[:, 32:288].rearrange("p (a b) -> p a b", a=4)
    small(B(2), A["memT"], 1)
    small(cst[:, NFIRST:NCONST], A["consts"][:, NFIRST:NCONST], 1)
    small(sm[:, 0:16], A["wa_sink"].partition_broadcast(P), 1)
    small(sm[:, 16:32], A["sinks_a_2"].partition_broadcast(P), 1)
    for i, n in enumerate(("da_lambda_q1", "da_lambda_k1", "da_lambda_q2", "da_lambda_k2")):
        small(LAM[:, i, :], A[n].partition_broadcast(P), 1)
    CONST2 = ("const2", sems["s_small2"], ldc[1])
    NSINK = sm[:, 288:320]
    LV = sm[:, 320:328]
    ST = sm[:, 384:512].rearrange("p (r c) -> p r c", r=4)
    RSTD = sm[:, 512:768]
    SM2 = sm[:, 768:1024]

    DB = Banks([0, 1])
    KB = Banks([0, 1, 2, 3, 4, 5, 6, 7])

    def fmsum(src, n, bank, w, ready):
        for f in range(n):
            t = PE.do(MM(ps[:, bank, 0:T], C("ones"), src[:, f, :], f == 0, f == n - 1), w, ready[f], inc=f == n - 1)
        return t

    def rstd_of(src, tmp, eps, banks, ready):
        r = []
        for j in range(4):
            v = slice(2 * j, 2 * j + 2)
            r += [AT.do(AC(F(tmp)[:, v, :], F(src)[:, v, :], ACT.Square), ready[j])] * 2
        b, w = banks.get()
        t = fmsum(F(tmp), 8, b, w, r)
        t = DV.do(TS(RSTD, ps[:, b, 0:T], eps, None, ALU.add), t, AT.now())
        free_bank(b, t)
        t = AT.do(AC(RSTD, RSTD, ACT.Sqrt), t)
        return DV.do(RCP(RSTD, RSTD), t)

    def split(src, pair, k, *toks):
        hi, lo = (F(v, v.shape[1] // T)[:, k, :] for v in pair)
        a = AT.do(AC(hi, src, ACT.Copy), *toks)
        return [a, DV.do(TT(lo, src, f_(hi), ALU.subtract), a)]

    def staged(n, first, second, lag=2):
        a, r = [], []
        for f in range(n + lag):
            if f < n:
                a.append(first(f))
            if f >= lag:
                r.append(second(f - lag, a[f - lag]))
        return r

    def rms(src, tmp, dst, eps, g, banks, *toks, pair=None, pair_w=()):
        t = rstd_of(src, tmp, eps, banks, [list(toks)] * 4)
        pe = PE.now()

        def first(f):
            o = F(dst)[:, f, :]
            d = DV.do(STT(o, F(src)[:, f, :], g(f), RSTD, ALU.mult, ALU.mult), t, pe)
            return d if pair is None else (d, AT.do(AC(F(pair[0])[:, f, :], o, ACT.Copy), d, list(pair_w)))

        def second(f, d):
            if pair is None:
                return [d]
            d, a = d
            hi, lo = (F(v)[:, f, :] for v in pair)
            return [a, DV.do(TT(lo, F(dst)[:, f, :], f_(hi), ALU.subtract), d, a)]
        return staged(8, first, second)

    def ln(y, tmp, dst, eps, g, b_, banks, ready, pair):
        b, w = banks.get()
        t = fmsum(F(y), 8, b, w, [ready[f // 2] for f in range(8)])
        mu = ps[:, b, 0:T].unsqueeze(1).broadcast_to((P, 2, T))
        r = []
        for j in range(4):
            v = F(y)[:, 2 * j:2 * j + 2, :]
            r.append(DV.do(TT(v, v, mu, ALU.subtract), t))
        free_bank(b, r[-1])
        t0 = r[-1]
        t = rstd_of(y, tmp, eps, banks, r)
        pe = PE.now()

        def first(f):
            s, o = F(tmp)[:, f, :], F(dst)[:, f, :]
            a = DV.do(STT(s, F(y)[:, f, :], g(f), RSTD, ALU.mult, ALU.mult), t, pe)
            h = AT.do(AC(F(pair[0])[:, f, :], s, ACT.Identity, bias=b_(f)), a) if pair else None
            if f % 2:
                c = DV.do(TS(o, s, b_(f), None, ALU.add), a, t0)
            else:
                c = AT.do(AC(o, s, ACT.Identity, bias=b_(f)), a, t0)
            return c, h

        def second(f, ch):
            if pair is None:
                return [ch[0]]
            hi, lo = (F(v)[:, f, :] for v in pair)
            return [*ch, DV.do(TT(lo, F(dst)[:, f, :], f_(hi), ALU.subtract), *ch)]
        return staged(8, first, second)

    def MM3(o, left, right, start, stop, *toks, inc=False, skip=False):
        (lh, ll), (rh, rl) = left, right
        PE.do(MM(o, lh, rh, start, False, skip), *toks, inc=False)
        PE.do(MM(o, lh, rl, False, False, skip), inc=False)
        return PE.do(MM(o, ll, rh, False, stop, skip), inc=inc)

    def both(pair, fn):
        return fn(pair[0]), fn(pair[1])

    def rdy(ready, k):
        return ready[k] if isinstance(ready, tuple) else ready

    def fm(x, wl, evac, ready, banks):
        wp, ends, jb = wl
        wp = both(wp, k_)
        b, w = banks.get()
        for h in range(2):
            for i in range(2):
                for k in range(4 * h, 4 * h + 4):
                    t = MM3(ps[:, b, i * T:(i + 1) * T], both(wp, lambda v: v[:, k, i * P:(i + 1) * P]),
                            both(x, lambda v: v[:, k, :]), k == 0 and i == 0, k == 7,
                            w, ends[h], rdy(ready, k), inc=(i == 1 and k % 4 == 3), skip=True)
            wfree[jb][h] = [t]
            if h == 1:
                free_bank(b, *evac(ps[:, b, :].rearrange("p (i t) -> p i t", t=T), t))
            yield t

    def run(g):
        last = None
        for last in g:
            pass
        return last

    def k_(ap, k=8):
        return ap.rearrange("p (k n) -> p k n", k=k)

    def wk(src, c0, n=256):
        return (lambda s: k_(s[:, 0:8 * n]), src.rearrange("(k p) n -> p k n", p=P)[:, :, c0:c0 + n])

    def proj_fm(x, src, c0, ncols, evac, ready, banks):
        for c in range(0, ncols, 256):
            yield from fm(x, split_load(2048, wk(src, c0 + c)), lambda bk, t, c=c: evac(c // 256, bk, t), ready, banks)

    def proj_tm(x, src, c0, ncols, evac, ready, banks):
        for c in range(0, ncols, 256):
            n = min(256, ncols - c)
            wp, ends, j = split_load(8 * n, wk(src, c0 + c, n))
            v = both(wp, k_)
            b, w = banks.get()
            for h in range(2):
                for tt in range(2):
                    for k in range(4 * h, 4 * h + 4):
                        t = MM3(ps[:, b, tt * n:(tt + 1) * n], both(x, lambda u: u[:, k, tt * P:(tt + 1) * P]),
                                both(v, lambda u: u[:, k, :]), k == 0 and tt == 0, k == 7, w, rdy(ready, k), ends[h],
                                inc=(tt == 1 and k % 4 == 3), skip=True)
                wfree[j][h] = [t]
                if h == 1:
                    free_bank(b, *evac(c, ps[:, b, 0:2 * n].rearrange("p (t n) -> p t n", t=2), t))
                yield t

    def proj_dup(x, src, c0, nkv, evac, ready, banks):
        sv = src.rearrange("(k p) n -> p k n", p=P)
        for j0 in range(0, nkv, 2):
            def at(s, jj, d):
                return s.rearrange("p (k j d e) -> p k j d e", k=8, j=2, d=2)[:, :, jj, d, :]
            parts = []
            for jj in range(2):
                c = c0 + 64 * (j0 + jj)
                for d in range(2):
                    parts.append((lambda s, d=d, jj=jj: at(s, jj, d), sv[:, :, c:c + 64]))
            yield from fm(x, split_load(2048, *parts), lambda bk, t, j0=j0: evac(j0 // 2, bk, t), ready, banks)

    def acc_fm(x, nk, src, evac, ready, banks4):
        bk = [banks4.get() for _ in range(4)]
        sv = src.rearrange("(k p) n -> p k n", p=P)
        for k0 in range(0, nk, 2):
            wp, ends, j = split_load(2048, (lambda q: k_(q, 2), sv[:, k0:k0 + 2, :]))
            v = both(wp, lambda u: k_(u, 2))
            for kk in range(2):
                k = k0 + kk
                for f in range(8):
                    b, w = bk[f // 2]
                    i = f % 2
                    t = MM3(ps[:, b, i * T:(i + 1) * T], both(v, lambda u: u[:, kk, f * P:(f + 1) * P]),
                            both(x, lambda u: u[:, k, :]), k == 0 and i == 0, k == nk - 1,
                            rdy(ready, k), w, ends[kk], inc=f == 7 or (k == nk - 1 and i == 1), skip=True)
                    if k == nk - 1 and i == 1:
                        free_bank(b, *evac(f // 2, ps[:, b, :].rearrange("p (i t) -> p i t", t=T), t))
                wfree[j][kk] = [t]
                yield t

    def cp_act(dst, scale=None):
        def f(j, bk, t):
            n = bk.shape[1]
            kw = {} if scale is None else {"scale": scale}
            return [AT.do(AC(dst[:, 2 * j:2 * j + n, :], bk, ACT.Copy, **kw), t)]
        return f

    def cp_tm(dst):
        def f(c, bk, t):
            return [AT.do(AC(dst[:, :, c:c + bk.shape[2]], bk, ACT.Copy), t)]
        return f

    def to_tm(src, dst, banks, *toks):
        r = []
        first = True
        for tt in range(2):
            for h in range(2):
                b, w = banks.get()
                for i in range(4):
                    f = 4 * h + i
                    t = PE.do(TR(ps[:, b, i * P:(i + 1) * P], src[:, f, tt * P:(tt + 1) * P], IDN),
                              *((w, *toks) if i == 0 else ()), inc=i == 3)
                q = DV if h else AT
                o = dst[:, tt, h * 512:(h + 1) * 512]
                fn = CP(o, ps[:, b, :]) if h else AC(o, ps[:, b, :], ACT.Copy)
                t = q.do(fn, t)
                free_bank(b, t)
                r.append(t)
        return r

    def to_fm(src, evac, banks, *toks):
        r = []
        for j in range(4):
            b, w = banks.get()
            for i in range(2):
                for tt in range(2):
                    f = 2 * j + i
                    t = PE.do(TR(ps[:, b, i * T + tt * P:i * T + (tt + 1) * P], src[:, tt, f * P:(f + 1) * P], IDN),
                              *((w, *toks) if i == 0 and tt == 0 else ()), inc=(i == 1 and tt == 1))
            q = evac(j, ps[:, b, :].rearrange("p (i t) -> p i t", t=T), t)
            free_bank(b, *q)
            r += q
        return r

    S2 = Banks([2])
    PT2 = Banks([4])
    OB = Banks([6, 7])
    xfree = [[], [], []]
    ptfree = [[]]

    def attention(units, ready, done):
        state = []

        def stage_a(i, u):
            X = xw[:, (i % 3) * 1024:(i % 3 + 1) * 1024].rearrange("p (m c) -> p m c", m=2)
            st = ST[:, i % 4, :]
            b0, w0 = S2.get()
            w0 = w0 + bank_rel[b0 + 1]
            for qt in range(2):
                for m in range(2):
                    t = u["scores"](m, qt, ps[:, b0 + m, qt * T:(qt + 1) * T], [w0, ready, u.get("ready")] if m + qt == 0 else [], qt == 1 and m == 1)
            S = ps[:, b0:b0 + 2, :]
            wx = xfree[i % 3]
            if u["bias"] is None:
                tx = DV.do(CP(X, S), t, wx)
            elif len(u["bias"]) == 1:
                tab, fac = u["bias"][0]
                tx = DV.do(STT(X, tab.unsqueeze(1).broadcast_to((P, 2, 512)), fac, S, ALU.mult, ALU.add), t, wx)
            else:
                for m, (tab, fac) in enumerate(u["bias"]):
                    tx = DV.do(STT(X[:, m, :], tab, fac, S[:, m, :], ALU.mult, ALU.add), t, wx)
            free_bank(b0, tx)
            free_bank(b0 + 1, tx)
            X4 = X.rearrange("p m (q k) -> p (m q) k", q=2)
            nm, s, r = st[:, 0:4], st[:, 4:8], st[:, 8:12]
            t = DV.do(RED(nm, X4, ALU.max, neg=True), tx)
            sink = u["sink"]
            if sink is not None:
                ns = NSINK[:, sink:sink + 2].unsqueeze(2).broadcast_to((P, 2, 2))
                sk = SINK[:, sink:sink + 2].unsqueeze(2).broadcast_to((P, 2, 2))
                n3 = nm.rearrange("p (m q) -> p m q", m=2)
                t = DV.do(TT(n3, n3, ns, ALU.min), t)
                e3 = st[:, 12:16].rearrange("p (m q) -> p m q", m=2)
                te = DV.do(TT(e3, n3, sk, ALU.add), t)
            return X4, st, t, te if sink is not None else None

        def stage_e(u, X4, st, t, te):
            nm, s = st[:, 0:4], st[:, 4:8]
            for g in range(4):
                ta = AT.do(AC(X4[:, g, :], X4[:, g, :], ACT.Exp, bias=nm[:, g:g + 1], accum_out=s[:, g:g + 1]), t)
            if u["sink"] is not None:
                ta = AT.do(AC(st[:, 12:16], st[:, 12:16], ACT.Exp), te)
            return X4, st, ta

        def stage_n(i, u, X4, st, ta):
            s, r = st[:, 4:8], st[:, 8:12]
            if u["sink"] is not None:
                ta = DV.do(TT(s, s, st[:, 12:16], ALU.add), ta)
            t = DV.do(RCP(r, s), ta)
            if u["lam"] is not None:
                t = DV.do(TS(r[:, 2:4], r[:, 2:4], u["lam"], None, ALU.mult), t)
                maps = [0]
                for qt in range(2):
                    t2 = DV.do(TS(X4[:, 2 + qt, :], X4[:, 2 + qt, :], r[:, 2 + qt:3 + qt], None, ALU.mult), t)
                    tn = DV.do(STT(X4[:, qt, :], X4[:, qt, :], r[:, qt:qt + 1], X4[:, 2 + qt, :], ALU.mult, ALU.add), t2)
            else:
                maps = [0, 1]
                for g in range(4):
                    tn = DV.do(TS(X4[:, g, :], X4[:, g, :], r[:, g:g + 1], None, ALU.mult), t)
            return i, X4, maps, tn

        def stage_b(u, i, X4, maps, tn):
            PT = ptw[:, :].rearrange("p (m k q) -> p m k q", m=2, k=2)
            tp = []
            for m in maps:
                b = 4 + m
                w = bank_rel[b]
                for kt in range(2):
                    for qt in range(2):
                        t = PE.do(TR(ps[:, b, kt * T + qt * P:kt * T + (qt + 1) * P],
                                     X4[:, 2 * m + qt, kt * P:(kt + 1) * P], IDN),
                                  *((w, tn) if kt + qt == 0 else ()), inc=kt + qt == 2)
                q = AT.do(AC(PT[:, m, :, :], ps[:, b, :].rearrange("p (k q) -> p k q", k=2), ACT.Copy), t, ptfree[0])
                free_bank(b, q)
                tp.append(q)
            xfree[i % 3] = [PE.now()]
            return u, PT, tp

        def stage_c(u, PT, tp):
            ptfree[0] = u["pv"](PT, tp)
            done.append(ptfree[0])

        prev = None
        for i, u in enumerate(units):
            if prev is not None:
                n = stage_n(*prev)
            a = stage_a(i, u)
            yield
            if prev is not None:
                c = stage_b(prev[1], *n)
            a = stage_e(u, *a)
            yield
            if prev is not None:
                stage_c(*c)
                yield
            prev = (i, u, *a)
        n = stage_n(*prev)
        yield
        c = stage_b(prev[1], *n)
        yield
        stage_c(*c)
        yield

    def par(a, b, ra=1, rb=1):
        live, at = {0: a, 1: b}, [0, 0]
        while live:
            i = min(live, key=lambda i: (at[i] + 1) / (ra, rb)[i])
            at[i] += 1
            try:
                next(live[i])
            except StopIteration:
                del live[i]

    def pv_pair(fns, ob=OB):
        v, dst = fns

        def go(PT, tp):
            b, w = ob.get()
            for kt in range(2):
                for m in range(2):
                    t = PE.do(MM(ps[64 * m:64 * m + 64, b, 0:T], v(m, kt), PT[:, m, kt, :], kt == 0, kt == 1),
                              *((w, tp) if m + kt == 0 else ()), inc=(m == 1 and kt == 1))
            d = AT.do(AC(dst, ps[:, b, 0:T], ACT.Copy), t)
            free_bank(b, d)
            return [t, d]
        return go

    def score_pair(q, k):
        def go(m, qt, o, w, inc):
            return PE.do(MM(o, q(m)[:, qt * P:(qt + 1) * P], k(m), True, True), *w, inc=inc)
        return go

    for q in (DV, PE, AT, PO):
        q.wait([CONST])
    x = B(0)
    H = both(XP, F)
    pr = lambda i, j: (R(i), R(j))
    t_h = tuple(rms(x, B(9), B(8), 1e-6, lambda f: V("attn_norm_g", f), KB, pair=XP))
    W1 = A["w_in"]
    daq, dak, dav, waq, wakv, xaq, mk = B(3), B(4), B(5), B(6), B(7), B(8), B(9)
    wak = F(wakv[:, 0:1024], 4)
    wav = wakv[:, 1024:1536].rearrange("p (t n) -> p t n", t=2)
    xtm = lambda b: b.rearrange("p (t n) -> p t n", t=2)
    WK = A["w_mem_kv"]
    mp = pr(6, 7)

    def first():
        yield from proj_fm(H, W1, 0, 1024, cp_act(F(daq), 0.125), t_h, DB)

    tm2 = []

    def memory_norm():
        for q in (DV, AT, PE, PO):
            q.wait([CONST2])
        DV.do(TS(NSINK, SINK, -1.0, None, ALU.mult))
        lt = tw[:, 0:128].rearrange("p (a b) -> p a b", a=2)
        t = DV.do(TT(lt[:, 0, :], LAM[:, 0, :], LAM[:, 1, :], ALU.mult))
        t = DV.do(TT(lt[:, 1, :], LAM[:, 2, :], LAM[:, 3, :], ALU.mult))
        t = DV.do(RED(LV[:, 0:2], lt, ALU.add), t)
        t = AT.do(AC(LV[:, 2:4], LV[:, 0:2], ACT.Exp), t)
        t = DV.do(TT(LV[:, 4:5], LV[:, 3:4], LV[:, 2:3], ALU.subtract), t)
        lam_init = 0.8 - 0.6 * float(np.exp(-0.3 * 0))
        t = DV.do(TS(LV[:, 5:6], LV[:, 4:5], -lam_init, None, ALU.add), t)
        t = DV.do(TS(LV[:, 6:7], V("da_subln_g"), 1.0 - lam_init, None, ALU.mult))
        yield
        tm2.extend(rms(B(2), B(9), B(8), 1e-6, lambda f: V("mem_norm_g", f), Banks([2, 3]), bar(), pair=mp))
        yield
    NLAM, SUBG = LV[:, 5:6], LV[:, 6:7]
    par(first(), memory_norm(), 2, 1)
    tmv = tm2
    run(proj_fm(H, W1, 1024, 1024, cp_act(F(dak)), t_h, KB))
    run(proj_tm(H, W1, 2048, 1024, cp_tm(xtm(dav)), t_h, KB))
    mvb = xaq
    odt = B(2)
    tda = bar()
    oda = []
    ODT = xtm(odt)

    def da_units():
        for h in range(8):
            def pv(PT, tp, h=h):
                b, w = OB.get()
                for qt in range(2):
                    for kt in range(2):
                        t = PE.do(MM(ps[:, b, qt * P:(qt + 1) * P], PT[:, 0, kt, qt * P:(qt + 1) * P],
                                     xtm(dav)[:, kt, h * P:(h + 1) * P], kt == 0, kt == 1),
                                  *((w, tp) if qt + kt == 0 else ()), inc=qt + kt == 2)
                d = AT.do(AC(ODT[:, :, h * P:(h + 1) * P], ps[:, b, 0:T].rearrange("p (q e) -> p q e", q=2),
                             ACT.Copy), t, tmv)
                free_bank(b, d)
                return [t, d]
            slope = 2.0 ** (-(h + 1))
            yield {"scores": score_pair(lambda m, h=h: F(daq)[64 * m:64 * m + 64, h, :],
                                        lambda m, h=h: F(dak)[64 * m:64 * m + 64, h, :]),
                   "bias": [(C("d1"), -slope)], "sink": None, "lam": NLAM, "pv": pv}

    def dense_a():
        yield from proj_fm(both(mp, F), WK, 0, 1024, cp_act(F(mk)), tm2, DB)
        yield from proj_tm(both(mp, F), WK, 1024, 1024, cp_tm(xtm(xaq)), tm2, DB)
        AT.wait([PE.now()])
        yield from proj_fm(H, W1, 3072, 1024, cp_act(F(waq), 0.125), t_h, DB)
        yield from proj_dup(H, W1, 4096, 4, cp_act(wak), t_h, DB)
        yield from proj_tm(H, W1, 4352, 256, cp_tm(wav), t_h, DB)
        yield from proj_fm(H, W1, 4608, 1024, cp_act(F(xq2), 0.0625), t_h, DB)

    xq2 = B(1)
    par(attention(da_units(), tda, oda), dense_a(), 26, 39)
    twa = bar()

    def wa_units():
        for j in range(8):
            kv = j // 2
            slopes = [float(np.exp2(np.float32(-8.0) * np.float32(h + 1) / np.float32(16))) for h in (2 * j, 2 * j + 1)]
            yield {"scores": score_pair(lambda m, j=j: F(waq)[64 * m:64 * m + 64, j, :],
                                        lambda m, kv=kv: wak[64 * m:64 * m + 64, kv, :]),
                   "bias": [(C("d2"), -slopes[0]), (C("d2"), -slopes[1])], "sink": 2 * j, "lam": None,
                   "pv": pv_pair((lambda m, kt, kv=kv: wav[:, kt, kv * 64:kv * 64 + 64], F(waq)[:, j, :]))}

    def da_norm():
        sq = B(4)
        o16 = odt.rearrange("p (a e) -> p a e", e=P)
        t = AT.do(AC(sq, odt, ACT.Square), twa)
        r16 = SM2[:, 0:16]
        t = DV.do(RED(r16, sq.rearrange("p (a e) -> p a e", e=P), ALU.add), t)
        t = DV.do(TS(r16, r16, 1.0 / 128, 1e-6, ALU.mult, ALU.add), t)
        t = AT.do(AC(r16, r16, ACT.Sqrt), t)
        t = DV.do(RCP(r16, r16), t)
        t = DV.do(TT(o16, o16, r16.unsqueeze(2).broadcast_to((P, 16, P)), ALU.mult), t)
        return t

    t = da_norm()
    op = pr(3, 4)

    def oda_split(j, bk, t):
        hi, lo = (F(v)[:, 2 * j:2 * j + 2, :] for v in op)
        a = AT.do(AC(hi, bk, ACT.Copy, scale=SUBG), t)
        return [a, DV.do(STT(lo, bk, SUBG, f_(hi), ALU.mult, ALU.subtract), a)]
    to_fm(ODT, oda_split, DB, t)
    tod = bar()
    merged = B(5)

    def gate(n, dst):
        def ev(j, bk, t):
            return [AT.do(AC(F(dst)[:, 2 * j:2 * j + 2, :], bk, ACT.Sigmoid), t)]
        return proj_fm(H, W1, 5632 + n * 1024, 1024, ev, t_h, DB)

    def branch(o, wname, ready, G, add):
        def ev(j, bk, t):
            g, dst = (F(v)[:, 2 * j:2 * j + 2, :] for v in (G, merged))
            if not add:
                return [DV.do(TT(dst, bk, g, ALU.mult), t, AT.now())]
            q = DV.do(TT(g, bk, g, ALU.mult), t, AT.now())
            PO.do(TT(dst, dst, g, ALU.add), q)
            return [q]
        return proj_fm(o, A[wname], 0, 1024, ev, ready, DB)

    def dense_b():
        yield from gate(0, B(2))
        yield from branch(both(op, F), "w_da_o", tod, B(2), False)
        AT.wait([DV.now()])
        yield from gate(1, B(2))

    owa = []
    par(attention(wa_units(), twa, owa), dense_b(), 26, 25)
    txa = bar()
    wp2 = pr(3, 4)
    tsp = tuple(split(F(waq)[:, f, :], wp2, f, txa) for f in range(8))

    def xa_units():
        for h in range(0, 4, 2):
            def scores(m, qt, o, w, inc, h=h):
                for kk in range(2):
                    f = 2 * (h + m) + kk
                    t = PE.do(MM(o, F(xq2)[:, f, qt * P:(qt + 1) * P], F(mk)[:, f, :], kk == 0, kk == 1),
                              *(w if kk == 0 else ()), inc=inc and kk == 1)
                return t

            def pv(PT, tp, h=h):
                r = []
                for m in range(2):
                    b, w = OB.get()
                    for e in range(2):
                        for kt in range(2):
                            c = (h + m) * 256 + e * P
                            t = PE.do(MM(ps[:, b, e * T:(e + 1) * T], xtm(mvb)[:, kt, c:c + P], PT[:, m, kt, :],
                                         kt == 0, kt == 1), *((w, tp) if e + kt == 0 else ()), inc=e + kt == 2)
                    f = 2 * (h + m)
                    d = AT.do(AC(F(xq2)[:, f:f + 2, :], ps[:, b, :].rearrange("p (e t) -> p e t", t=T), ACT.Copy), t)
                    free_bank(b, d)
                    r += [t, d]
                return r
            yield {"scores": scores, "bias": None, "sink": None, "lam": None, "pv": pv}

    oxa = []

    def dense_c():
        yield from gate(2, B(7))
        yield from branch(both(wp2, F), "w_wa_o", tsp, B(2), True)
    par(attention(xa_units(), txa, oxa), dense_c(), 8, 17)
    txo = bar()
    xp2 = pr(6, 2)
    tsp = tuple(split(F(xq2)[:, f, :], xp2, f, txo) for f in range(8))
    run(branch(both(xp2, F), "w_xa_o", tsp, B(7), True))
    tmg = bar()
    mgp = pr(8, 9)
    tmg = tuple(split(F(merged)[:, f, :], mgp, f, tmg) for f in range(8))
    X = F(x)

    def resid(j, bk, t, scale=None):
        d = X[:, 2 * j:2 * j + 2, :]
        if scale is None:
            return [DV.do(TT(d, bk, d, ALU.add), t)]
        return [DV.do(STT(d, d, scale, bk, ALU.mult, ALU.add), t)]
    run(proj_fm(both(mgp, F), A["w_out"], 0, 1024, resid, tmg, KB))
    t1 = bar()

    def finish(src):
        SP.wait(bar())

        def go(e, src=src):
            e.dma_start(out, src).then_inc(out_sem, 16)
        SP.ops.append(go)

    def fin():
        return (PE, DV, AT, PO, SP), 16

    sd = [0, 0]

    def side(dst, src, *toks, g=0):
        PO.wait(toks)

        def go(e, dst=dst, src=src):
            e.dma_start(dst, src).then_inc(side_sem[g], 16)
        PO.ops.append(go)
        sd[g] += 16
        return ("side%d" % g, side_sem[g], sd[g])

    fence()
    tx4 = bar()
    for i in range(4, 11):
        slots.append(i)
        free_slot(i, *tx4)
    h2 = B(1)
    th = rms(x, B(9), h2, 1e-6, lambda f: V("ffn_norm_g", f), KB, t1)
    H2T = xtm(B(2))
    s, base, tl = load((lambda q: q[:, 0:128].rearrange("p (k n) -> p k n", k=8),
                        A["w_router"].rearrange("(k p) n -> p k n", p=P)))
    wr = base[:, 0:128].rearrange("p (k n) -> p k n", k=8)
    b, w = KB.get()
    for tt in range(2):
        for k in range(8):
            t = PE.do(MM(ps[:, b, tt * 16:tt * 16 + 16], F(h2)[:, k, tt * P:(tt + 1) * P], wr[:, k, :], k == 0, k == 7),
                      *((w, th, tl) if k + tt == 0 else ()), inc=k == 7)
    free_slot(s, t)
    trt = t
    tt_ = to_tm(F(h2), H2T, Banks([(b + i) % 8 for i in range(1, 5)]), th)
    t = trt
    lg = SM2[:, 0:32].rearrange("p (t e) -> p t e", t=2)
    lmax = SM2[:, 32:34]
    lsum = SM2[:, 34:36]
    l2 = SM2[:, 36:68].rearrange("p (t e) -> p t e", t=2)
    pb = ps[:, b, 0:32].rearrange("p (t e) -> p t e", t=2)
    t = DV.do(RED(lmax, pb, ALU.max, neg=True), t)
    t = DV.do(TT(lg, pb, lmax.unsqueeze(2).broadcast_to((P, 2, 16)), ALU.add), t)
    free_bank(b, t)
    t = AT.do(AC(l2, lg, ACT.Exp), t)
    t = DV.do(RED(lsum, l2, ALU.add), t)
    t = DV.do(RCP(lsum, lsum), t)
    t = DV.do(TT(lg, l2, lsum.unsqueeze(2).broadcast_to((P, 2, 16)), ALU.mult), t)
    taff = t
    b, w = KB.get()
    for tt in range(2):
        t = PE.do(TR(ps[0:16, b, tt * P:(tt + 1) * P], lg[:, tt, :], IDN), *((w, t) if tt == 0 else ()), inc=tt == 1)
    aff_, wk2, msk, pos = (B(9)[0:16, i * T:(i + 1) * T] for i in range(4))
    m8 = SM2[0:16, 72:80]
    t = DV.do(CP(aff_, ps[0:16, b, 0:T]), t)
    free_bank(b, t)
    cur, nxt = aff_, wk2
    for r in range(4):
        t = DV.do(lambda e, o=m8, i=cur: e.max(o, i), t)
        t = DV.do(lambda e, o=nxt, m=m8, i=cur: e.match_replace(o, m, i, -1.0), t)
        cur, nxt = nxt, cur
    t = DV.do(TS(msk, cur, 0.0, None, ALU.is_lt), t)
    t = DV.do(lambda e: e.memset(nxt, 1.0), t)
    t = DV.do(lambda e: e.tensor_tensor_scan(pos, nxt, msk, 0.0, ALU.mult, ALU.add), t)
    t = DV.do(TT(pos, pos, msk, ALU.mult), t)
    t = DV.do(TS(pos, pos, -1.0, None, ALU.add), t)
    b, w = KB.get()
    for tt in range(2):
        t = PE.do(TR(ps[:, b, tt * 16:tt * 16 + 16], pos[:, tt * P:(tt + 1) * P], IDN[0:16, 0:16]),
                  *((w, t) if tt == 0 else ()), inc=tt == 1)
    posT = l2.rearrange("p t e -> p (t e)")
    t = DV.do(CP(posT, ps[:, b, 0:32]), t)
    free_bank(b, t)
    OH = B(5)[:, 0:1024]
    GW = B(5)[:, 1024:2048]
    a32 = lambda v: v.rearrange("p (a j) -> p a j", j=32)
    t = DV.do(TT(a32(OH), posT.unsqueeze(2).broadcast_to((P, 32, 32)),
                 C("iota32").unsqueeze(1).broadcast_to((P, 32, 32)), ALU.is_equal), t)
    toh = t
    t = DV.do(TT(a32(GW), a32(OH), lg.rearrange("p t e -> p (t e)").unsqueeze(2).broadcast_to((P, 32, 32)), ALU.mult), t)
    tgw = t
    XE = B(3, 2).rearrange("p (d c) -> p d c", d=8)
    EB, TB, YB = Banks([0, 1, 2, 3]), Banks([4, 5]), Banks([6, 7])

    def gather(g):
        r = []
        for half in range(2):
            b, w = TB.get()
            for i in range(4):
                d = 4 * half + i
                for tt in range(2):
                    t = PE.do(MM(ps[:, b, i * P:(i + 1) * P], H2T[:, tt, d * P:(d + 1) * P],
                                 OH[:, tt * 512 + g * P:tt * 512 + (g + 1) * P], tt == 0, tt == 1),
                              w, tt_, toh, inc=i == 3 and tt == 1)
            o, v = XE[:, 4 * half:4 * half + 4, g * P:(g + 1) * P], ps[:, b, :].rearrange("p (i c) -> p i c", i=4)
            t = AT.do(AC(o, v, ACT.Copy), t) if half else DV.do(CP(o, v), t)
            free_bank(b, t)
            r.append(t)
        return r

    GT = B(7)[:, 0:1024].rearrange("p (g t) -> p g t", g=4)

    def weights_out():
        r = []
        for g2 in range(2):
            b, w = TB.get()
            for i in range(2):
                for tt in range(2):
                    g = 2 * g2 + i
                    t = PE.do(TR(ps[:, b, i * T + tt * P:i * T + (tt + 1) * P], GW[:, tt * 512 + g * P:tt * 512 + (g + 1) * P], IDN),
                              *((w, tgw) if i + tt == 0 else ()), inc=i + tt == 2)
            t = DV.do(CP(GT[:, 2 * g2:2 * g2 + 2, :], ps[:, b, :].rearrange("p (g t) -> p g t", g=2)), t)
            free_bank(b, t)
            r.append(t)
        return r
    txe = gather(0)
    YE = B(7)[:, 1024:2048]
    AT_ = B(6).rearrange("p (f c) -> p f c", f=16)
    afree = [[], []]
    tat = []
    tye = []
    for g in range(4):
        for q in range(4):
            ba, wa_ = EB.get()
            bu, wu = EB.get()
            for k in range(8):
                for n, bb in (("w_exp_gate", ba), ("w_exp_up", bu)):
                    s, base, tl = load((lambda s: k_(s, 4),
                                        A[n][4 * g:4 * g + 4, k * P:(k + 1) * P, q * 512:(q + 1) * 512].rearrange("e p n -> p e n")))
                    for e in range(4):
                        c = (4 * g + e) * 32
                        t = PE.do(MM(ps[32 * e:32 * e + 32, bb, :], XE[:, k, c:c + 32], k_(base, 4)[:, e, :], k == 0, k == 7),
                                  tl, txe, wa_, wu, inc=e == 3)
                    free_slot(s, t)
            S1 = tw[:, (q % 2) * 512:(q % 2 + 1) * 512]
            t1_ = AT.do(AC(S1, ps[:, ba, :], ACT.Silu), t, afree[q % 2])
            free_bank(ba, t1_)
            t = DV.do(TT(S1, S1, ps[:, bu, :], ALU.mult), t1_)
            free_bank(bu, t)
            b, w = TB.get()
            for i in range(4):
                t = PE.do(TR(ps[:, b, i * P:(i + 1) * P], S1[:, i * P:(i + 1) * P], IDN),
                          *((w, t) if i == 0 else ()), inc=i == 3)
            afree[q % 2] = [t]
            t = DV.do(CP(AT_[:, 4 * q:4 * q + 4, :], ps[:, b, :].rearrange("p (f c) -> p f c", f=4)), t)
            free_bank(b, t)
            tat = [t]
            if q == 0 and g == 0:
                tgt = weights_out()
            if q == 1 and g < 3:
                tnext = gather(g + 1)
        by = [YB.get() for _ in range(2)]
        for k in range(16):
            for c in range(2):
                s, base, tl = load((lambda s: k_(s, 4),
                                    A["w_exp_down"][4 * g:4 * g + 4, k * P:(k + 1) * P, c * 512:(c + 1) * 512].rearrange("e p n -> p e n")))
                for e in range(4):
                    t = PE.do(MM(ps[32 * e:32 * e + 32, by[c][0], :], AT_[:, k, 32 * e:32 * e + 32],
                                 k_(base, 4)[:, e, :], k == 0, k == 15),
                              tl, tat, by[0][1], by[1][1], inc=e == 3)
                free_slot(s, t)
        ty = [AT.do(AC(YE[:, 0:512], ps[:, by[0][0], :], ACT.Copy), t, tye),
              DV.do(CP(YE[:, 512:1024], ps[:, by[1][0], :]), t, tye)]
        free_bank(by[0][0], ty[0])
        free_bank(by[1][0], ty[1])
        for j in range(4):
            b, w = TB.get()
            for i in range(2):
                d = 2 * j + i
                t = PE.do(MM(ps[:, b, i * T:(i + 1) * T], YE[:, d * P:(d + 1) * P], GT[:, g, :], True, True),
                          *((w, ty, tgt) if i == 0 else ()), inc=i == 1)
            free_bank(b, *resid(j, ps[:, b, :].rearrange("p (i t) -> p i t", t=T), t))
        tye = [t]
        txe = tnext
    del slots[4:]
    tx4 = bar()
    wfree[0], wfree[1] = [tx4, tx4], [tx4, tx4]
    fence()
    xb = B(1)
    tx = rms(x, B(9), xb, 1e-6, lambda f: V("final_norm_g", f), KB, bar())
    x = xb
    X = F(x)

    for l in range(2):
        src, nkv = (A["w_in_a_2"], 2) if l == 0 else (A["w_in_b_2"], 4)
        tn = tuple(rms(x, B(9), B(2), 1e-5, lambda f, l=l: V("norm_g_2", 8 * l + f), KB, tx, bar(), pair=XP, pair_w=bar()))
        HN = H
        qb, kvb, zb = B(3), B(5), B(6)
        kd = F(kvb[:, 0:128 * 2 * nkv], nkv)
        vt = kvb[:, 1024:1024 + 2 * 64 * nkv].rearrange("p (t n) -> p t n", t=2)
        RB = Banks([4, 5])

        def rope(dst, j, ready, *toks):
            d = dst[:, 2 * j:2 * j + 2, :]
            b, w = RB.get()
            t = PE.do(MM(ps[:, b, :], C("rot"), d, True, True), w, *toks)
            tmp = tw[:, (j % 2) * 512:(j % 2 + 1) * 512].rearrange("p (i t) -> p i t", t=T)
            cs = C("cos").unsqueeze(1).broadcast_to((P, 2, T))
            sn = C("sin").unsqueeze(1).broadcast_to((P, 2, T))
            ta = DV.do(TT(tmp, ps[:, b, :].rearrange("p (i t) -> p i t", t=T), sn, ALU.mult), t)
            free_bank(b, ta)
            t = DV.do(TT(d, d, cs, ALU.mult), t)
            ready.append(DV.do(TT(d, d, tmp, ALU.add), t, ta))

        kr, qr, qtok = [], [], []

        def dense_q(j0, j1):
            for j in range(j0, j1):
                def ev(_, bk, t, j=j):
                    qtok.append(cp_act(F(qb), 0.125)(j, bk, t))
                    return qtok[j]
                yield from proj_fm(HN, src, 256 * j, 256, ev, tn, DB)
                if j >= 1:
                    rope(F(qb), j - 1, qr, qtok[j - 1])
                    yield
        run(proj_dup(HN, src, 1024, nkv, cp_act(kd), tn, DB))
        run(proj_tm(HN, src, 1024 + 64 * nkv, 64 * nkv, cp_tm(vt), tn, DB))
        for j in range(nkv // 2):
            rope(kd, j, kr, AT.now())
        run(dense_q(0, 2))
        trope = [kr, bar()]

        def units():
            for j in range(8):
                kv_ = 2 * j // (16 // nkv)
                yield {"ready": qr[j // 2], "scores": score_pair(lambda m, j=j: F(qb)[64 * m:64 * m + 64, j, :],
                                            lambda m, kv_=kv_: kd[64 * m:64 * m + 64, kv_, :]),
                       "bias": [(C("ma") if l == 0 else C("mb"), 1.0)], "sink": 16 + 2 * j if l == 0 else None,
                       "lam": None,
                       "pv": pv_pair((lambda m, kt, kv_=kv_: vt[:, kt, kv_ * 64:kv_ * 64 + 64], F(qb)[:, j, :]))}

        def silu_z(j, bk, t):
            return [AT.do(AC(F(zb)[:, 2 * j:2 * j + 2, :], bk, ACT.Silu), t)]

        def dense_z():
            yield from dense_q(2, 4)
            rope(F(qb), 3, qr, qtok[3])
            yield
            yield from proj_fm(HN, src, 1024 + 128 * nkv, 1024, silu_z, tn, DB)
        par(attention(units(), trope, []), dense_z(), 26, 16)
        tb = bar()
        tz = []
        zp = pr(7, 8)
        for f in range(8):
            q_ = F(qb)[:, f, :]
            t = DV.do(TT(q_, q_, F(zb)[:, f, :], ALU.mult), tb)
            tz.append(split(q_, zp, f, t))
        run(proj_fm(both(zp, F), A["w_out_2"][l], 0, 1024, resid, tuple(tz), KB))
        tx = bar()
    x3 = B(0)
    tx = rms(x, B(9), x3, 1e-5, lambda f: V("final_g_2", f), KB, tx, pair=XP, pair_w=bar())
    x = x3
    X = F(x)
    side(xw[:, 0:sum(CT[n] for n in LATE)], A["consts2"], bar())
    TMP, Y = B(1), B(2)
    FB, QB = Banks([0, 1, 2, 3]), Banks([4, 5, 6, 7])
    ALPHA = float((2 * 2) ** 0.25)

    ytok = [None] * 4

    def ynew(scale):
        def f(j, bk, t):
            ytok[j] = DV.do(STT(F(Y)[:, 2 * j:2 * j + 2, :], X[:, 2 * j:2 * j + 2, :], scale, bk, ALU.mult, ALU.add), t)
            return [ytok[j]]
        return f

    def norm3(l, i, eps, pair=XP):
        return ln(Y, TMP, x, eps, lambda f: V("ln_g_3", (3 * l + i) * 8 + f), lambda f: V("ln_b_3", (3 * l + i) * 8 + f),
                  FB, list(ytok), pair)

    def ffn(l, idx, ready):
        ready = tuple(ready)
        src = A["ffn_w_in_3"][l, idx]
        ap_ = (unit_r(18, 6)[:, 0:22 * T], unit_r(24, 6)[:, 0:22 * T])
        act = both(ap_, lambda v: F(v, 22))
        tfree = [[] for _ in range(4)]
        tst = bar()
        ta = []
        for c in range(11):
            G = tw[:, (c % 4) * 512:(c % 4 + 1) * 512].rearrange("p (i t) -> p i t", t=T)
            tk = []

            def ev0(bk, t):
                tk.append(AT.do(AC(G, bk, ACT.Silu), t, tfree[c % 4]))
                return tk

            def ev1(bk, t):
                d = DV.do(TT(G, G, bk, ALU.mult), t, tk)
                hi, lo = (v[:, 2 * c:2 * c + 2, :] for v in act)
                a = AT.do(AC(hi, G, ACT.Copy), d, tst)
                tfree[c % 4] = [a, DV.do(TT(lo, G, f_(hi), ALU.subtract), a)]
                ta.extend([tfree[c % 4]] * 2)
                return [d]
            for i, ev in enumerate((ev0, ev1)):
                run(fm(H, split_load(2048, wk(src, i * 2816 + c * 256)), ev, ready, FB))
        run(acc_fm(act, 22, A["ffn_w_out_3"][l, idx], ynew(2 * ALPHA), tuple(ta), QB))

    def sgu(ready):
        ready = tuple(ready)
        tb = bar()
        VB, UB = B(5, 2), B(3, 2)
        U_, Vt = F(UB, 16), VB.rearrange("p (t n) -> p t n", t=2)
        side(B(7), A["b_in_v"].partition_broadcast(P), tb)
        side(B(8), A["sgu_ln_g_3"].partition_broadcast(P))
        ts_ = side(B(9), A["sgu_ln_b_3"].partition_broadcast(P))
        side(B(1), A["spT"], g=1)
        tl = side(B(2), A["b_sp"].partition_broadcast(P), g=1)
        sp, bs = (B(i).rearrange("p (g t) -> p g t", g=16) for i in (1, 2))
        tm = PO.do(lambda e: e.affine_select(out=sp, in_=sp, compare_op=ALU.is_ge, fill=0.0, base=0,
                                             pattern=[[0, 16], [1, P]], channel_multiplier=-1), tl)

        def ev_v(c, bk, t):
            d = Vt[:, :, c:c + 256]
            t = DV.do(TT(d, bk, B(7)[:, c:c + 256].unsqueeze(1).broadcast_to((P, 2, 256)), ALU.add), t, ts_)
            AT.do(AC(d, d, ACT.Gelu), t)
            return [t]

        def ev_u(j, bk, t):
            for i in range(2):
                r = AT.do(AC(U_[:, 2 * j + i, :], bk[:, i, :], ACT.Gelu, bias=V("sgu_b_in_3", 2 * j + i)), t)
            utok.append(r)
            return [r]
        run(proj_tm(H, A["sgu_w_in_3"], 2048, 2048, ev_v, ready, FB))
        tv = bar()
        stt = SM2[:, 0:48].rearrange("p (t c s) -> p t c s", t=2, c=4)
        mvv = SM2[:, 48:52].rearrange("p (t c) -> p t c", t=2)
        rs = SM2[:, 52:54]
        vdone = []

        def v_norm():
            t = tv
            for tt in range(2):
                for c in range(4):
                    t = DV.do(lambda e, o=stt[:, tt, c, :], i=Vt[:, tt, c * 512:(c + 1) * 512]: e.bn_stats(o, i), tv)
                t = DV.do(lambda e, o=mvv[:, tt, :], i=stt[:, tt, :, :]: e.bn_aggr(o, i), t)
                yield
            t = DV.do(TS(rs, mvv[:, :, 1], 1e-5, None, ALU.add), t)
            t = AT.do(AC(rs, rs, ACT.Sqrt), t)
            yield
            t = DV.do(RCP(rs, rs), t)
            for tt in range(2):
                for c in range(2):
                    q = slice(c * 1024, c * 1024 + 1024)
                    d = Vt[:, tt, q]
                    a = DV.do(TS(d, d, mvv[:, tt, 0:1], rs[:, tt:tt + 1], ALU.subtract, ALU.mult), t)
                    a = DV.do(TT(d, d, B(8)[:, q], ALU.mult), a)
                    vdone.append(DV.do(TT(d, d, B(9)[:, q], ALU.add), a))
                    yield

        uh, ul = F(R(7, 2), 16), F(R(3, 2), 16)
        fr = [[], []]
        r = []
        utok = []

        def spatial(j):
            b, w = FB.get()
            for i in range(2):
                for c in range(2):
                    g = 2 * j + i
                    t = PE.do(MM(ps[:, b, i * T + c * P:i * T + (c + 1) * P], Vt[:, c, g * P:(g + 1) * P], sp[:, g, :], True, True),
                              *((w, vdone, tm) if i + c == 0 else ()), inc=i + c == 2)
            tmp = tw[:, (j % 2) * 512:(j % 2 + 1) * 512].rearrange("p (i c t) -> p i c t", i=2, c=2)
            t = DV.do(TT(tmp, ps[:, b, :].rearrange("p (i c t) -> p i c t", i=2, c=2),
                         bs[:, 2 * j:2 * j + 2, :].unsqueeze(2).broadcast_to((P, 2, 2, P)), ALU.add), t, tl, fr[j % 2])
            free_bank(b, t)
            g_ = tmp.rearrange("p i c t -> p i (c t)")
            t = DV.do(TT(g_, U_[:, 2 * j:2 * j + 2, :], g_, ALU.mult), t, utok[j])
            a = AT.do(AC(uh[:, 2 * j:2 * j + 2, :], g_, ACT.Copy), t, vdone)
            fr[j % 2] = [a, DV.do(TT(ul[:, 2 * j:2 * j + 2, :], g_, f_(uh[:, 2 * j:2 * j + 2, :]), ALU.subtract), a)]
            r.extend([fr[j % 2]] * 2)

        def dense_u():
            n = 0
            for _ in proj_fm(H, A["sgu_w_in_3"], 0, 2048, ev_u, ready, FB):
                n += 1
                if n > 8:
                    spatial(n - 9)
                yield
        par(dense_u(), v_norm(), 17, 16)
        run(acc_fm((uh, ul), 16, A["sgu_w_out_3"], ynew(ALPHA), tuple(r), QB))

    ffn(0, 0, tx)
    tx = norm3(0, 0, 4e-5)
    sgu(tx)
    tx = norm3(0, 1, 1e-5)
    ffn(0, 1, tx)
    tx = norm3(0, 2, 4e-5)
    ffn(1, 0, tx)
    norm3(1, 0, 4e-5, None)
    def rwkv():
        t0 = bar()
        S0, S1, S2_, S3 = (unit_f(u, 2) for u in (0, 2, 4, 6))
        DT = cst[:, NFIRST:NFIRST + BIG]
        XX = B(1)
        R_, K_, SG, A_, G_, VV = B(3), B(4), B(5), B(6), B(7), B(8)
        ta = DV.do(TT(F(XX)[:, :, 1:T], X[:, :, 0:T - 1], X[:, :, 1:T], ALU.subtract), t0)
        tb = DV.do(TS(F(XX)[:, :, 0:1], X[:, :, 0:1], -1.0, None, ALU.mult), t0)
        txx = [ta, tb]
        PA, PB = pr(5, 6), pr(7, 9)

        def mixed(m, d, w, pair=None):
            def first(f):
                t = DV.do(STT(F(d)[:, f, :], F(XX)[:, f, :], V("rwkv_mu_3", 8 * m + f), X[:, f, :], ALU.mult, ALU.add),
                          txx, w)
                return (t, AT.do(AC(F(pair[0])[:, f, :], F(d)[:, f, :], ACT.Copy), t, w)) if pair else t

            def second(f, t):
                if not pair:
                    return t
                hi, lo = (F(v)[:, f, :] for v in pair)
                return [t[1], DV.do(TT(lo, F(d)[:, f, :], f_(hi), ALU.subtract), *t)]
            return tuple(staged(8, first, second))

        def lora(xm, t, wv, tl, n, func, dst):
            b, w = FB.get()
            for k in range(8):
                t = PE.do(MM(ps[0:n, b, 0:T], wv[:, k, :], xm[:, k, :], k == 0, k == 7),
                          *((w, t, tl) if k == 0 else ()), inc=k == 7)
            q = AT.do(AC(dst, ps[0:n, b, 0:T], func), t)
            free_bank(b, q)
            return t, q

        m2 = mixed(2, B(2), t0, XP)
        gv = proj_tm(H, A["rwkv_w_rkv_3"][2], 0, 1024, cp_tm(xtm(VV)), m2, FB)
        next(gv)
        m0 = mixed(0, B(4), t0, PA)
        run(gv)
        pv_done = bar()
        gr = proj_fm(both(PA, F), A["rwkv_w_rkv_3"][0], 0, 1024, cp_act(F(R_)), m0, FB)
        next(gr)
        m1 = mixed(1, B(2), pv_done, PB)
        run(gr)
        run(proj_fm(both(PB, F), A["rwkv_w_rkv_3"][1], 0, 1024, cp_act(F(K_)), m1, FB))
        tdn = bar()
        kv_ = lambda n: A[n].rearrange("(k p) n -> p k n", p=P)
        s1, b1, tl1 = load((lambda q: k_(q[:, 0:512]), kv_("rwkv_w1_3")), (lambda q: k_(q[:, 512:1024]), kv_("rwkv_a1_3")))
        s3, b3_, tl3 = load((lambda q: k_(q[:, 0:1280]), kv_("rwkv_g1_3")))
        s2, b2, tl2 = load((lambda q: q[0:64, 0:1024], A["rwkv_w2_3"]), (lambda q: q[0:64, 1024:2048], A["rwkv_a2_3"]))
        s4, b4, tl4 = load((lambda q: q[:, 0:1024], A["rwkv_g2_3"][0:P, :]), (lambda q: q[0:32, 1024:2048], A["rwkv_g2_3"][P:160, :]))
        fence()
        k8 = lambda v: v.rearrange("p (k n) -> p k n", k=8)
        z1, z2 = tw[0:64, 0:T], tw[0:64, T:2 * T]
        z3, z4 = tw[:, 2 * T:3 * T], tw[0:32, 3 * T:4 * T]

        def second(parts, j):
            b, w = FB.get()
            for i in range(2):
                f = 2 * j + i
                for n, (wv, z, t) in enumerate(parts):
                    t = PE.do(MM(ps[:, b, i * T:(i + 1) * T], wv[:, f * P:(f + 1) * P], z, n == 0, n == len(parts) - 1),
                              w, t, tl2, tl4, inc=n == len(parts) - 1)
            return b, t
        tside = [("side0", side_sem[0], sd[0])]
        KK, BV = B(2), B(9)
        sel = C("sel").rearrange("p (f h) -> p f h", f=8)
        selt = C("selt").rearrange("p (f m) -> p f m", f=8)

        def first_of(m, d, w, wv, z, func):
            xm = mixed(m, d, w)
            return lora(F(d), list(xm), k8(wv), tl1, 64, func, z)

        def second_of(w2, z, t, bias, dst):
            for j in range(4):
                b, t2 = second([(w2, z, t)], j)
                for i in range(2):
                    r = AT.do(AC(F(dst)[:, 2 * j + i, :], ps[:, b, i * T:(i + 1) * T], ACT.Sigmoid, bias=V(bias, 2 * j + i)), t2)
                free_bank(b, r)
            return r
        p3, t3_ = first_of(3, S0, tdn, b1[:, 0:512], z1, ACT.Tanh)
        p4, t4_ = first_of(4, S3, tdn, b1[:, 512:1024], z2, ACT.Copy)
        tsg = second_of(b2[0:64, 0:1024], z1, t3_, "rwkv_w0_3", SG)
        tas = second_of(b2[0:64, 1024:2048], z2, t4_, "rwkv_a0_3", A_)
        for f in range(8):
            t = DV.do(TS(F(KK)[:, f, :], F(K_)[:, f, :], V("rwkv_k_k_3", f), None, ALU.mult), tdn)
        t = AT.do(AC(BV, KK, ACT.Square), t, tdn)
        xm5 = list(mixed(5, S0, [p3]))
        b, w = FB.get()
        for f in range(8):
            t = PE.do(MM(ps[0:16, b, 0:T], sel[:, f, :], F(BV)[:, f, :], f == 0, f == 7), w, t, tside, inc=f == 7)
        tsq = t
        n16 = SM2[0:16, 0:T]
        t = AT.do(AC(n16, ps[0:16, b, 0:T], ACT.Sqrt), t)
        free_bank(b, t)
        t = DV.do(TS(n16, n16, 1e-12, None, ALU.max), t)
        tn16 = DV.do(RCP(n16, n16), t)
        for f in range(8):
            t2 = DV.do(lambda e, o=F(S1)[:, f, :], i=F(SG)[:, f, :]: e.tensor_tensor_scan(o, C("reset"), i, 0.0, ALU.mult, ALU.add),
                       tsg, tdn, tside)
        g1 = k8(b3_[:, 0:1280])
        tp, ta = lora(F(S0), xm5, g1[:, :, 0:P], tl3, P, ACT.Sigmoid, z3)
        tp, tb = lora(F(S0), xm5, g1[:, :, P:160], tl3, 32, ACT.Sigmoid, z4)
        tk = []
        for j in range(4):
            b, w = FB.get()
            for i in range(2):
                t = PE.do(MM(ps[:, b, i * T:(i + 1) * T], selt[0:16, 2 * j + i, :], n16, True, True), w, tn16, inc=i == 1)
            d = F(KK)[:, 2 * j:2 * j + 2, :]
            t = DV.do(TT(d, d, ps[:, b, :].rearrange("p (i t) -> p i t", t=T), ALU.mult), t)
            free_bank(b, t)
            tk.append(t)
        for j in range(4):
            b, t = second([(b4[:, 0:1024], z3, ta), (b4[0:32, 1024:2048], z4, tb)], j)
            r = AT.do(AC(F(G_)[:, 2 * j:2 * j + 2, :], ps[:, b, :].rearrange("p (i t) -> p i t", t=T), ACT.Copy), t)
            free_bank(b, r)
        free_slot(s1, PE.now())
        for s_ in (s2, s3, s4):
            free_slot(s_, PE.now())
        t = DV.do(TT(BV, KK, A_, ALU.mult), tk, tsq, tas)
        for f in range(8):
            t = DV.do(TS(F(A_)[:, f, :], F(A_)[:, f, :], -1.0, V("rwkv_k_a_3", f), ALU.add, ALU.mult), t)
        tK = DV.do(STT(K_, A_, 1.0, K_, ALU.add, ALU.mult), t)
        for f in range(8):
            t = DV.do(STT(F(S0)[:, f, :], F(R_)[:, f, :], V("rwkv_r_k_3", f), F(K_)[:, f, :], ALU.mult, ALU.mult), tK, tp)
        b, w = FB.get()
        for tt in range(2):
            for f in range(8):
                t = PE.do(MM(ps[:, b, tt * 16:tt * 16 + 16], F(S0)[:, f, tt * P:(tt + 1) * P], sel[:, f, :], f == 0, f == 7),
                          w, t, inc=f == 7)
        BON = RSTD[:, 0:32]
        BON_t = DV.do(CP(BON, ps[:, b, 0:32]), t)
        free_bank(b, BON_t)
        cd = -float(np.exp(-0.5))
        t = DV.do(TT(SG, S1, SG, ALU.subtract), t2)
        c = AT.do(AC(S2_, S1, ACT.Exp, scale=-cd), t2)
        a = AT.do(AC(SG, SG, ACT.Exp, scale=cd), t)
        e_ = AT.do(AC(S1, S1, ACT.Exp, scale=cd), t)
        t2 = DV.do(TT(BV, BV, S2_, ALU.mult), c)
        t3 = DV.do(TT(K_, K_, S2_, ALU.mult), c, tK)
        t1 = DV.do(STT(KK, KK, -1.0, SG, ALU.mult, ALU.mult), a)
        t4 = DV.do(TT(R_, R_, S1, ALU.mult), e_)
        PC = RSTD[:, 32:64].rearrange("p (f c) -> p f c", f=8)
        t5 = DV.do(CP(PC, S1.rearrange("p (f c t) -> p f c t", f=8, c=4)[:, :, :, 63]), e_)
        tall = [t1, t2, t3, t4, t5]
        AT_m, BT_m, KT_m = xtm(S0), xtm(S1), xtm(S2_)
        ttm = to_tm(F(KK), AT_m, QB, tall) + to_tm(F(BV), BT_m, QB, tall) + to_tm(F(K_), KT_m, QB, tall)

        def v4(m):
            return m.rearrange("p (t h i s) -> p t h i s", t=2, h=2, i=8)

        def pairs(left, right, mask, dst, banks):
            for tt in range(2):
                for par_ in range(2):
                    b, w = banks.get()
                    for i in range(8):
                        for cp in range(2):
                            c0 = tt * P + cp * 64
                            rows = slice(64 * par_, 64 * par_ + 64)
                            t = PE.do(MM(ps[64 * cp:64 * cp + 64, b, i * 64:(i + 1) * 64], F(left)[rows, i, c0:c0 + 64],
                                         F(right)[rows, i, c0:c0 + 64], True, True),
                                      w, tall, inc=(i == 7 and cp == 1))
                    o = v4(dst)[:, tt, par_, :, :]
                    t = DV.do(TT(o, ps[:, b, :].rearrange("p (i s) -> p i s", i=8),
                                 C(mask).unsqueeze(1).broadcast_to((P, 8, 64)), ALU.mult), t, pairs_w)
                    free_bank(b, t)
            return t
        pairs_w = bar()
        N_, NT, A2T, RBT, RKT = S3, DT, B(1), B(5), B(6)
        pairs(KK, BV, "low", N_, FB)
        pairs(BV, KK, "upp", NT, FB)
        pairs(K_, KK, "upp", A2T, KB)
        pairs(K_, R_, "uppi", RKT, KB)
        tp = PE.now()
        T_, G, XS = B(2), B(4), B(9)
        bc = lambda n: C(n).unsqueeze(1).broadcast_to((P, 32, 64))
        m3 = lambda v: v.rearrange("p (a s) -> p a s", s=64)
        NM = tw
        t = DV.do(TT(m3(T_), m3(N_), bc("ml0"), ALU.mult), tp, ttm)
        t2 = DV.do(TT(m3(G), m3(NT), bc("mu0"), ALU.mult), tp, ttm)
        tn = DV.do(TT(m3(NM[:, :]), m3(NT), bc("mu1"), ALU.mult), tp)
        tT = [DV.do(TT(m3(T_), m3(T_), bc("eye64"), ALU.add), t)] * 4
        tG = [DV.do(TT(m3(G), m3(G), bc("eye64"), ALU.add), t2)] * 4
        pairs(BV, R_, "uppi", RBT, KB)
        gread = PE.now()

        def blk(left, right, banks, fn, *toks, q=None):
            r = []
            for tt in range(2):
                for h in range(2):
                    b, w = banks.get()
                    for i in range(8):
                        for cp in range(2):
                            rows = slice(64 * cp, 64 * cp + 64)
                            t = PE.do(MM(ps[rows, b, i * 64:(i + 1) * 64], left(tt, h, i)[rows, :], right(tt, h, i)[rows, :], True, True),
                                      w, *toks, q(tt, h) if q else [], inc=(i == 7 and cp == 1))
                    t = fn(tt, h, ps[:, b, :].rearrange("p (i s) -> p i s", i=8), t)
                    free_bank(b, t)
                    r.append(t)
            return r

        def at4(m):
            return lambda tt, h, i: v4(m)[:, tt, h, i, :]

        def vat(m):
            return lambda tt, h, i: m[:, tt, (2 * i + h) * 64:(2 * i + h) * 64 + 64]
        def of(*lists):
            return lambda tt, h: [v[2 * tt + h] for v in lists]
        for lev in range(1, 6):
            tX = blk(at4(NM), at4(T_), KB,
                     lambda tt, h, bk, t: AT.do(AC(v4(XS)[:, tt, h, :, :], bk, ACT.Copy), t, gread), tn, q=of(tT))
            nmdone = PE.now()
            if lev < 5:
                tn = DV.do(TT(m3(NM[:, :]), m3(NT), bc("mu%d" % (lev + 1)), ALU.mult), nmdone)

            def add_to(m, *toks):
                def f(tt, h, bk, t):
                    o = v4(m)[:, tt, h, :, :]
                    return DV.do(TT(o, o, bk, ALU.add), t, *toks)
                return f
            if lev < 5:
                tT = blk(at4(G), at4(XS), KB, add_to(T_, nmdone), q=of(tG, tX))
            tG = blk(at4(XS), at4(G), KB, add_to(G), q=of(tG, tX))
            gread = PE.now()
        tgn = side(tw[:, 0:1024], A["rwkv_gn_g_3"].partition_broadcast(P), nmdone, g=1)
        tgn = side(tw[:, 1024:2048], A["rwkv_gn_b_3"].partition_broadcast(P), g=1)
        tinv = [nmdone]
        W1 = S3.rearrange("p (i c t) -> p i c t", i=8, c=4)
        tw1 = []
        for c in range(4):
            tt, cp = c // 2, c % 2
            b, w = QB.get()
            rows = slice(64 * cp, 64 * cp + 64)
            for i in range(8):
                for h in range(2):
                    t = PE.do(MM(ps[64 * h:64 * h + 64, b, i * 64:(i + 1) * 64], vat(AT_m)(tt, h, i)[rows, :], at4(G)(tt, h, i)[rows, :], True, True),
                              w, tG[2 * tt], tG[2 * tt + 1], inc=(i == 7 and h == 1))
            t = AT.do(AC(W1[:, :, c, :], ps[:, b, :].rearrange("p (i t) -> p i t", i=8), ACT.Copy), t, tinv)
            free_bank(b, t)
            tw1.append(t)
        Vm = xtm(VV)
        Z, W2, YI = B(9), B(2), DT
        tz = blk(at4(A2T), vat(Vm), FB, lambda tt, h, bk, t: AT.do(AC(v4(Z)[:, tt, h, :, :], bk, ACT.Copy), t, gread))
        tyi = blk(at4(RKT), vat(Vm), FB, lambda tt, h, bk, t: AT.do(AC(v4(YI)[:, tt, h, :, :], bk, ACT.Copy), t, tn))
        tw2 = blk(at4(G), at4(Z), QB, lambda tt, h, bk, t: DV.do(CP(v4(W2)[:, tt, h, :, :], bk), t, tinv), q=of(tz, tG))
        tz_read = PE.now()
        ST_ = ptw[:, 0:512].rearrange("p (i v) -> p i v", i=8)
        SX = ptw[:, 512:1024].rearrange("p (i v) -> p i v", i=8)
        Us = B(1)[:, 0:1024].rearrange("p (h i v) -> p h i v", h=2, i=8)
        ts = DV.do(lambda e: e.memset(ptw[:, 0:512], 0.0))
        SQ, YN, VB = Z, B(4), B(6)
        st, sv = SM2[:, 0:32], SM2[:, 32:64]
        gg = tw[:, 0:1024].rearrange("p (i h v) -> p i h v", i=8, h=2)
        gb = tw[:, 1024:2048].unsqueeze(1).broadcast_to((P, 2, 1024))
        vb = PO.do(TT(m3(VB), m3(VV), BON.unsqueeze(2).broadcast_to((P, 32, 64)), ALU.mult), tz_read, BON_t)
        vb = PO.do(TT(xtm(VB), xtm(VB), gb, ALU.add), vb, tgn)

        def group_norm(tt, *toks):
            half = slice(tt * 1024, tt * 1024 + 1024)
            y3 = YI[:, half].rearrange("p (a s) -> p a s", s=64)
            z3_ = SQ[:, half].rearrange("p (a s) -> p a s", s=64)
            s_, v_ = st[:, 16 * tt:16 * tt + 16], sv[:, 16 * tt:16 * tt + 16]
            t = DV.do(RED(s_, y3, ALU.add), *toks)
            t = DV.do(TS(s_, s_, 1.0 / 64, None, ALU.mult), t)
            t = DV.do(TT(y3, y3, s_.unsqueeze(2).broadcast_to((P, 16, 64)), ALU.subtract), t)
            t = AT.do(AC(SQ[:, half], YI[:, half], ACT.Square), t, tz_read)
            yield
            t = DV.do(RED(v_, z3_, ALU.add), t)
            t = DV.do(TS(v_, v_, 1.0 / 64, 64e-5, ALU.mult, ALU.add), t)
            t = AT.do(AC(v_, v_, ACT.Sqrt), t)
            yield
            t = DV.do(RCP(v_, v_), t)
            t = DV.do(TT(y3, y3, v_.unsqueeze(2).broadcast_to((P, 16, 64)), ALU.mult), t)
            yield
            yn = YN[:, half].rearrange("p (i h v) -> p i h v", i=8, h=2)
            r = [DV.do(TT(yn[:, :, h, :], v4(YI)[:, tt, h, :, :], gg[:, :, h, :], ALU.mult), t, tgn, tz_read) for h in range(2)]
            yield
            tgn_done.append(DV.do(TT(YN[:, half], YN[:, half], VB[:, half], ALU.add), r, vb))
        tgn_done = []
        side_work = None
        tw_all = tw1 + tw2 + tyi
        b3 = lambda b, rows: ps[rows, b, :].rearrange("p (i v) -> p i v", i=8)
        for c in range(4):
            tt, cp = c // 2, c % 2
            rows = slice(64 * cp, 64 * cp + 64)
            tu, ty = [], []
            for h in range(2):
                hr = slice(64 * h, 64 * h + 64)
                w = bank_rel[h]
                for i in range(8):
                    t = PE.do(MM(ps[rows, h, i * 64:(i + 1) * 64], W1[hr, i, c, :], ST_[hr, i, :], True, True),
                              w, ts, tw_all, inc=i == 7)
                t = DV.do(TT(Us[rows, h, :, :], b3(h, rows), v4(W2)[rows, tt, h, :, :], ALU.add), t)
                free_bank(h, t)
                tu.append(t)
            for h in range(2):
                hr = slice(64 * h, 64 * h + 64)
                w = bank_rel[2 + h]
                for i in range(8):
                    t = PE.do(MM(ps[rows, 2 + h, i * 64:(i + 1) * 64], F(R_)[hr, i, c * 64:(c + 1) * 64], ST_[hr, i, :], True, True),
                              w, ts, inc=i == 7)
                ty.append(t)
            w = bank_rel[6]
            for i in range(8):
                for h in range(2):
                    hr = slice(64 * h, 64 * h + 64)
                    o = ps[hr, 6, i * 64:(i + 1) * 64]
                    PE.do(MM(o, vat(KT_m)(tt, h, i)[rows, :], vat(Vm)(tt, h, i)[rows, :], True, False), w, inc=False)
                    t = PE.do(MM(o, vat(BT_m)(tt, h, i)[rows, :], Us[rows, h, i, :], False, True), tu, inc=(i == 7 and h == 1))
            tsx = DV.do(TT(SX, ST_, ps[:, 6, :].rearrange("p (i v) -> p i v", i=8), ALU.add), t)
            free_bank(6, tsx)
            ts = DV.do(TT(ST_, SX, PC[:, :, c:c + 1].broadcast_to((P, 8, 64)), ALU.mult), tsx, ty)
            for h in range(2):
                w = bank_rel[4 + h]
                for i in range(8):
                    t = PE.do(MM(ps[rows, 4 + h, i * 64:(i + 1) * 64], at4(RBT)(tt, h, i)[rows, :], Us[rows, h, i, :], True, True),
                              w, tu, inc=i == 7)
                y = v4(YI)[rows, tt, h, :, :]
                a = DV.do(TT(y, y, b3(2 + h, rows), ALU.add), ty[h])
                free_bank(2 + h, a)
                a = DV.do(TT(y, y, b3(4 + h, rows), ALU.add), t, a)
                free_bank(4 + h, a)
                if side_work:
                    next(side_work, None)
            if c == 1:
                side_work = group_norm(0, a)
        run(side_work)
        run(group_norm(1, a))
        r = []

        def gated(j, bk, t):
            t = DV.do(TT(F(R_)[:, 2 * j:2 * j + 2, :], bk, F(G_)[:, 2 * j:2 * j + 2, :], ALU.mult), t)
            q = split(F(R_)[:, 2 * j:2 * j + 2, :], XP, slice(2 * j, 2 * j + 2), t)
            r.extend([q, q])
            return [t]
        tw0 = bar()
        wfree[0], wfree[1] = [tw0, tw0], [tw0, tw0]
        to_fm(xtm(YN), gated, QB, tgn_done)
        run(proj_fm(H, A["rwkv_w_o_3"], 0, 1024, ynew(ALPHA), tuple(r), FB))

    rwkv()
    tx = norm3(1, 1, 1e-5)
    ffn(1, 1, tx)
    norm3(1, 2, 4e-5, None)
    finish(x)
    return fin()


def kernel(**inputs):
    import concourse.bacc as _bacc
    from concourse.bass_utils import run_bass_kernel_spmd as _run

    I = {n: np.asarray(a) for n, a in inputs.items()}
    nc = _bacc.Bacc("TRN2", target_bir_lowering=False, num_devices=1)
    arrays, A = {}, {}

    def give(name, a):
        a = np.ascontiguousarray(a)
        arrays["in_" + name] = a
        A[name] = nc.dram_tensor("in_" + name, a.shape, mybir.dt.from_np(a.dtype), kind="ExternalInput").ap()

    def fmaj(a):
        return a.reshape(T, 8, P).transpose(2, 1, 0).reshape(P, 8 * T)

    give("xT", fmaj(I["x"]))
    give("memT", fmaj(I["mem"]))
    tabs = const_tables()
    give("consts", np.concatenate([tabs[n] for n in EARLY], axis=1))
    give("consts2", np.concatenate([tabs[n] for n in LATE], axis=1))
    give("vecs", np.concatenate([I[n].reshape(-1, P).T for n in list(VEC)], axis=1))
    for n in ("wa_sink", "sinks_a_2", "da_lambda_q1", "da_lambda_k1", "da_lambda_q2", "da_lambda_k2"):
        give(n, I[n].reshape(-1))
    for n in ("w_in", "w_mem_kv", "w_da_o", "w_wa_o", "w_xa_o", "w_out", "w_router", "w_exp_gate", "w_exp_up",
              "w_exp_down", "w_in_a_2", "w_in_b_2", "w_out_2", "ffn_w_in_3", "ffn_w_out_3", "sgu_w_in_3",
              "sgu_w_out_3", "rwkv_w_rkv_3", "rwkv_w1_3", "rwkv_w2_3", "rwkv_a1_3", "rwkv_a2_3", "rwkv_g1_3",
              "rwkv_g2_3", "rwkv_w_o_3"):
        a = I[n]
        give(n, a[0] if a.shape[0] == 1 else a)
    give("spT", I["sgu_w_sp_3"][0].transpose(2, 0, 1).reshape(P, 16 * P))
    give("b_sp", I["sgu_b_sp_3"][0].reshape(-1))
    for n in ("sgu_ln_g_3", "sgu_ln_b_3", "rwkv_gn_g_3", "rwkv_gn_b_3"):
        give(n, I[n].reshape(-1))
    give("b_in_v", I["sgu_b_in_3"].reshape(-1)[2048:])
    o = nc.dram_tensor("out_0_dram", (P, 8 * T), F32, kind="ExternalOutput").ap()
    build(nc, A, o)
    r = _run(nc, [arrays], core_ids=[0])
    y = r.results[0]["out_0_dram"]
    return np.ascontiguousarray(y.reshape(P, 8, T).transpose(2, 1, 0)).reshape(1, T, D)
```
